# Optimizing a Trainium2 kernel written in Bass

```python
import jax
import jax.numpy as jnp
from jax import lax
import numpy as np
import math
import jax, jax.numpy as jnp

D_MODEL = 1024
BATCH = 1
SEQ = 512
DEPTH = 2

N_META = 16
NORM_EPS = 1e-6
SSM_D_INNER = 2 * D_MODEL
SSM_HEAD_DIM = 64
SSM_HEADS = SSM_D_INNER // SSM_HEAD_DIM
SSM_GROUPS = 4
SSM_HEADS_PER_GROUP = SSM_HEADS // SSM_GROUPS
SSM_STATE = 128
SSM_CONV = 4
SSM_CHUNK = 256
SSM_CONV_DIM = SSM_D_INNER + 2 * SSM_GROUPS * SSM_STATE
SSM_IN_DIM = SSM_D_INNER + SSM_CONV_DIM + SSM_HEADS
SB_HEAD_DIM = 64
SB_HEADS = D_MODEL // SB_HEAD_DIM
SB_WIDTH = SB_HEADS * SB_HEAD_DIM
SB_Q_BLOCK = 128
D_FF = 256 * ((8 * D_MODEL // 3 + 255) // 256)
FFN_CONV = 3


def _rmsnorm(x, g):
    x32 = x.astype(jnp.float32)
    y = x32 * lax.rsqrt(jnp.mean(x32 * x32, axis=-1, keepdims=True) + NORM_EPS)
    return (y * g.astype(jnp.float32)).astype(x.dtype)

def _causal_dwconv(x, w, bias):
    width = w.shape[0]
    L = x.shape[1]
    xp = jnp.pad(x, ((0, 0), (width - 1, 0), (0, 0)))
    y = xp[:, 0:L] * w[0] + bias
    for k in range(1, width):
        y = y + xp[:, k:k + L] * w[k]
    return y

def _ssd_mixer(u, w_in, conv_w, conv_b, dt_bias, a_log, d_skip, gate_g, w_out):
    b, L, _ = u.shape
    G, E, P, N, Q = SSM_GROUPS, SSM_HEADS_PER_GROUP, SSM_HEAD_DIM, SSM_STATE, SSM_CHUNK
    f32 = jnp.float32
    z, xbc, dt_raw = jnp.split(u @ w_in, [SSM_D_INNER, SSM_D_INNER + SSM_CONV_DIM], axis=-1)
    xbc = jax.nn.silu(_causal_dwconv(xbc, conv_w, conv_b))
    xs, b_in, c_in = jnp.split(xbc, [SSM_D_INNER, SSM_D_INNER + G * N], axis=-1)
    dt = jax.nn.softplus(dt_raw.astype(f32) + dt_bias.astype(f32))
    a = -jnp.exp(a_log.astype(f32))
    pf = (-N_META) % Q
    pe = (-(pf + L)) % Q
    nc = (pf + L + pe) // Q

    def to_chunks(t, tail):
        return jnp.pad(t, ((0, 0), (pf, pe), (0, 0))).reshape((b, nc, Q) + tail)

    x_c = to_chunks(xs, (G, E, P)).astype(f32)
    b_c = to_chunks(b_in, (G, N)).astype(f32)
    c_c = to_chunks(c_in, (G, N)).astype(f32)
    dt_c = to_chunks(dt, (G, E))
    xdt = x_c * dt_c[..., None]
    a_cs = jnp.cumsum(jnp.transpose(dt_c * a.reshape(G, E), (0, 3, 4, 1, 2)), axis=-1)
    causal = jnp.tril(jnp.ones((Q, Q), dtype=bool))
    decay_in = jnp.exp(jnp.where(causal, a_cs[..., :, None] - a_cs[..., None, :], -jnp.inf))
    cb = jnp.einsum('bclgn,bcsgn->bgcls', c_c, b_c)
    y_diag = jnp.einsum('bgcls,bgecls,bcsgep->bclgep', cb, decay_in, xdt)
    decay_to_end = jnp.exp(a_cs[..., -1:] - a_cs)
    chunk_states = jnp.einsum('bclgn,bgecl,bclgep->cbgepn', b_c, decay_to_end, xdt)
    chunk_decay = jnp.moveaxis(jnp.exp(a_cs[..., -1]), -1, 0)

    def step(state, inp):
        s_new, d = inp
        return state * d[..., None, None] + s_new, state

    _, prev_states = lax.scan(step, jnp.zeros((b, G, E, P, N), f32), (chunk_states, chunk_decay))
    y_off = jnp.einsum('bclgn,cbgepn,bgecl->bclgep', c_c, prev_states, jnp.exp(a_cs))
    y = (y_diag + y_off).reshape(b, nc * Q, SSM_D_INNER)[:, pf:pf + L]
    y = y + (xs.reshape(b, L, SSM_HEADS, P).astype(f32) * d_skip.astype(f32)[:, None]).reshape(b, L, SSM_D_INNER)
    hg = (y * jax.nn.silu(z.astype(f32))).reshape(b, L, G, SSM_D_INNER // G)
    hg = hg * lax.rsqrt(jnp.mean(hg * hg, axis=-1, keepdims=True) + NORM_EPS)
    hg = hg.reshape(b, L, SSM_D_INNER) * gate_g.astype(f32)
    return hg.astype(u.dtype) @ w_out

def _stick_breaking_attention(q, k, v):
    b, L, H, Dh = q.shape
    lp = -(-L // SB_Q_BLOCK) * SB_Q_BLOCK
    pad = ((0, 0), (0, lp - L), (0, 0), (0, 0))
    q, k, v = jnp.pad(q, pad), jnp.pad(k, pad), jnp.pad(v, pad)
    scale = Dh ** -0.5
    outs = []
    for i in range(lp // SB_Q_BLOCK):
        t0, t1 = i * SB_Q_BLOCK, (i + 1) * SB_Q_BLOCK
        logits = jnp.einsum('bthd,bshd->bhts', q[:, t0:t1], k[:, :t1]).astype(jnp.float32) * scale
        t_idx = t0 + jnp.arange(SB_Q_BLOCK)[:, None]
        s_idx = jnp.arange(t1)[None, :]
        visible = s_idx < t_idx
        log_keep = jnp.where(visible, jax.nn.log_sigmoid(-logits), 0.0)
        later = lax.cumsum(log_keep, axis=3, reverse=True) - log_keep
        log_w = jnp.where(visible, jax.nn.log_sigmoid(logits) + later, -jnp.inf)
        w = jnp.exp(log_w).astype(v.dtype)
        outs.append(jnp.einsum('bhts,bshd->bthd', w, v[:, :t1]))
    return jnp.concatenate(outs, axis=1)[:, :L]

def _conv_ffn(u, w_up, conv_w, conv_b, w_down):
    h = _causal_dwconv(u @ w_up, conv_w, conv_b)
    g, val = jnp.split(h, 2, axis=-1)
    return (jax.nn.silu(g) * val) @ w_down

def first_inputs(seed: int = 0) -> dict:
    key = jax.random.key(seed)
    ks = jax.random.split(key, 32)
    n_a = DEPTH // 2
    n_b = DEPTH - n_a
    f32 = jnp.float32

    def nrm(k, shape, scale):
        return jax.random.normal(k, shape, f32) * scale

    def gain(k, shape):
        return 1.0 + 0.02 * jax.random.normal(k, shape, f32)

    dt0 = jnp.exp(jax.random.uniform(ks[6], (n_a, SSM_HEADS), f32, np.log(1e-3), np.log(1e-1)))
    dt_bias = dt0 + jnp.log(-jnp.expm1(-dt0))
    return {
        'x': jax.random.normal(ks[0], (BATCH, SEQ, D_MODEL), f32),
        'meta_tokens': nrm(ks[1], (N_META, D_MODEL), 1.0),
        'ssd_norm': gain(ks[2], (n_a, D_MODEL)),
        'ssd_w_in': nrm(ks[3], (n_a, D_MODEL, SSM_IN_DIM), D_MODEL ** -0.5),
        'ssd_conv_w': nrm(ks[4], (n_a, SSM_CONV, SSM_CONV_DIM), SSM_CONV ** -0.5),
        'ssd_conv_b': nrm(ks[5], (n_a, SSM_CONV_DIM), 0.02),
        'ssd_dt_bias': dt_bias,
        'ssd_a_log': jnp.log(jax.random.uniform(ks[7], (n_a, SSM_HEADS), f32, 1.0, 16.0)),
        'ssd_d_skip': jax.random.uniform(ks[8], (n_a, SSM_HEADS), f32, 0.5, 1.5),
        'ssd_gate_norm': gain(ks[9], (n_a, SSM_D_INNER)),
        'ssd_w_out': nrm(ks[10], (n_a, SSM_D_INNER, D_MODEL), SSM_D_INNER ** -0.5),
        'kv_norm': gain(ks[11], (D_MODEL,)),
        'w_kv': nrm(ks[12], (D_MODEL, 2 * SB_WIDTH), D_MODEL ** -0.5),
        'sb_norm': gain(ks[13], (n_b, D_MODEL)),
        'sb_w_q': nrm(ks[14], (n_b, D_MODEL, SB_WIDTH), D_MODEL ** -0.5),
        'sb_w_o': nrm(ks[15], (n_b, SB_WIDTH, D_MODEL), SB_WIDTH ** -0.5),
        'ffn_norm': gain(ks[16], (DEPTH, D_MODEL)),
        'ffn_w_up': nrm(ks[17], (DEPTH, D_MODEL, 2 * D_FF), D_MODEL ** -0.5),
        'ffn_conv_w': nrm(ks[18], (DEPTH, FFN_CONV, 2 * D_FF), FFN_CONV ** -0.5),
        'ffn_conv_b': nrm(ks[19], (DEPTH, 2 * D_FF), 0.02),
        'ffn_w_down': nrm(ks[20], (DEPTH, D_FF, D_MODEL), D_FF ** -0.5),
        'final_norm': gain(ks[21], (D_MODEL,)),
    }

def first_block(x, meta_tokens, ssd_norm, ssd_w_in, ssd_conv_w, ssd_conv_b, ssd_dt_bias, ssd_a_log,
              ssd_d_skip, ssd_gate_norm, ssd_w_out, kv_norm, w_kv, sb_norm, sb_w_q, sb_w_o,
              ffn_norm, ffn_w_up, ffn_conv_w, ffn_conv_b, ffn_w_down, final_norm):
    b = x.shape[0]
    n_a = DEPTH // 2
    h = jnp.concatenate([jnp.broadcast_to(meta_tokens[None], (b, N_META, D_MODEL)).astype(x.dtype), x], axis=1)
    L = h.shape[1]
    k_shared = None
    v_shared = None
    for layer in range(DEPTH):
        if layer < n_a:
            h = h + _ssd_mixer(_rmsnorm(h, ssd_norm[layer]), ssd_w_in[layer], ssd_conv_w[layer],
                               ssd_conv_b[layer], ssd_dt_bias[layer], ssd_a_log[layer],
                               ssd_d_skip[layer], ssd_gate_norm[layer], ssd_w_out[layer])
        else:
            if layer == n_a:
                kv = _rmsnorm(h, kv_norm) @ w_kv
                k_shared, v_shared = jnp.split(kv.reshape(b, L, 2, SB_HEADS, SB_HEAD_DIM), 2, axis=2)
                k_shared, v_shared = k_shared[:, :, 0], v_shared[:, :, 0]
            j = layer - n_a
            q = (_rmsnorm(h, sb_norm[j]) @ sb_w_q[j]).reshape(b, L, SB_HEADS, SB_HEAD_DIM)
            o = _stick_breaking_attention(q, k_shared, v_shared).reshape(b, L, SB_WIDTH)
            h = h + o @ sb_w_o[j]
        h = h + _conv_ffn(_rmsnorm(h, ffn_norm[layer]), ffn_w_up[layer], ffn_conv_w[layer],
                          ffn_conv_b[layer], ffn_w_down[layer])
    return _rmsnorm(h, final_norm)[:, N_META:]


CHUNK = 64
LEFT_CHUNKS = 8
BAND = LEFT_CHUNKS + 1
ATTN_HEAD_DIM = 64
ATTN_HEADS = D_MODEL // ATTN_HEAD_DIM
MAX_REL = 256
DN_HEAD_DIM = 128
DN_HEADS = D_MODEL // DN_HEAD_DIM
DN_WIDTH = DN_HEADS * DN_HEAD_DIM
CONV_K = 4
D_FF_2 = 4 * D_MODEL
EPS = 1e-6
N_MIXERS = 2
N_ATTN_LAYERS = (DEPTH + 1) // 2
N_DN_LAYERS = DEPTH // 2


def rmsnorm(x, w):
    xf = x.astype(jnp.float32)
    y = xf * lax.rsqrt(jnp.mean(xf * xf, axis=-1, keepdims=True) + EPS)
    return (y * w.astype(jnp.float32)).astype(x.dtype)

def l2norm(x):
    xf = x.astype(jnp.float32)
    return xf * lax.rsqrt(jnp.sum(xf * xf, axis=-1, keepdims=True) + EPS)

def chunked_rel_attention(h, w_qkv, rel_bias, w_o):
    B, S, _ = h.shape
    nc = S // CHUNK
    qkv = h @ w_qkv
    q, k, v = jnp.split(qkv, 3, axis=-1)
    q = q.reshape(B, S, ATTN_HEADS, ATTN_HEAD_DIM)
    k = k.reshape(B, S, ATTN_HEADS, ATTN_HEAD_DIM)
    v = v.reshape(B, S, ATTN_HEADS, ATTN_HEAD_DIM)
    pad = ((0, 0), (LEFT_CHUNKS * CHUNK, 0), (0, 0), (0, 0))
    kpad = jnp.pad(k, pad)
    vpad = jnp.pad(v, pad)
    q_off = jnp.arange(CHUNK)[:, None]
    k_off = jnp.arange(BAND * CHUNK)[None, :] - LEFT_CHUNKS * CHUNK
    dist = jnp.clip(q_off - k_off, -MAX_REL, MAX_REL) + MAX_REL
    bias = rel_bias[:, dist].astype(jnp.float32)
    scale = ATTN_HEAD_DIM ** -0.5

    def one_chunk(c):
        start = c * CHUNK
        q_c = lax.dynamic_slice_in_dim(q, start, CHUNK, axis=1)
        k_b = lax.dynamic_slice_in_dim(kpad, start, BAND * CHUNK, axis=1)
        v_b = lax.dynamic_slice_in_dim(vpad, start, BAND * CHUNK, axis=1)
        s = jnp.einsum('bqhd,bkhd->bhqk', q_c, k_b,
                       preferred_element_type=jnp.float32) * scale + bias[None]
        k_abs = start - LEFT_CHUNKS * CHUNK + jnp.arange(BAND * CHUNK)
        s = jnp.where((k_abs >= 0)[None, None, None, :], s, -jnp.inf)
        p = jax.nn.softmax(s, axis=-1).astype(v.dtype)
        return jnp.einsum('bhqk,bkhd->bqhd', p, v_b)

    o = lax.map(one_chunk, jnp.arange(nc))
    o = jnp.moveaxis(o, 0, 1).reshape(B, S, D_MODEL)
    return o @ w_o

def causal_conv(x, w):
    S = x.shape[1]
    xp = jnp.pad(x, ((0, 0), (CONV_K - 1, 0), (0, 0)))
    y = xp[:, 0:S] * w[0]
    for j in range(1, CONV_K):
        y = y + xp[:, j:j + S] * w[j]
    return y

def chunk_gated_delta_rule(q, k, v, g, beta):
    B, S, H, dk = q.shape
    dv = v.shape[-1]
    nc = S // CHUNK

    def to_chunks(t):
        t = t.astype(jnp.float32).reshape((B, nc, CHUNK, H) + t.shape[3:])
        return jnp.moveaxis(t, 3, 1)

    q, k, v, g, beta = map(to_chunks, (q, k, v, g, beta))
    gc = jnp.cumsum(g, axis=-1)
    idx = jnp.arange(CHUNK)
    incl = idx[:, None] >= idx[None, :]
    strict = idx[:, None] > idx[None, :]
    decay = jnp.exp(jnp.where(incl, gc[..., :, None] - gc[..., None, :], -jnp.inf))
    kb = k * beta[..., None]
    vb = v * beta[..., None]
    L = jnp.where(strict, jnp.einsum('bhnid,bhnjd->bhnij', kb, k) * decay, 0.0)
    M = L + jnp.eye(CHUNK, dtype=jnp.float32)
    rhs = jnp.concatenate([vb, kb * jnp.exp(gc)[..., None]], axis=-1)
    sol = lax.linalg.triangular_solve(M, rhs, left_side=True, lower=True,
                                      unit_diagonal=True)
    u, w = sol[..., :dv], sol[..., dv:]
    qk = jnp.einsum('bhnid,bhnjd->bhnij', q, k) * decay
    q_dec = q * jnp.exp(gc)[..., None]
    k_dec = k * jnp.exp(gc[..., -1:] - gc)[..., None]
    g_last = jnp.exp(gc[..., -1])
    xs = tuple(jnp.moveaxis(t, 2, 0) for t in (u, w, qk, q_dec, k_dec, g_last))

    def step(state, inp):
        u_c, w_c, qk_c, qd_c, kd_c, gl_c = inp
        v_new = u_c - jnp.einsum('bhck,bhkv->bhcv', w_c, state)
        o_c = jnp.einsum('bhck,bhkv->bhcv', qd_c, state) + jnp.einsum('bhij,bhjv->bhiv', qk_c, v_new)
        state = state * gl_c[..., None, None] + jnp.einsum('bhck,bhcv->bhkv', kd_c, v_new)
        return state, o_c

    s0 = jnp.zeros((B, H, dk, dv), jnp.float32)
    _, o = lax.scan(step, s0, xs)
    o = jnp.transpose(o, (1, 0, 3, 2, 4))
    return o.reshape(B, S, H, dv)

def gated_deltanet(h, w_in, conv_w, a_log, dt_bias, head_norm, w_o):
    B, S, _ = h.shape
    proj = h @ w_in
    qkv = proj[..., :3 * DN_WIDTH]
    z = proj[..., 3 * DN_WIDTH:4 * DN_WIDTH]
    a = proj[..., 4 * DN_WIDTH:4 * DN_WIDTH + DN_HEADS]
    b = proj[..., 4 * DN_WIDTH + DN_HEADS:]
    qkv = jax.nn.silu(causal_conv(qkv, conv_w))
    q, k, v = jnp.split(qkv, 3, axis=-1)
    q = l2norm(q.reshape(B, S, DN_HEADS, DN_HEAD_DIM)) * (DN_HEAD_DIM ** -0.5)
    k = l2norm(k.reshape(B, S, DN_HEADS, DN_HEAD_DIM))
    v = v.reshape(B, S, DN_HEADS, DN_HEAD_DIM)
    beta = jax.nn.sigmoid(b.astype(jnp.float32))
    g = -jnp.exp(a_log.astype(jnp.float32)) * jax.nn.softplus(
        a.astype(jnp.float32) + dt_bias.astype(jnp.float32))
    o = chunk_gated_delta_rule(q, k, v, g, beta)
    o = rmsnorm(o, head_norm) * jax.nn.silu(
        z.astype(jnp.float32).reshape(B, S, DN_HEADS, DN_HEAD_DIM))
    return o.reshape(B, S, DN_WIDTH).astype(h.dtype) @ w_o

def squared_relu_mlp(h, w_up, w_down):
    return jnp.square(jax.nn.relu(h @ w_up)) @ w_down

def second_inputs(seed: int = 0) -> dict:
    key = jax.random.key(seed)
    ks = jax.random.split(key, 18)
    f32 = jnp.float32

    def nrm(k, shape, fan_in, gain=1.0):
        return jax.random.normal(k, shape, f32) * (gain * fan_in ** -0.5)

    def gains(k, shape):
        return 1.0 + 0.02 * jax.random.normal(k, shape, f32)

    NA, NB = N_ATTN_LAYERS, N_DN_LAYERS
    x = jax.random.normal(ks[0], (BATCH, SEQ, D_MODEL), f32)
    attn_norm = gains(ks[1], (NA, D_MODEL))
    attn_w_qkv = nrm(ks[2], (NA, D_MODEL, 3 * D_MODEL), D_MODEL)
    attn_rel_bias = 0.1 * jax.random.normal(ks[3], (NA, ATTN_HEADS, 2 * MAX_REL + 1), f32)
    attn_w_o = nrm(ks[4], (NA, D_MODEL, D_MODEL), D_MODEL)
    dn_norm = gains(ks[5], (NB, D_MODEL))
    dn_w_in = nrm(ks[6], (NB, D_MODEL, 4 * DN_WIDTH + 2 * DN_HEADS), D_MODEL)
    dn_conv_w = nrm(ks[7], (NB, CONV_K, 3 * DN_WIDTH), CONV_K)
    dn_a_log = jnp.log(jax.random.uniform(ks[8], (NB, DN_HEADS), f32, 1.0, 16.0))
    dt = jnp.exp(jax.random.uniform(ks[9], (NB, DN_HEADS), f32,
                                    math.log(1e-3), math.log(1e-1)))
    dn_dt_bias = dt + jnp.log(-jnp.expm1(-dt))
    dn_head_norm = gains(ks[10], (NB, DN_HEAD_DIM))
    dn_w_o = nrm(ks[11], (NB, DN_WIDTH, D_MODEL), DN_WIDTH)
    mlp_norm = gains(ks[12], (DEPTH, D_MODEL))
    mlp_w_up = nrm(ks[13], (DEPTH, D_MODEL, D_FF_2), D_MODEL)
    mlp_w_down = nrm(ks[14], (DEPTH, D_FF_2, D_MODEL), D_FF_2, gain=0.5)
    final_norm = gains(ks[15], (D_MODEL,))
    return {"x": x, "attn_norm": attn_norm, "attn_w_qkv": attn_w_qkv,
            "attn_rel_bias": attn_rel_bias, "attn_w_o": attn_w_o,
            "dn_norm": dn_norm, "dn_w_in": dn_w_in, "dn_conv_w": dn_conv_w,
            "dn_a_log": dn_a_log, "dn_dt_bias": dn_dt_bias, "dn_head_norm": dn_head_norm,
            "dn_w_o": dn_w_o, "mlp_norm": mlp_norm, "mlp_w_up": mlp_w_up,
            "mlp_w_down": mlp_w_down, "final_norm": final_norm}

def second_block(x, attn_norm, attn_w_qkv, attn_rel_bias, attn_w_o,
              dn_norm, dn_w_in, dn_conv_w, dn_a_log, dn_dt_bias, dn_head_norm, dn_w_o,
              mlp_norm, mlp_w_up, mlp_w_down, final_norm):
    for i in range(DEPTH):
        j = i // N_MIXERS
        if i % N_MIXERS == 0:
            x = x + chunked_rel_attention(rmsnorm(x, attn_norm[j]), attn_w_qkv[j],
                                          attn_rel_bias[j], attn_w_o[j])
        else:
            x = x + gated_deltanet(rmsnorm(x, dn_norm[j]), dn_w_in[j], dn_conv_w[j],
                                   dn_a_log[j], dn_dt_bias[j], dn_head_norm[j], dn_w_o[j])
        x = x + squared_relu_mlp(rmsnorm(x, mlp_norm[i]), mlp_w_up[i], mlp_w_down[i])
    return rmsnorm(x, final_norm)


def setup_inputs(seed=0):
    out = dict(first_inputs(seed))
    for name, value in second_inputs(seed + 1).items():
        if name != "x":
            out[name + "_2"] = value
    return out


def reference(
    x, meta_tokens, ssd_norm, ssd_w_in, ssd_conv_w, ssd_conv_b, ssd_dt_bias, ssd_a_log,
    ssd_d_skip, ssd_gate_norm, ssd_w_out, kv_norm, w_kv, sb_norm, sb_w_q, sb_w_o, ffn_norm,
    ffn_w_up, ffn_conv_w, ffn_conv_b, ffn_w_down, final_norm, attn_norm_2, attn_w_qkv_2,
    attn_rel_bias_2, attn_w_o_2, dn_norm_2, dn_w_in_2, dn_conv_w_2, dn_a_log_2, dn_dt_bias_2,
    dn_head_norm_2, dn_w_o_2, mlp_norm_2, mlp_w_up_2, mlp_w_down_2, final_norm_2,
):
    x = first_block(
        x, meta_tokens, ssd_norm, ssd_w_in, ssd_conv_w, ssd_conv_b, ssd_dt_bias, ssd_a_log,
        ssd_d_skip, ssd_gate_norm, ssd_w_out, kv_norm, w_kv, sb_norm, sb_w_q, sb_w_o, ffn_norm,
        ffn_w_up, ffn_conv_w, ffn_conv_b, ffn_w_down, final_norm,
    )
    return second_block(
        x, attn_norm_2, attn_w_qkv_2, attn_rel_bias_2, attn_w_o_2, dn_norm_2, dn_w_in_2,
        dn_conv_w_2, dn_a_log_2, dn_dt_bias_2, dn_head_norm_2, dn_w_o_2, mlp_norm_2, mlp_w_up_2,
        mlp_w_down_2, final_norm_2,
    )


_drawn_inputs = setup_inputs


def setup_inputs(seed=0):
    import zlib

    import numpy as np

    out = dict(_drawn_inputs(seed))
    spreads = {}
    factors = {'kv_norm': 4.79,
     'sb_norm': 8.0,
     'ffn_norm': 2.884,
     'ffn_conv_b': 2.796,
     'attn_norm_2': 8.0,
     'attn_rel_bias_2': 4.111,
     'dn_norm_2': 3.619,
     'dn_head_norm_2': 6.276,
     'mlp_norm_2': 3.118,
     'final_norm_2': 2.872}
    for name, (base, spread) in spreads.items():
        noise = np.random.default_rng([zlib.crc32(name.encode()), seed]).standard_normal(out[name].shape)
        drawn = base * np.exp(spread * noise) if base else spread * noise
        out[name] = jnp.asarray(drawn.astype(out[name].dtype))
    for name, factor in factors.items():
        out[name] = (out[name] * factor).astype(out[name].dtype)
    return out
```

```python
from contextlib import ExitStack

import concourse.bass as bass
from concourse import mybir

F32 = mybir.dt.float32
F32R = mybir.dt.float32r
ACT = mybir.ActivationFunctionType
ALU = mybir.AluOpType
AX = mybir.AxisListType.X

P = 128
D = 1024
KT = D // P
META = 16
SEQ = 512
LA = META + SEQ
EPS = 1e-6
SSM_IN = 2048
GROUPS = 4
SSM_HEADS = 32
HPG = SSM_HEADS // GROUPS
XT = SSM_IN // P
FF = 2816
FT = FF // P
FFN_ROUNDS = [8, 8, FT - 16]
MT = 4096 // P
RING = 4
AHEAD = 2
BIG = 1e30

PARAM_COLS = [
    ("ssd_norm", KT), ("ssd_conv_w", 24 * 4), ("ssd_conv_b", 24), ("ssd_dt_bias", 1), ("ssd_a_log", 1),
    ("ssd_d_skip", XT), ("ssd_gate_norm", XT), ("kv_norm", KT), ("sb_norm", KT), ("ffn_norm", 2 * KT),
    ("ffn_conv_w", 2 * 2 * FT * 3), ("ffn_conv_b", 2 * 2 * FT), ("final_norm", KT), ("attn_norm_2", KT),
    ("dn_norm_2", KT), ("dn_conv_w_2", 24 * 4), ("dn_a_log_2", 1), ("dn_dt_bias_2", 1),
    ("dn_head_norm_2", 1), ("mlp_norm_2", 2 * KT), ("final_norm_2", KT),
]
PARAM_AT = {}
_n = 0
for _name, _c in PARAM_COLS:
    PARAM_AT[_name] = _n
    _n += _c
N_PARAM = _n
N_CONST = 12 * P + LA
REL_ROW = 640

STAGES = [("dt", 1, 1), ("bc", 8, 1), ("xs", 16, 1), ("z", 16, 1), ("ssd_out", 8, 2)]


def _ffn_stages(layer):
    for r, k in enumerate(FFN_ROUNDS):
        yield (f"ffn{layer}_up{r}", 2 * k, 1)
        yield (f"ffn{layer}_down{r}", KT, 1)


def _mlp_stages(layer):
    for r in range(MT // KT):
        yield (f"mlp{layer}_up{r}", KT, 1)
        yield (f"mlp{layer}_down{r}", KT, 1)


STAGES += list(_ffn_stages(0)) + [("kv", 16, 1), ("q", 8, 1), ("sb_out", 8, 1)] + list(_ffn_stages(1))
STAGES += [("rq", 8, 1), ("rk", 8, 1), ("rv", 8, 1), ("rel_out", 8, 1)] + list(_mlp_stages(0))
STAGES += [("ab", 1, 1), ("dn_qk", 16, 1), ("dn_v", 8, 1), ("dn_z", 8, 1), ("dn_out", 8, 1)] + list(_mlp_stages(1))
SLAB0, TILE0, TILES, KGS = {}, {}, {}, {}
_s = _t = 0
for _name, _tiles, _kgs in STAGES:
    SLAB0[_name], TILE0[_name], TILES[_name], KGS[_name] = _s, _t, _tiles, _kgs
    _s += _tiles * _kgs
    _t += _tiles
N_SLABS = _s

NORM_AFTER = [None, "ssd_out", "ffn0_down2", "sb_out", "ffn1_down2", None, "rel_out", "mlp0_down3",
              "dn_out", "mlp1_down3"]
CONV0 = {"ffn0": 96, "ffn1": 96 + 132, "dn_in": 96 + 264}
MID0 = {"ffn0": 0, "ffn1": FT, "mlp0": 2 * FT, "mlp1": 2 * FT + MT}

LBLK = [(128 * i, min(P, LA - 128 * i), LA - 128 * i) for i in range(5)]
LOFF = [0, 528, 928, 1200, 1344]
LPK = 1360
LBANK = [[(0, 0, 0, 256), (1, 0, 256, 272)], [(2, 0, 128, 400)], [(3, 0, 256, 272)],
         [(3, 272, 384, 144)], [(3, 416, 512, 16)]]


def build_program(nc, slabs, params, x_in, rel_in, consts_in, out, last=99):
    ctx = ExitStack()
    with ctx:
        sems = {}

        def S(name):
            if name not in sems:
                sems[name] = ctx.enter_context(nc.semaphore(name))
            return sems[name]

        cursor = [(nc.sbuf_base + 63) // 64 * 64]

        def place(name, shape, dt=F32, at=None):
            size = 4
            for n in shape[1:]:
                size *= n
            if at is None:
                at = cursor[0]
                cursor[0] += (size + 31) // 32 * 32
            return nc.alloc_sbuf_tensor_at(name, shape, dt, offset=at), at

        def sb(name, *shape, dt=F32, at=None):
            return place(name, [P, *shape], dt, at)[0]

        h = sb("h", KT, LA)
        xh, A0 = place("x_hi", [P, KT, LA], F32R)
        xl, _ = place("x_lo", [P, KT, LA], F32R)
        A_SIZE = 2 * KT * LA * 4
        w_raw, W0 = place("w_raw", [P, RING, D])
        w_low = sb("w_low", RING, D, dt=F32R, at=W0)
        w_high = sb("w_high", RING, D, dt=F32R)
        mh, M0 = place("mid_hi", [P, KT, LA], F32R)
        ml, M1 = place("mid_lo", [P, KT, LA], F32R)
        X, X0 = place("mix_x", [P, 16, LA])
        B, B0 = place("mix_b", [P, 5, D])
        z_t = sb("z_t", XT, LA, at=M0)
        bc_t = sb("bc_t", 8, LA, at=B0)
        hg_hi = sb("hg_hi", XT, LA, dt=F32R, at=M0)
        hg_lo = sb("hg_lo", XT, LA, dt=F32R, at=X0)
        v_tmp = sb("v_tmp", KT, LA, at=M0)
        zd_t = sb("zd_t", KT, LA, at=M1)

        rstd = sb("rstd", LA)
        rvar = sb("rvar", LA)
        sqa = sb("sqa", LA)
        sqb = sb("sqb", LA)
        par = sb("par", N_PARAM)
        cst = sb("consts", N_CONST)
        ident = cst[:, 0:P]
        neg_ones = cst[:, P:2 * P]
        neg_tri = cst[:, 2 * P:3 * P]
        causal = cst[:, 3 * P:4 * P]
        flip = cst[:, 4 * P:5 * P]
        levels = cst[:, 5 * P:12 * P].rearrange("p (k n) -> p k n", k=7)
        ones = cst[:, 12 * P:N_CONST]
        pad, PAD_AT = place("conv_in", [P, 2, 3 + LA])
        cacc, CACC_AT = place("conv_acc", [P, 2, LA])
        t1, T1_AT = place("t1", [P, 2, LA])
        t2, T2_AT = place("t2", [P, 2, LA])
        C0 = cursor[0]
        C_SIZE = nc.sbuf_usable_end - C0
        ps = ctx.enter_context(nc.psum_tensor("ps", [P, 8, 512], F32))

        def scratch(prefix, start, size):
            at = [start]

            def take(name, *shape):
                at[0] = (at[0] + 31) // 32 * 32
                n = 4
                for s in shape:
                    n *= s
                at[0] += n
                assert at[0] <= start + size, (prefix, name, at[0] - start - size)
                return sb(prefix + name, *shape, at=at[0] - n)
            return take

        def col(name, k=0, rows=slice(0, P)):
            return par[rows, PARAM_AT[name] + k:PARAM_AT[name] + k + 1]

        def rcol(name, base, step_expr):
            return par[:, bass.ds(PARAM_AT[name] + base + step_expr, 1)]

        def ps_tile(slot, T):
            return ps[:, 2 * slot:2 * slot + 2, 0:264] if T == LA else ps[:, 2 * slot, 0:SEQ]

        def halves(T):
            return ((0, 264), (264, 264)) if T == LA else ((0, SEQ),)

        def cut(ap, T):
            return ap.rearrange("p (a b) -> p a b", a=2) if T == LA else ap

        def hv(kt, T):
            return h[:, kt, LA - T:LA]

        def after_residual(n, kt):
            if n == 0:
                return S("x_loaded"), 16
            if n == 5:
                return S("x2_done"), kt + 1
            return S("tile_taken"), 2 + TILE0[NORM_AFTER[n]] + kt + 1

        def slab_hi(act, s, i=0):
            n = s + AHEAD
            act.wait_ge(S(f"w_loaded{n % RING}"), 16 * (n // RING + 1) + 16 * i)
            act.activation(w_high[:, n % RING, :], w_raw[:, n % RING, :], ACT.Copy).then_inc(S("w_hi"), 1)

        def slab_lo(dve, s, i=0):
            n = s + AHEAD
            dve.wait_ge(S("w_hi"), n + 1 + 4 * i)
            dve.tensor_tensor(w_low[:, n % RING, :], w_raw[:, n % RING, :],
                              w_high[:, n % RING, :].bitcast(F32), ALU.subtract).then_inc(S("w_lo"), 1)

        def steps(eng, name, body, lastloop=False):
            n = TILES[name] * KGS[name]
            if n < RING or n == RING:
                for j in range(n):
                    body(j, 0)
                return
            with eng.Fori(0, n // RING) as i:
                for j in range(RING):
                    body(j, i)

        def gemm(pe, name, hi, lo, T, blocks=KT, ready=None):
            s0, t0, kgs = SLAB0[name], TILE0[name], KGS[name]

            def body(j, i):
                slot, kg = (s0 + j) % RING, j % kgs
                tslot = (t0 + j // kgs) % 2
                pe.wait_ge(S("w_lo"), s0 + j + 1 + 4 * i)
                if kg == 0:
                    pe.wait_ge(S("tile_taken"), t0 + j // kgs + 1 + (4 // kgs) * i)
                for b in range(blocks):
                    kb = kg * KT + b
                    if ready is not None and j < kgs:
                        pe.wait_ge(ready[0], ready[1] + kb + 1)
                    wh = w_high[:, slot, b * P:(b + 1) * P]
                    wl = w_low[:, slot, b * P:(b + 1) * P]
                    end = kg == kgs - 1 and b == blocks - 1
                    for w, a, first, fin in ((wh, hi, kb == 0, False), (wh, lo, False, False), (wl, hi, False, end)):
                        for k, (c, n) in enumerate(halves(T)):
                            mm = pe.matmul(ps[:, 2 * tslot + k, 0:n], w, a[:, kb, c:c + n], start=first, stop=fin)
                mm.then_inc(S("slab_done"), 1)
            steps(pe, name, body)

        def taken(name, j, i, per=4):
            return 2 + TILE0[name] + j + 1 + per * i

        def take_scaled(dve, name, j, i, dst, T, scale=None):
            dve.wait_ge(S("slab_done"), SLAB0[name] + j + 1 + 4 * i)
            src = ps_tile((TILE0[name] + j) % 2, T)
            if scale is None:
                op = dve.tensor_tensor(cut(dst, T), src, cut(rstd[:, 0:T], T), ALU.mult)
            else:
                op = dve.scalar_tensor_tensor(cut(dst, T), src, scale, cut(rstd[:, 0:T], T), ALU.mult, ALU.mult)
            op.then_inc(S("tile_taken"), 1)

        def conv_taps(dve, name, j, i, width, wcol, conv0, T):
            src, acc = pad[:, j % 2, :], cacc[:, j % 2, 0:T]
            off = 4 - width
            dve.wait_ge(S("tile_taken"), taken(name, j, i))
            dve.tensor_scalar(acc, src[:, off:off + T], wcol(0), None, ALU.mult).then_inc(S("conv"), 1)
            for k in range(1, width):
                dve.wait_ge(S("conv"), conv0 + width * j + k + width * 4 * i)
                dve.scalar_tensor_tensor(acc, src[:, off + k:off + k + T], wcol(k), acc,
                                         ALU.mult, ALU.add).then_inc(S("conv"), 1)

        def residual_pe(pe, name, hi, lo, T, blocks=KT, ready=None):
            gemm(pe, name, hi, lo, T, blocks, ready)

        def split_hi(act, n, xi, kt, gain, T, gk=0):
            sem, v = after_residual(n, kt)
            act.wait_ge(sem, v)
            act.activation(xh[:, kt, 0:T], hv(kt, T), ACT.Copy, scale=col(gain, gk + kt)).then_inc(S("x_hi"), 1)

        def split_lo(dve, xi, kt, gain, T, gk=0):
            dve.wait_ge(S("x_hi"), KT * xi + kt + 1)
            dve.scalar_tensor_tensor(xl[:, kt, 0:T], hv(kt, T), col(gain, gk + kt), xh[:, kt, 0:T].bitcast(F32),
                                     ALU.mult, ALU.subtract).then_inc(S("x_lo"), 1)

        def residual_dve(dve, name, T, split=None):
            s0, kgs = SLAB0[name], KGS[name]
            for u in range(KT):
                for kg in range(kgs):
                    s = s0 + u * kgs + kg
                    if s + AHEAD < N_SLABS:
                        slab_lo(dve, s)
                dve.wait_ge(S("slab_done"), s0 + (u + 1) * kgs)
                dve.tensor_tensor(cut(hv(u, T), T), ps_tile((TILE0[name] + u) % 2, T), cut(hv(u, T), T),
                                  ALU.add).then_inc(S("tile_taken"), 1)
                if split and u >= 1:
                    split_lo(dve, split[0], u - 1, split[1], T, split[2])
            if split:
                split_lo(dve, split[0], KT - 1, split[1], T, split[2])

        def residual_act(act, name, T, n=None, split=None):
            s0, kgs = SLAB0[name], KGS[name]
            for u in range(KT):
                for kg in range(kgs):
                    s = s0 + u * kgs + kg
                    if s + AHEAD < N_SLABS:
                        slab_hi(act, s)
                if split:
                    split_hi(act, n, split[0], u, split[1], T, split[2])

        def stats_pool(pool, n, T):
            c = 15 * n
            for kt in range(KT):
                sem, v = after_residual(n, kt)
                pool.wait_ge(sem, v)
                if kt == 0:
                    if n:
                        pool.wait_ge(S("stat_ready"), n)
                    pool.tensor_tensor(sqa[:, 0:T], hv(0, T), hv(0, T), ALU.mult).then_inc(S("sumsq"), 1)
                    c += 1
                    continue
                pool.wait_ge(S("sumsq"), c)
                pool.tensor_tensor(sqb[:, 0:T], hv(kt, T), hv(kt, T), ALU.mult).then_inc(S("sumsq"), 1)
                pool.wait_ge(S("sumsq"), c + 1)
                pool.tensor_tensor(sqa[:, 0:T], sqa[:, 0:T], sqb[:, 0:T], ALU.add).then_inc(S("sumsq"), 1)
                c += 2

        def stats_pe(pe, n, T):
            pe.wait_ge(S("sumsq"), 15 * (n + 1))
            for k, (c, m) in enumerate(halves(T)):
                mm = pe.matmul(ps[:, 4 + k, 0:m], ones[:, 0:P], sqa[:, c:c + m], start=True, stop=True)
            mm.then_inc(S("stat_ready"), 1)

        def stats_dve(dve, n, T):
            dve.wait_ge(S("stat_ready"), n + 1)
            dve.tensor_scalar(cut(rvar[:, 0:T], T), ps_tile(2, T), 1.0 / D, EPS, ALU.mult, ALU.add)\
               .then_inc(S("stat_var"), 1)
            dve.wait_ge(S("stat_var"), 2 * n + 1)
            dve.reciprocal(rvar[:, 0:T], rvar[:, 0:T]).then_inc(S("stat_var"), 1)
            dve.wait_ge(S("rstd_ready"), n + 1)

        def stats_act(act, n, T):
            act.wait_ge(S("stat_var"), 2 * (n + 1))
            act.activation(rstd[:, 0:T], rvar[:, 0:T], ACT.Sqrt).then_inc(S("rstd_ready"), 1)

        def ffn_pe(pe, layer, xi):
            pair = 0
            for r, k in enumerate(FFN_ROUNDS):
                gemm(pe, f"ffn{layer}_up{r}", xh, xl, LA, ready=(S("x_lo"), KT * xi) if r == 0 else None)
                gemm(pe, f"ffn{layer}_down{r}", mh, ml, LA, k, ready=(S("mid_lo"), MID0[f"ffn{layer}"] + pair))
                pair += k

        def ffn_dve(dve, layer, n, split):
            stats_dve(dve, n, LA)
            pair = 0
            for r, k in enumerate(FFN_ROUNDS):
                name = f"ffn{layer}_up{r}"
                conv0 = CONV0[f"ffn{layer}"] + 6 * pair
                mid0 = MID0[f"ffn{layer}"] + pair
                g0 = layer * FT + pair

                def hid_lo(q, i):
                    dve.wait_ge(S("mid_hi"), mid0 + q + 1 + 2 * i)
                    dve.tensor_tensor(ml[:, bass.ds(q + 2 * i, 1), :].rearrange("p a t -> p (a t)"), t1[:, q, :],
                                      mh[:, bass.ds(q + 2 * i, 1), :].rearrange("p a t -> p (a t)").bitcast(F32),
                                      ALU.subtract).then_inc(S("mid_lo"), 1)

                def body(j, i):
                    q = j // 2
                    tile = layer * 2 * FT + 2 * pair + j
                    slab_lo(dve, SLAB0[name] + j, i)
                    take_scaled(dve, name, j, i, pad[:, j % 2, 3:3 + LA], LA)
                    conv_taps(dve, name, j, i, 3, lambda t: rcol("ffn_conv_w", tile * 3 + t, 12 * i), conv0, LA)
                    if j == 2:
                        hid_lo(0, i)
                    if j % 2:
                        dve.wait_ge(S("conv"), conv0 + 3 * (j + 1) + 12 * i)
                        dve.wait_ge(S("gate"), g0 + q + 1 + 2 * i)
                        dve.scalar_tensor_tensor(t1[:, q, :], cacc[:, 1, :], rcol("ffn_conv_b", tile, 4 * i),
                                                 t2[:, q, :], ALU.add, ALU.mult).then_inc(S("hidden"), 1)
                    if j == 3:
                        hid_lo(1, i)
                steps(dve, name, body)
                pair += k
                residual_dve(dve, f"ffn{layer}_down{r}", LA, split if r == 2 else None)

        def ffn_act(act, layer, n, n_next, split):
            stats_act(act, n, LA)
            pair = 0
            for r, k in enumerate(FFN_ROUNDS):
                name = f"ffn{layer}_up{r}"
                conv0 = CONV0[f"ffn{layer}"] + 6 * pair
                g0 = layer * FT + pair

                def body(j, i):
                    q = j // 2
                    tile = layer * 2 * FT + 2 * pair + j
                    slab_hi(act, SLAB0[name] + j, i)
                    if j % 2 == 0:
                        act.wait_ge(S("conv"), conv0 + 3 * (j + 1) + 12 * i)
                        act.activation(t2[:, q, :], cacc[:, 0, :], ACT.Silu,
                                       bias=rcol("ffn_conv_b", tile, 4 * i)).then_inc(S("gate"), 1)
                    else:
                        act.wait_ge(S("hidden"), g0 + q + 1 + 2 * i)
                        act.activation(mh[:, bass.ds(q + 2 * i, 1), :].rearrange("p a t -> p (a t)"), t1[:, q, :],
                                       ACT.Copy).then_inc(S("mid_hi"), 1)
                steps(act, name, body)
                pair += k
                residual_act(act, f"ffn{layer}_down{r}", LA, n_next, split if r == 2 else None)

        def mlp_pe(pe, layer, xi):
            for r in range(MT // KT):
                gemm(pe, f"mlp{layer}_up{r}", xh, xl, SEQ, ready=(S("x_lo"), KT * xi) if r == 0 else None)
                gemm(pe, f"mlp{layer}_down{r}", mh, ml, SEQ, ready=(S("mid_lo"), MID0[f"mlp{layer}"] + KT * r))

        def mlp_dve(dve, layer, n, split):
            stats_dve(dve, n, SEQ)
            for r in range(MT // KT):
                name = f"mlp{layer}_up{r}"
                mid0, u0 = MID0[f"mlp{layer}"] + KT * r, 32 * layer + KT * r

                def hid_lo(j, i):
                    dve.wait_ge(S("mid_hi"), mid0 + j + 1 + 4 * i)
                    dve.wait_ge(S("squared"), u0 + j + 1 + 4 * i)
                    dve.tensor_tensor(ml[:, bass.ds(j + 4 * i, 1), 0:SEQ].rearrange("p a t -> p (a t)"),
                                      t2[:, j % 2, 0:SEQ],
                                      mh[:, bass.ds(j + 4 * i, 1), 0:SEQ].rearrange("p a t -> p (a t)").bitcast(F32),
                                      ALU.subtract).then_inc(S("mid_lo"), 1)

                def body(j, i):
                    slab_lo(dve, SLAB0[name] + j, i)
                    dve.wait_ge(S("slab_done"), SLAB0[name] + j + 1 + 4 * i)
                    dve.scalar_tensor_tensor(t1[:, j % 2, 0:SEQ], ps_tile((TILE0[name] + j) % 2, SEQ), 0.0,
                                             rstd[:, 0:SEQ], ALU.max, ALU.mult).then_inc(S("tile_taken"), 1)
                    if j:
                        hid_lo(j - 1, i)
                    dve.wait_ge(S("tile_taken"), taken(name, j, i))
                    dve.tensor_tensor(t2[:, j % 2, 0:SEQ], t1[:, j % 2, 0:SEQ], t1[:, j % 2, 0:SEQ],
                                      ALU.mult).then_inc(S("squared"), 1)
                    if j == 3:
                        hid_lo(3, i)
                steps(dve, name, body)
                residual_dve(dve, f"mlp{layer}_down{r}", SEQ, split if r == 3 else None)

        def mlp_act(act, layer, n, n_next, split):
            stats_act(act, n, SEQ)
            for r in range(MT // KT):
                name = f"mlp{layer}_up{r}"

                def body(j, i):
                    slab_hi(act, SLAB0[name] + j, i)
                    act.wait_ge(S("tile_taken"), taken(name, j, i))
                    act.activation(mh[:, bass.ds(j + 4 * i, 1), 0:SEQ].rearrange("p a t -> p (a t)"),
                                   t1[:, j % 2, 0:SEQ], ACT.Square).then_inc(S("mid_hi"), 1)
                steps(act, name, body)
                residual_act(act, f"mlp{layer}_down{r}", SEQ, n_next, split if r == 3 else None)

        def softplus_act(act, sem, base, x, bias, e, l):
            act.activation(e, x, ACT.Abs, bias=bias).then_inc(sem, 1)
            act.wait_ge(sem, base + 1)
            act.activation(e, e, ACT.Exp, scale=-1.0).then_inc(sem, 1)
            act.wait_ge(sem, base + 2)
            act.activation(l, e, ACT.Ln, bias=1.0).then_inc(sem, 1)

        def softplus_dve(dve, sem, base, act_sem, act_val, x, bias, e, l, u, m, dst):
            def step(k, op):
                op.then_inc(sem, 1)
                dve.wait_ge(sem, base + k)
            dve.wait_ge(act_sem, act_val)
            step(1, dve.tensor_scalar(u, e, 1.0, -1.0, ALU.add, ALU.add))
            step(2, dve.tensor_scalar(m, u, 0.0, None, ALU.is_equal))
            step(3, dve.tensor_tensor(u, u, m, ALU.add))
            step(4, dve.tensor_tensor(l, l, m, ALU.add))
            step(5, dve.reciprocal(u, u))
            step(6, dve.tensor_tensor(l, l, e, ALU.mult))
            step(7, dve.tensor_tensor(l, l, u, ALU.mult))
            step(8, dve.tensor_scalar(m, x, bias, 0.0, ALU.add, ALU.max))
            step(9, dve.tensor_tensor(dst, m, l, ALU.add))

        def tiles_out(name):
            return 2 + TILE0[name] + TILES[name]

        def scaled_stage_dve(dve, name, dst, T, scale=None):
            def body(j, i):
                slab_lo(dve, SLAB0[name] + j, i)
                take_scaled(dve, name, j, i, dst(j + 4 * i), T, scale)
            steps(dve, name, body)

        def slabs_act(act, name):
            steps(act, name, lambda j, i: slab_hi(act, SLAB0[name] + j, i))

        def conv_stage_dve(dve, name, first, wname, conv0, T):
            def body(j, i):
                slab_lo(dve, SLAB0[name] + j, i)
                take_scaled(dve, name, j, i, pad[:, j % 2, 3:3 + T], T)
                dve.wait_ge(S("conv_used"), first + j + 1 + 4 * i)
                conv_taps(dve, name, j, i, 4, lambda t: rcol(wname, 4 * (first % 24 + j) + t, 16 * i), conv0, T)
            steps(dve, name, body)

        def conv_stage_act(act, name, first, bname, conv0, T, dst):
            def body(j, i):
                slab_hi(act, SLAB0[name] + j, i)
                act.wait_ge(S("conv"), conv0 + 4 * (j + 1) + 16 * i)
                kw = {"bias": rcol(bname, first + j, 4 * i)} if bname else {}
                act.activation(dst(j + 4 * i), cacc[:, j % 2, 0:T], ACT.Silu, **kw).then_inc(S("conv_used"), 1)
            steps(act, name, body)

        def tile_of(t, k, T):
            return t[:, bass.ds(k, 1), 0:T].rearrange("p a t -> p (a t)")

        def vtok_pe(pe, src, T, sem, base, first):
            for i in range(-(-T // P)):
                n = min(P, T - P * i)
                b = 4 + 2 * (i % 2)
                if i >= 2:
                    pe.wait_ge(S("vtok_taken"), first + i - 1)
                if i == 0:
                    pe.wait_ge(sem, base)
                for f in range(KT):
                    mm = pe.transpose(ps[0:n, b + f // 4, P * (f % 4):P * (f % 4 + 1)], src(f)[:, P * i:P * i + n], ident[:])
                mm.then_inc(S("vtok_ready"), 1)

        def vtok_dve(dve, dst, T, first):
            for i in range(-(-T // P)):
                n = min(P, T - P * i)
                b = 4 + 2 * (i % 2)
                dve.wait_ge(S("vtok_ready"), first + i + 1)
                dve.tensor_copy(dst[0:n, i, :].rearrange("p (a n) -> p a n", a=2), ps[0:n, b:b + 2, :])\
                   .then_inc(S("vtok_taken"), 1)

        take = scratch("ssd_", A0, A_SIZE)
        dec = take("decay", 2, LPK)
        cbm = take("cb", LPK)
        x_tok = take("x_tok", 5, 512)
        gacc = take("gacc", LA)
        dt_tok = take("dt_tok", 5, SSM_HEADS)
        a_tok = take("a_tok", 5, SSM_HEADS)
        dt_rows, a_rows = rvar, sqb
        take_c = scratch("ssdc_", C0, C_SIZE)
        dt_in = take_c("dt_in", LA)
        nega = take_c("nega", 1)
        R32 = slice(0, SSM_HEADS)
        HALF = ((0, 0, 256), (1, 256, 272))
        PIECES = []
        for s0_, ns_, nl_ in LBLK:
            PIECES.append([(bk, max(s0_ - l0, 0), max(s0_, l0), l0 + n - max(s0_, l0))
                           for bk, l0, n in HALF if l0 + n > s0_])

        def packed(i, t):
            return LOFF[i] + t - LBLK[i][0]

        def ssd_pe(pe):
            stats_pe(pe, 0, LA)
            gemm(pe, "dt", xh, xl, LA, ready=(S("x_lo"), 0))
            for name in ("bc", "xs", "z"):
                gemm(pe, name, xh, xl, LA)
            pe.wait_ge(S("tile_taken"), tiles_out("z"))
            pe.wait_ge(S("conv_used"), 2 + 24)

            pe.wait_ge(S("ssd_scan"), 1)
            for i, (s0, n, _) in enumerate(LBLK):
                pe.transpose(ps[0:n, 6, 32 * i:32 * i + 32], dt_rows[R32, s0:s0 + n], ident[R32, R32])
            for i, (s0, n, _) in enumerate(LBLK):
                mm = pe.transpose(ps[0:n, 7, 32 * i:32 * i + 32], a_rows[R32, s0:s0 + n], ident[R32, R32])
            mm.then_inc(S("ssd_rows_t"), 1)

            def bcast(hh):
                if hh == 0:
                    pe.wait_ge(S("ssd_tok"), 1)
                else:
                    pe.wait_ge(S("ssd_min"), hh)
                for bk, l0, n in HALF:
                    mm = pe.matmul(ps[:, 6 + bk, 0:n], ident[R32, hh:hh + 1].to_broadcast((SSM_HEADS, P)),
                                   a_rows[R32, l0:l0 + n], start=True, stop=True)
                mm.then_inc(S("ssd_bc"), 1)

            def group_products(g):
                if g:
                    pe.wait_ge(S("ssd_y_taken"), 4 * g)
                if g > 1:
                    pe.wait_ge(S("ssd_gvar"), 2 * (g - 2) + 1)
                for i, (s0, n, _) in enumerate(LBLK):
                    for bk, c, t, m in LBANK[i]:
                        mm = pe.matmul(ps[0:n, bk, c:c + m], bc_t[:, g, s0:s0 + n], bc_t[:, GROUPS + g, t:t + m],
                                       start=True, stop=True)
                mm.then_inc(S("ssd_cb"), 1)
                pe.wait_ge(S("ssd_cb_taken"), g + 1)
                for i, (s0, n, _) in enumerate(LBLK):
                    if i == 4:
                        pe.wait_ge(S("ssd_xt_taken"), 5 * g + 1)
                    for f in range(4):
                        mm = pe.transpose(ps[0:n, i % 4, P * f:P * f + P], X[:, 4 * g + f, s0:s0 + n], ident[:])
                    mm.then_inc(S("ssd_xt"), 1)

            def y_product(hh):
                p, po, e = hh // 2, 64 * (hh % 2), hh % HPG
                yb = 4 if p % 2 == 0 else 2
                if hh % 2 == 0 and p >= 2:
                    pe.wait_ge(S("ssd_y_taken"), p - 1)
                if e == 0:
                    pe.wait_ge(S("ssd_xt_taken"), 5 * (hh // HPG) + 5)
                pe.wait_ge(S("ssd_m"), hh + 1)
                for i, (s0, n, _) in enumerate(LBLK):
                    for bk, c, t, m in PIECES[i]:
                        mm = pe.matmul(ps[po:po + 64, yb + bk, c:c + m], x_tok[0:n, i, 64 * e:64 * e + 64],
                                       dec[0:n, hh % 2, packed(i, t):packed(i, t) + m], start=i == 0,
                                       stop=(bk, i) in ((0, 1), (1, 4)), skip_group_check=True)
                mm.then_inc(S("ssd_y"), 1)

            def group_sum(g):
                pe.wait_ge(S("ssd_gsq"), 7 * (g + 1))
                for k, (c, m) in enumerate(halves(LA)):
                    mm = pe.matmul(ps[:, k, 0:m], ones[:, 0:P], (sqa if g % 2 else gacc)[:, c:c + m], start=True, stop=True)
                mm.then_inc(S("ssd_gsum"), 1)

            bcast(0)
            for g in range(GROUPS):
                group_products(g)
                for e in range(HPG):
                    hh = HPG * g + e
                    if hh + 1 < SSM_HEADS:
                        bcast(hh + 1)
                    y_product(hh)
                if g:
                    group_sum(g - 1)
            pe.wait_ge(S("ssd_gvar"), 2 * (GROUPS - 2) + 1)
            group_sum(GROUPS - 1)
            pe.wait_ge(S("ssd_gvar"), 2 * GROUPS - 1)
            pe.wait_ge(S("ssd_y_taken"), 16)
            gemm(pe, "ssd_out", hg_hi, hg_lo, LA, ready=(S("hg_lo"), 0))
            stats_pe(pe, 1, LA)

        def ssd_act(act):
            for kt in range(KT):
                split_hi(act, 0, 0, kt, "ssd_norm", LA)
            stats_act(act, 0, LA)
            slabs_act(act, "dt")
            conv_stage_act(act, "bc", 0, "ssd_conv_b", 0, LA, lambda k: tile_of(bc_t, k, LA))
            conv_stage_act(act, "xs", 8, "ssd_conv_b", 32, LA, lambda k: tile_of(X, k, LA))

            def z_body(j, i):
                slab_hi(act, SLAB0["z"] + j, i)
                act.wait_ge(S("tile_taken"), taken("z", j, i))
                zt = tile_of(z_t, j + 4 * i, LA)
                act.activation(zt, zt, ACT.Silu).then_inc(S("z_silu"), 1)
            steps(act, "z", z_body)
            act.wait_ge(S("slab_done"), SLAB0["ssd_out"])
            sem = S("ssd_softplus")
            softplus_act(act, sem, 0, dt_in[R32, :], col("ssd_dt_bias", 0, R32), dec[R32, 0, 0:LA], dec[R32, 1, 0:LA])
            act.activation(nega[R32, :], col("ssd_a_log", 0, R32), ACT.Exp).then_inc(sem, 1)

            def decay(hh):
                act.wait_ge(S("ssd_min"), hh + 1)
                d = dec[:, hh % 2, :]
                act.activation(d[:, 0:LOFF[4]], d[:, 0:LOFF[4]], ACT.Exp)
                act.activation(d[0:META, LOFF[4]:LPK], d[0:META, LOFF[4]:LPK], ACT.Exp).then_inc(S("ssd_exp"), 1)

            def group_norm(g):
                act.wait_ge(S("ssd_gvar"), 2 * g + 2)
                act.activation(rstd[:], rvar[:], ACT.Sqrt).then_inc(S("ssd_grs"), 1)
                for f in range(4):
                    t = 4 * g + f
                    act.wait_ge(S("hg_full"), t + 1)
                    act.activation(hg_hi[:, t, :], X[:, t, :], ACT.Copy).then_inc(S("hg_hi"), 1)

            for hh in range(SSM_HEADS):
                decay(hh)
                if hh % HPG == HPG - 1 and hh > HPG:
                    group_norm(hh // HPG - 1)
            group_norm(GROUPS - 1)
            residual_act(act, "ssd_out", LA, 1, (1, "ffn_norm", 0))

        def ssd_dve(dve):
            for kt in range(KT):
                split_lo(dve, 0, kt, "ssd_norm", LA)
            stats_dve(dve, 0, LA)
            slab_lo(dve, SLAB0["dt"])
            take_scaled(dve, "dt", 0, 0, dt_in[:, :], LA)
            conv_stage_dve(dve, "bc", 0, "ssd_conv_w", 0, LA)
            conv_stage_dve(dve, "xs", 8, "ssd_conv_w", 32, LA)
            scaled_stage_dve(dve, "z", lambda k: tile_of(z_t, k, LA), LA)

            sem = S("ssd_rows")
            dve.wait_ge(S("slab_done"), SLAB0["ssd_out"])
            softplus_dve(dve, sem, 0, S("ssd_softplus"), 3, dt_in[R32, :], col("ssd_dt_bias", 0, R32), dec[R32, 0, 0:LA],
                         dec[R32, 1, 0:LA], cbm[R32, 0:LA], cbm[R32, LA:2 * LA], dt_rows[R32, :])
            dve.wait_ge(S("ssd_softplus"), 4)
            dve.tensor_scalar(nega[R32, :], nega[R32, :], -1.0, None, ALU.mult).then_inc(sem, 1)
            dve.wait_ge(sem, 10)
            dve.tensor_scalar(cbm[R32, 0:LA], dt_rows[R32, :], nega[R32, :], None, ALU.mult).then_inc(sem, 1)
            dve.wait_ge(sem, 11)
            dve.wait_ge(S("sumsq"), 15)
            dve.tensor_tensor_scan(a_rows[R32, :], ones[R32, :], cbm[R32, 0:LA], 0.0, ALU.mult, ALU.add)\
               .then_inc(S("ssd_scan"), 1)
            dve.wait_ge(S("ssd_rows_t"), 1)
            for t, bk in ((dt_tok, 6), (a_tok, 7)):
                dve.tensor_copy(t[:, 0:4, :].rearrange("p a b -> p (a b)"), ps[:, bk, 0:128])
                op = dve.tensor_copy(t[0:META, 4, :], ps[0:META, bk, 128:160])
            op.then_inc(S("ssd_tok"), 1)
            dve.wait_ge(S("ssd_tok"), 1)

            def take_group(g):
                dve.wait_ge(S("ssd_cb"), g + 1)
                for i, (s0, n, _) in enumerate(LBLK):
                    for bk, c, t, m in LBANK[i]:
                        if t == s0:
                            op = dve.tensor_tensor(cbm[0:n, LOFF[i]:LOFF[i] + n], ps[0:n, bk, c:c + n], causal[0:n, 0:n], ALU.mult)
                            c, t, m = c + n, t + n, m - n
                        if m:
                            op = dve.tensor_copy(cbm[0:n, packed(i, t):packed(i, t) + m], ps[0:n, bk, c:c + m])
                op.then_inc(S("ssd_cb_taken"), 1)
                if g:
                    dve.wait_ge(S("ssd_y"), HPG * g)
                for i, (s0, n, _) in enumerate(LBLK):
                    dve.wait_ge(S("ssd_xt"), 5 * g + i + 1)
                    dve.tensor_tensor(x_tok[0:n, i, :].rearrange("p (e d) -> p e d", e=HPG),
                                      ps[0:n, i % 4, :].rearrange("p (e d) -> p e d", e=HPG),
                                      dt_tok[0:n, i, HPG * g:HPG * g + HPG].rearrange("p (e o) -> p e o", o=1)
                                      .to_broadcast((n, HPG, 64)), ALU.mult).then_inc(S("ssd_xt_taken"), 1)

            def log_decay(hh):
                dve.wait_ge(S("ssd_bc"), hh + 1)
                if hh >= 2:
                    dve.wait_ge(S("ssd_y"), hh - 1)
                for i, (s0, n, _) in enumerate(LBLK):
                    for bk, c, t, m in PIECES[i]:
                        op = dve.tensor_scalar(dec[0:n, hh % 2, packed(i, t):packed(i, t) + m], ps[0:n, 6 + bk, c:c + m],
                                               a_tok[0:n, i, hh:hh + 1], 0.0, ALU.subtract, ALU.min)
                op.then_inc(S("ssd_min"), 1)

            def weights(hh):
                dve.wait_ge(S("ssd_exp"), hh + 1)
                if hh % HPG == 0:
                    dve.wait_ge(S("ssd_cb_taken"), hh // HPG + 1)
                d = dec[:, hh % 2, :]
                dve.tensor_tensor(d[:, 0:LOFF[4]], d[:, 0:LOFF[4]], cbm[:, 0:LOFF[4]], ALU.mult)
                dve.tensor_tensor(d[0:META, LOFF[4]:LPK], d[0:META, LOFF[4]:LPK], cbm[0:META, LOFF[4]:LPK],
                                  ALU.mult).then_inc(S("ssd_m"), 1)

            def take_y(p):
                yb = 4 if p % 2 == 0 else 2
                dve.wait_ge(S("ssd_y"), 2 * p + 2)
                for bk, l0, n in HALF:
                    op = dve.scalar_tensor_tensor(X[:, p, l0:l0 + n], X[:, p, l0:l0 + n], col("ssd_d_skip", p),
                                                  ps[:, yb + bk, 0:n], ALU.mult, ALU.add)
                op.then_inc(S("ssd_y_taken"), 1)
                dve.wait_ge(S("ssd_y_taken"), p + 1)
                if p == 0:
                    dve.wait_ge(S("z_silu"), 16)
                dve.tensor_tensor(X[:, p, :], X[:, p, :], z_t[:, p, :], ALU.mult).then_inc(S("ssd_gated"), 1)

            def group_norm(g):
                dve.wait_ge(S("ssd_gsum"), g + 1)
                if g:
                    dve.wait_ge(S("ssd_grs"), g)
                dve.tensor_scalar(cut(rvar[:], LA), ps[:, 0:2, 0:264], 1.0 / 512, EPS, ALU.mult, ALU.add)\
                   .then_inc(S("ssd_gvar"), 1)
                dve.wait_ge(S("ssd_gvar"), 2 * g + 1)
                dve.reciprocal(rvar[:], rvar[:]).then_inc(S("ssd_gvar"), 1)
                dve.wait_ge(S("ssd_grs"), g + 1)
                for f in range(4):
                    t = 4 * g + f
                    dve.scalar_tensor_tensor(X[:, t, :], X[:, t, :], col("ssd_gate_norm", t), rstd[:], ALU.mult,
                                             ALU.mult).then_inc(S("hg_full"), 1)
                for f in range(4):
                    t = 4 * g + f
                    dve.wait_ge(S("hg_hi"), t + 1)
                    dve.tensor_tensor(hg_lo[:, t, :], X[:, t, :], hg_hi[:, t, :].bitcast(F32),
                                      ALU.subtract).then_inc(S("hg_lo"), 1)

            log_decay(0)
            for g in range(GROUPS):
                take_group(g)
                for e in range(HPG):
                    hh = HPG * g + e
                    if hh + 1 < SSM_HEADS:
                        log_decay(hh + 1)
                    weights(hh)
                    if e % 2 and e > 1:
                        take_y(hh // 2 - 1)
                take_y(4 * g + 3)
                if g:
                    group_norm(g - 1)
            group_norm(GROUPS - 1)
            residual_dve(dve, "ssd_out", LA, (1, "ffn_norm", 0))

        def ssd_pool(pool):
            stats_pool(pool, 0, LA)
            c = 0
            for g in range(GROUPS):
                acc = sqa if g % 2 else gacc
                for f in range(4):
                    t = 4 * g + f
                    pool.wait_ge(S("ssd_gated"), t + 1)
                    if f == 0:
                        if g == 1:
                            pool.wait_ge(S("stat_ready"), 1)
                        if g >= 2:
                            pool.wait_ge(S("ssd_gsum"), g - 1)
                        pool.tensor_tensor(acc[:], X[:, t, :], X[:, t, :], ALU.mult).then_inc(S("ssd_gsq"), 1)
                        c += 1
                        continue
                    pool.wait_ge(S("ssd_gsq"), c)
                    pool.tensor_tensor(t2[:, 0, :], X[:, t, :], X[:, t, :], ALU.mult).then_inc(S("ssd_gsq"), 1)
                    pool.wait_ge(S("ssd_gsq"), c + 1)
                    pool.tensor_tensor(acc[:], acc[:], t2[:, 0, :], ALU.add).then_inc(S("ssd_gsq"), 1)
                    c += 2
            pool.wait_ge(S("ssd_gsum"), GROUPS)
            stats_pool(pool, 1, LA)

        take = scratch("sb_", A0, A_SIZE)
        sp_t = take("softplus", 2, LPK)
        sw_t = take("weights", 2, LPK)
        SPANS = [(P, 0, 0, 0, 256), (P, 1, 0, 256, 272), (P, 2, 0, LOFF[1], 400), (P, 3, 0, LOFF[2], 416),
                 (META, 3, 416, LOFF[4], 16)]
        PARTS = ((P, 0, LOFF[4]), (META, LOFF[4], LPK))
        NH = 16

        def sb_pe(pe):
            gemm(pe, "kv", xh, xl, LA, ready=(S("x_lo"), 16))
            vtok_pe(pe, lambda f: X[:, 8 + f, :], LA, S("tile_taken"), tiles_out("kv"), 0)
            gemm(pe, "q", xh, xl, LA, ready=(S("x_lo"), 24))
            pe.wait_ge(S("tile_taken"), tiles_out("q"))
            pe.wait_ge(S("vtok_taken"), 5)

            def logits(hh):
                f, po, b0 = hh // 2, 64 * (hh % 2), 4 * (hh % 2)
                if hh >= 2:
                    pe.wait_ge(S("sb_o"), hh - 1)
                for i, (s0, n, _) in enumerate(LBLK):
                    for bk, c, t, m in LBANK[i]:
                        mm = pe.matmul(ps[0:n, b0 + bk, c:c + m], X[po:po + 64, f, s0:s0 + n], X[po:po + 64, 8 + f, t:t + m],
                                       start=i <= 2, stop=True, skip_group_check=True)
                mm.then_inc(S("sb_logits"), 1)

            def subtract_sums(hh):
                b0 = 4 * (hh % 2)
                pe.wait_ge(S("sb_masked"), hh + 1)
                for i, (s0, n, _) in enumerate(LBLK):
                    for bk, c, t, m in LBANK[i]:
                        mm = pe.matmul(ps[0:n, b0 + bk, c:c + m], neg_tri[0:n, 0:n],
                                       sp_t[0:n, hh % 2, packed(i, t):packed(i, t) + m],
                                       start=False, stop=True, skip_group_check=True)
                        for j in range(i + 1, 5):
                            sj, nj, _ = LBLK[j]
                            a = max(t, sj)
                            if a < t + m:
                                mm = pe.matmul(ps[0:n, b0 + bk, c + a - t:c + m], neg_ones[0:nj, 0:n],
                                               sp_t[0:nj, hh % 2, packed(j, a):packed(j, a) + t + m - a],
                                               start=False, stop=True, skip_group_check=True)
                mm.then_inc(S("sb_sums"), 1)

            def values(hh):
                po, b0 = 64 * (hh % 2), 4 * (hh % 2)
                pe.wait_ge(S("sb_w"), hh + 1)
                for i, (s0, n, _) in enumerate(LBLK):
                    for bk, c, t, m in PIECES[i]:
                        mm = pe.matmul(ps[po:po + 64, b0 + bk, c:c + m], B[0:n, i, 64 * hh:64 * hh + 64],
                                       sw_t[0:n, hh % 2, packed(i, t):packed(i, t) + m], start=i == 0,
                                       stop=(bk, i) in ((0, 1), (1, 4)), skip_group_check=True)
                mm.then_inc(S("sb_values"), 1)

            logits(0)
            for hh in range(NH):
                if hh + 1 < NH:
                    logits(hh + 1)
                subtract_sums(hh)
                values(hh)
            pe.wait_ge(S("sb_o"), NH)
            gemm(pe, "sb_out", mh, ml, LA)
            stats_pe(pe, 3, LA)

        def sb_act(act):
            stats_act(act, 2, LA)
            slabs_act(act, "kv")
            act.wait_ge(S("slab_done"), SLAB0["q"])
            for kt in range(KT):
                split_hi(act, 2, 3, kt, "sb_norm", LA)
            slabs_act(act, "q")
            act.wait_ge(S("slab_done"), SLAB0["sb_out"])

            def softplus_parts(hh):
                b0, w = 4 * (hh % 2), sw_t[:, hh % 2, :]
                act.wait_ge(S("sb_logits"), hh + 1)
                if hh >= 2:
                    act.wait_ge(S("sb_values"), hh - 1)
                for n, bk, c, o, m in SPANS:
                    op = act.activation(w[0:n, o:o + m], ps[0:n, b0 + bk, c:c + m], ACT.Abs)
                op.then_inc(S("sb_ln"), 1)
                act.wait_ge(S("sb_ln"), 3 * hh + 1)
                for n, o, e in PARTS:
                    op = act.activation(w[0:n, o:e], w[0:n, o:e], ACT.Exp, scale=-1.0)
                op.then_inc(S("sb_ln"), 1)
                act.wait_ge(S("sb_ln"), 3 * hh + 2)
                for n, o, e in PARTS:
                    op = act.activation(w[0:n, o:e], w[0:n, o:e], ACT.Ln, bias=1.0)
                op.then_inc(S("sb_ln"), 1)

            def weights(hh):
                w = sw_t[:, hh % 2, :]
                act.wait_ge(S("sb_min"), hh + 1)
                for n, o, e in PARTS:
                    op = act.activation(w[0:n, o:e], w[0:n, o:e], ACT.Exp)
                op.then_inc(S("sb_exp"), 1)

            def out_hi(hh):
                po, b0 = 64 * (hh % 2), 4 * (hh % 2)
                act.wait_ge(S("sb_values"), hh + 1)
                for bk, l0, n in HALF:
                    op = act.activation(mh[po:po + 64, hh // 2, l0:l0 + n], ps[po:po + 64, b0 + bk, 0:n], ACT.Copy)
                op.then_inc(S("sb_o_hi"), 1)

            softplus_parts(0)
            for hh in range(NH):
                if hh + 1 < NH:
                    softplus_parts(hh + 1)
                weights(hh)
                out_hi(hh)
            residual_act(act, "sb_out", LA, 3, (4, "ffn_norm", KT))

        def sb_dve(dve):
            stats_dve(dve, 2, LA)
            scaled_stage_dve(dve, "kv", lambda k: tile_of(X, k, LA), LA)
            for kt in range(KT):
                split_lo(dve, 3, kt, "sb_norm", LA)
            vtok_dve(dve, B, LA, 0)
            scaled_stage_dve(dve, "q", lambda k: tile_of(X, 8 + k, LA), LA, scale=0.125)

            def softplus_sum(hh):
                b0, w, s = 4 * (hh % 2), sw_t[:, hh % 2, :], sp_t[:, hh % 2, :]
                dve.wait_ge(S("sb_ln"), 3 * hh + 3)
                if hh >= 2:
                    dve.wait_ge(S("sb_sums"), hh - 1)
                for n, bk, c, o, m in SPANS:
                    op = dve.scalar_tensor_tensor(s[0:n, o:o + m], ps[0:n, b0 + bk, c:c + m], 0.0, w[0:n, o:o + m],
                                                  ALU.max, ALU.add)
                op.then_inc(S("sb_softplus"), 1)

            def log_weights(hh):
                b0, w = 4 * (hh % 2), sw_t[:, hh % 2, :]
                dve.wait_ge(S("sb_sums"), hh + 1)
                for n, bk, c, o, m in SPANS:
                    op = dve.tensor_scalar(w[0:n, o:o + m], ps[0:n, b0 + bk, c:c + m], 0.0, None, ALU.min)
                op.then_inc(S("sb_min"), 1)

            def out_lo(hh):
                po, b0 = 64 * (hh % 2), 4 * (hh % 2)
                dve.wait_ge(S("sb_o_hi"), hh + 1)
                for bk, l0, n in HALF:
                    op = dve.tensor_tensor(ml[po:po + 64, hh // 2, l0:l0 + n], ps[po:po + 64, b0 + bk, 0:n],
                                           mh[po:po + 64, hh // 2, l0:l0 + n].bitcast(F32), ALU.subtract)
                op.then_inc(S("sb_o"), 1)

            softplus_sum(0)
            for hh in range(NH):
                if hh + 1 < NH:
                    softplus_sum(hh + 1)
                log_weights(hh)
                out_lo(hh)
            residual_dve(dve, "sb_out", LA, (4, "ffn_norm", KT))

        def sb_pool(pool):
            def keep_earlier(t, sem):
                for i, (_, n, _) in enumerate(LBLK):
                    v = t[0:n, LOFF[i]:LOFF[i] + n]
                    op = pool.affine_select(out=v, in_=v, compare_op=ALU.is_gt, fill=0.0, base=0,
                                            pattern=[[1, n]], channel_multiplier=-1)
                op.then_inc(sem, 1)

            pool.wait_ge(S("sb_softplus"), 1)
            keep_earlier(sp_t[:, 0, :], S("sb_masked"))
            for hh in range(NH):
                if hh + 1 < NH:
                    pool.wait_ge(S("sb_softplus"), hh + 2)
                    keep_earlier(sp_t[:, (hh + 1) % 2, :], S("sb_masked"))
                pool.wait_ge(S("sb_exp"), hh + 1)
                keep_earlier(sw_t[:, hh % 2, :], S("sb_w"))
            stats_pool(pool, 3, LA)

        def join_dve(dve):
            stats_dve(dve, 4, LA)
            for kt in range(KT):
                dve.scalar_tensor_tensor(hv(kt, SEQ), hv(kt, SEQ), col("final_norm", kt), rstd[:, META:LA],
                                         ALU.mult, ALU.mult).then_inc(S("x2_done"), 1)
            for kt in range(KT):
                split_lo(dve, 5, kt, "attn_norm_2", SEQ)

        def join_act(act):
            stats_act(act, 4, LA)
            act.wait_ge(S("slab_done"), SLAB0["rq"])
            for kt in range(KT):
                split_hi(act, 5, 5, kt, "attn_norm_2", SEQ)

        take = scratch("rel_", A0, A_SIZE)
        rel_t = take("bias", 2, SEQ)
        prob = take("prob", 2, 1280)
        probT = take("probT", 2, 1280)
        rmax = take("rmax", 2, 4)
        rsum = take("rsum", 2, 4)
        POFF = [0, 128, 384, 768]
        TOFF = [0, 512, 896, 1152]

        def rel_pe(pe):
            stats_pe(pe, 5, SEQ)
            gemm(pe, "rq", xh, xl, SEQ, ready=(S("x_lo"), 40))
            gemm(pe, "rk", xh, xl, SEQ)
            gemm(pe, "rv", xh, xl, SEQ)
            pe.wait_ge(S("tile_taken"), tiles_out("rv"))
            vtok_pe(pe, lambda f: v_tmp[:, f, :], SEQ, S("tile_taken"), tiles_out("rv"), 5)
            pe.wait_ge(S("vtok_taken"), 9)

            def scores(hh):
                f, po = hh // 2, 64 * (hh % 2)
                pe.wait_ge(S("rel_bias"), 2 * hh + 2)
                for i in range(4):
                    n = P * (i + 1)
                    if hh:
                        pe.wait_ge(S("rel_exp"), 4 * (hh - 1) + i + 1)
                    pe.matmul(ps[:, i, 0:n], X[po:po + 64, f, P * i:P * i + P], X[po:po + 64, 8 + f, 0:n],
                              start=True, stop=False)
                    mm = pe.matmul(ps[:, i, 0:n], flip[:], rel_t[:, hh % 2, 384 - P * i:SEQ], start=False, stop=True)
                    mm.then_inc(S("rel_scores"), 1)

            def transposes(hh):
                if hh:
                    pe.wait_ge(S("rel_o"), hh)
                    pe.wait_ge(S("rel_ta"), hh)
                pe.wait_ge(S("rel_prob"), hh + 1)
                for j in range(4):
                    for i in range(j, 4):
                        mm = pe.transpose(ps[:, 4 + j, P * (i - j):P * (i - j + 1)],
                                          prob[:, hh % 2, POFF[i] + P * j:POFF[i] + P * j + P], ident[:])
                mm.then_inc(S("rel_t"), 1)

            def values(hh):
                po = 64 * (hh % 2)
                pe.wait_ge(S("rel_ta"), hh + 1)
                pe.wait_ge(S("rel_tb"), hh + 1)
                for j in range(4):
                    n = SEQ - P * j
                    mm = pe.matmul(ps[po:po + 64, 4, P * j:SEQ], B[:, j, 64 * hh:64 * hh + 64],
                                   probT[:, hh % 2, TOFF[j]:TOFF[j] + n], start=j == 0, stop=j == 3, skip_group_check=True)
                mm.then_inc(S("rel_values"), 1)

            scores(0)
            for hh in range(NH):
                if hh + 1 < NH:
                    scores(hh + 1)
                transposes(hh)
                values(hh)
            pe.wait_ge(S("rel_o"), NH)
            gemm(pe, "rel_out", mh, ml, SEQ)
            stats_pe(pe, 6, SEQ)

        def rel_act(act):
            stats_act(act, 5, SEQ)
            for name in ("rq", "rk", "rv"):
                slabs_act(act, name)

            def exps(hh):
                act.wait_ge(S("rel_max"), 2 * hh + 2)
                if hh >= 2:
                    act.wait_ge(S("rel_t"), hh - 1)
                for i in range(4):
                    n = P * (i + 1)
                    act.activation(prob[:, hh % 2, POFF[i]:POFF[i] + n], ps[:, i, 0:n], ACT.Exp,
                                   bias=rmax[:, hh % 2, i:i + 1], accum_out=rsum[:, hh % 2, i:i + 1]).then_inc(S("rel_exp"), 1)

            def take_t(hh):
                act.wait_ge(S("rel_t"), hh + 1)
                if hh >= 2:
                    act.wait_ge(S("rel_values"), hh - 1)
                act.activation(probT[:, hh % 2, 0:512], ps[:, 4, :], ACT.Copy).then_inc(S("rel_ta"), 1)

            def out_hi(hh):
                po = 64 * (hh % 2)
                act.wait_ge(S("rel_values"), hh + 1)
                act.activation(mh[po:po + 64, hh // 2, 0:SEQ], ps[po:po + 64, 4, :], ACT.Copy).then_inc(S("rel_o_hi"), 1)

            act.wait_ge(S("slab_done"), SLAB0["rel_out"])
            exps(0)
            for hh in range(NH):
                take_t(hh)
                if hh + 1 < NH:
                    exps(hh + 1)
                out_hi(hh)
            residual_act(act, "rel_out", SEQ, 6, (6, "mlp_norm_2", 0))

        def rel_dve(dve):
            stats_dve(dve, 5, SEQ)
            scaled_stage_dve(dve, "rq", lambda k: tile_of(X, k, SEQ), SEQ, scale=0.125)
            scaled_stage_dve(dve, "rk", lambda k: tile_of(X, 8 + k, SEQ), SEQ)
            scaled_stage_dve(dve, "rv", lambda k: tile_of(v_tmp, k, SEQ), SEQ)
            vtok_dve(dve, B, SEQ, 5)

            def maxima(hh):
                for i in range(4):
                    dve.wait_ge(S("rel_scores"), 4 * hh + i + 1)
                    op = dve.tensor_reduce(rmax[:, hh % 2, i:i + 1], ps[:, i, 0:P * (i + 1)], AX, ALU.max)
                op.then_inc(S("rel_max"), 1)
                dve.wait_ge(S("rel_max"), 2 * hh + 1)
                dve.tensor_scalar(rmax[:, hh % 2, :], rmax[:, hh % 2, :], -1.0, None, ALU.mult).then_inc(S("rel_max"), 1)

            def normalise(hh):
                r = rsum[:, hh % 2, :]
                dve.wait_ge(S("rel_exp"), 4 * hh + 4)
                dve.reciprocal(r, r).then_inc(S("rel_recip"), 1)
                dve.wait_ge(S("rel_recip"), hh + 1)
                for i in range(4):
                    v = prob[:, hh % 2, POFF[i]:POFF[i] + P * (i + 1)]
                    op = dve.tensor_scalar(v, v, r[:, i:i + 1], None, ALU.mult)
                op.then_inc(S("rel_prob"), 1)

            def take_t(hh):
                dve.wait_ge(S("rel_t"), hh + 1)
                if hh >= 2:
                    dve.wait_ge(S("rel_values"), hh - 1)
                for j in range(1, 4):
                    n = SEQ - P * j
                    op = dve.tensor_copy(probT[:, hh % 2, TOFF[j]:TOFF[j] + n], ps[:, 4 + j, 0:n])
                op.then_inc(S("rel_tb"), 1)

            def out_lo(hh):
                po = 64 * (hh % 2)
                dve.wait_ge(S("rel_o_hi"), hh + 1)
                dve.tensor_tensor(ml[po:po + 64, hh // 2, 0:SEQ], ps[po:po + 64, 4, :],
                                  mh[po:po + 64, hh // 2, 0:SEQ].bitcast(F32), ALU.subtract).then_inc(S("rel_o"), 1)

            maxima(0)
            for hh in range(NH):
                normalise(hh)
                if hh + 1 < NH:
                    maxima(hh + 1)
                take_t(hh)
                out_lo(hh)
            residual_dve(dve, "rel_out", SEQ, (6, "mlp_norm_2", 0))

        def rel_pool(pool):
            stats_pool(pool, 5, SEQ)
            pool.wait_ge(S("slab_done"), SLAB0["rel_out"])
            for hh in range(NH):
                if hh >= 2:
                    pool.wait_ge(S("rel_scores"), 4 * (hh - 1))
                src = bass.AP(rel_in.tensor, hh * REL_ROW, [[1, P], [1, SEQ]])
                pool.dma_start(rel_t[:, hh % 2, :], src).then_inc(S("rel_loaded"), 16)
                pool.wait_ge(S("rel_loaded"), 16 * (hh + 1))
                pool.memset(rel_t[64:P, hh % 2, 448:SEQ], -BIG).then_inc(S("rel_bias"), 2)
            stats_pool(pool, 6, SEQ)

        DH = 8
        CH = 4
        take = scratch("dn_", A0, A_SIZE)
        k_tok = take("k_tok", CH, D)
        big = [take(f"big{i}", CH, P) for i in range(8)]
        t1a = [sb(f"dn_t{i}", CH, P, at=at) for i, at in enumerate(
            [T1_AT, T1_AT + 2048, T2_AT, T2_AT + 2048, PAD_AT, PAD_AT + 2048, CACC_AT, CACC_AT + 2048])]
        take_c = scratch("dnc_", C0, C_SIZE)
        big += t1a + [take_c("c0", CH, P), take_c("c1", CH, P)]
        take_b = scratch("dnb_", B0 + 4 * D * 4, D * 4)
        state = [take_b(f"state{z}", P) for z in range(2)]
        vnew = [take_b(f"vnew{z}", P) for z in range(2)]
        resid = [take_b(f"resid{z}", P) for z in range(2)]
        gc_tok = take_b("gc_tok", CH, DH)
        be_tok = take_b("be_tok", CH, DH)
        nbe_tok = take_b("nbe_tok", CH, DH)
        glast = [take_b(f"glast{z}", CH) for z in range(2)]
        eglast = [take_b(f"eglast{z}", CH) for z in range(2)]
        kfac = [take_b(f"kfac{z}", CH) for z in range(2)]
        dneg = take_b("dneg", 1)
        KB, QG, BV, DM, LT, PM, XM, XTM, KD = range(9)
        buf = [big[0:9], big[9:18]]
        R8, RB = slice(0, DH), slice(32, 32 + DH)
        zsq = t_osq = rstd
        ab_t, g_rows = sqb, rvar

        def kc(hh, c):
            return X[:, 8 + hh, P * c:P * c + P]

        def bcast4(m):
            return m.rearrange("p (o n) -> p o n", o=1).to_broadcast((P, CH, P))

        def dn_pe(pe):
            gemm(pe, "ab", xh, xl, SEQ, ready=(S("x_lo"), KT * 7))
            for name in ("dn_qk", "dn_v", "dn_z"):
                gemm(pe, name, xh, xl, SEQ)
            pe.wait_ge(S("tile_taken"), tiles_out("dn_z"))
            pe.wait_ge(S("conv_used"), 2 + 48)
            for t in range(16):
                pe.wait_ge(S("l2_sq"), t + 1)
                if t >= 4:
                    pe.wait_ge(S("l2_var"), 2 * (t - 4) + 1)
                pe.matmul(ps[:, t % 4, :], ones[:, 0:P], (sqa if t % 2 else zsq)[:, 0:SEQ], start=True,
                          stop=True).then_inc(S("l2_sum"), 1)
            vtok_pe(pe, lambda f: v_tmp[:, f, :], SEQ, S("conv_used"), 2 + 48, 9)
            pe.wait_ge(S("vtok_taken"), 13)
            vtok_pe(pe, lambda f: X[:, 8 + f, :], SEQ, S("l2_done"), 16, 13)
            pe.wait_ge(S("vtok_taken"), 17)
            pe.wait_ge(S("dn_scan"), CH)
            pe.wait_ge(S("dn_softplus"), 5)
            for c in range(CH):
                pe.transpose(ps[:, 0, 8 * c:8 * c + 8], g_rows[R8, P * c:P * c + P], ident[R8, R8])
            for c in range(CH):
                mm = pe.transpose(ps[:, 1, 8 * c:8 * c + 8], ab_t[RB, P * c:P * c + P], ident[RB, RB])
            mm.then_inc(S("dn_rows_t"), 1)
            pe.wait_ge(S("dn_tok"), 2)

            for pr in range(DH // 2):
                both = [(z, 2 * pr + z, 4 * z, buf[z]) for z in range(2)]
                for z, hh, b0, w in both:
                    if pr:
                        pe.wait_ge(S("dn_ovar"), 2 * (hh - 2) + 1)
                    pe.matmul(ps[:, b0, :], ident[R8, hh:hh + 1].to_broadcast((DH, P)), g_rows[R8, 0:SEQ],
                              start=True, stop=True)
                    pe.matmul(ps[:, b0 + 1, :], ident[RB, 32 + hh:33 + hh].to_broadcast((DH, P)), ab_t[RB, 0:SEQ],
                              start=True, stop=True).then_inc(S("dn_bc"), 1)
                for z, hh, b0, w in both:
                    pe.wait_ge(S("dn_kb"), hh + 1)
                    for c in range(CH):
                        pe.matmul(ps[:, b0 + 2, P * c:P * c + P], kc(hh, c), w[KB][:, c, :], start=True, stop=True)
                    for c in range(CH):
                        mm = pe.matmul(ps[:, b0 + 3, P * c:P * c + P], kc(hh, c), X[:, hh, P * c:P * c + P],
                                       start=True, stop=True)
                    mm.then_inc(S("dn_kk"), 1)
                for z, hh, b0, w in both:
                    pe.wait_ge(S("dn_ltk"), 14 * pr + z + 1)
                    pe.wait_ge(S("dn_egc"), hh + 1)
                    for c in range(CH):
                        mm = pe.transpose(ps[:, b0, P * c:P * c + P], w[KB][:, c, :], ident[:])
                    mm.then_inc(S("dn_pw"), 1)
                for k in range(1, 7):
                    for z, hh, b0, w in both:
                        pe.wait_ge(S("dn_ltk"), 14 * pr + 2 * k + z + 1)
                        pe.wait_ge(S("dn_x"), 28 * pr + 4 * (k - 1) + 2 * z + 2)
                        for c in range(CH):
                            mm = pe.matmul(ps[:, b0, P * c:P * c + P], w[KB][:, c, :], w[XM][:, c, :], start=True, stop=True)
                        mm.then_inc(S("dn_pw"), 1)
                    for z, hh, b0, w in both:
                        pe.wait_ge(S("dn_w"), 12 * pr + 2 * (k - 1) + z + 1)
                        for c in range(CH):
                            pe.matmul(ps[:, b0 + 1, P * c:P * c + P], w[DM][:, c, :], w[XTM][:, c, :], start=True, stop=True)
                        for c in range(CH):
                            mm = pe.matmul(ps[:, b0 + 2, P * c:P * c + P], w[XTM][:, c, :], w[DM][:, c, :], start=True, stop=True)
                        mm.then_inc(S("dn_px"), 1)
                for c in range(CH):
                    if c:
                        for z, hh, b0, w in both:
                            pe.wait_ge(S("dn_state"), 8 * pr + 2 * (c - 1) + z + 1)
                            pe.matmul(ps[:, b0, 0:P], kc(hh, c), state[z][:], start=True, stop=True).then_inc(S("dn_ks"), 1)
                    for z, hh, b0, w in both:
                        if c:
                            pe.wait_ge(S("dn_resid"), 6 * pr + 2 * (c - 1) + z + 1)
                        else:
                            pe.wait_ge(S("dn_x"), 28 * pr + 24 + 2 * z + 2)
                            pe.wait_ge(S("dn_prep"), hh + 1)
                        pe.matmul(ps[:, b0 + 1, 0:P], w[XTM][:, c, :], resid[z][:] if c else w[BV][:, 0, :],
                                  start=True, stop=True).then_inc(S("dn_vp"), 1)
                    for z, hh, b0, w in both:
                        pe.wait_ge(S("dn_vnew"), 8 * pr + 2 * c + z + 1)
                        pe.matmul(ps[:, b0 + 2, P * c:P * c + P], vnew[z][:], w[PM][:, c, :], start=True, stop=c == 0)
                        if c:
                            pe.matmul(ps[:, b0 + 2, P * c:P * c + P], state[z][:], w[QG][:, c, :], start=False, stop=True)
                        pe.matmul(ps[:, b0 + 3, 0:P], w[KD][:, c, :], vnew[z][:], start=True, stop=True).then_inc(S("dn_sp"), 1)
                for z, hh, b0, w in both:
                    pe.wait_ge(S("dn_osq"), hh + 1)
                    pe.matmul(ps[:, b0 + 3, :], ones[:, 0:P], (sqa, t_osq)[z][:, 0:SEQ], start=True, stop=True)\
                      .then_inc(S("dn_osum"), 1)
            pe.wait_ge(S("dn_ovar"), 2 * DH)
            pe.wait_ge(S("dn_o"), 1)
            gemm(pe, "dn_out", mh, ml, SEQ, ready=(S("dn_o"), 0))
            stats_pe(pe, 8, SEQ)

        def dn_act(act):
            stats_act(act, 7, SEQ)
            slabs_act(act, "ab")
            conv_stage_act(act, "dn_qk", 24, None, CONV0["dn_in"], SEQ, lambda k: tile_of(X, k, SEQ))
            conv_stage_act(act, "dn_v", 40, None, CONV0["dn_in"] + 64, SEQ, lambda k: tile_of(v_tmp, k, SEQ))

            def z_body(j, i):
                slab_hi(act, SLAB0["dn_z"] + j, i)
                act.wait_ge(S("tile_taken"), taken("dn_z", j, i))
                zt = tile_of(zd_t, j + 4 * i, SEQ)
                act.activation(zt, zt, ACT.Silu).then_inc(S("dn_z_silu"), 1)
            steps(act, "dn_z", z_body)
            act.wait_ge(S("slab_done"), SLAB0["dn_out"])
            sem = S("dn_softplus")
            softplus_act(act, sem, 0, ab_t[R8, 0:SEQ], col("dn_dt_bias_2", 0, R8),
                         big[0][R8].rearrange("p a b -> p (a b)"), big[1][R8].rearrange("p a b -> p (a b)"))
            act.activation(dneg[R8, :], col("dn_a_log_2", 0, R8), ACT.Exp).then_inc(sem, 1)
            for t in range(16):
                act.wait_ge(S("l2_var"), 2 * t + 2)
                act.activation(t2[:, t % 2, 0:SEQ], t1[:, t % 2, 0:SEQ], ACT.Sqrt).then_inc(S("l2_r"), 1)
            act.activation(ab_t[RB, 0:SEQ], ab_t[RB, 0:SEQ], ACT.Sigmoid).then_inc(sem, 1)
            act.wait_ge(S("dn_tok"), 1)
            act.activation(nbe_tok[:].rearrange("p a b -> p (a b)"), gc_tok[:].rearrange("p a b -> p (a b)"),
                           ACT.Exp).then_inc(sem, 1)
            for pr in range(DH // 2):
                both = [(z, 2 * pr + z, 4 * z, buf[z]) for z in range(2)]
                for z, hh, b0, w in both:
                    act.wait_ge(S("dn_dm"), hh + 1)
                    act.activation(w[DM][:], w[DM][:], ACT.Exp).then_inc(S("dn_edm"), 1)
                    act.activation(w[QG][:].rearrange("p a b -> p (a b)"), ps[:, b0, :], ACT.Exp).then_inc(S("dn_egc"), 1)
                    for c in range(CH):
                        act.activation(kfac[z][:, c:c + 1], gc_tok[:, c, hh:hh + 1], ACT.Exp, scale=-1.0,
                                       bias=glast[z][:, c:c + 1])
                    act.activation(eglast[z][:], glast[z][:], ACT.Exp).then_inc(S("dn_kf"), 1)
                for z, hh, b0, w in both:
                    act.wait_ge(S("dn_ovar"), 2 * hh + 2)
                    act.activation(w[BV][:].rearrange("p a b -> p (a b)"), w[KB][:].rearrange("p a b -> p (a b)"),
                                   ACT.Sqrt).then_inc(S("dn_ors"), 1)
                for z, hh, b0, w in both:
                    act.wait_ge(S("dn_ofull"), 2 * hh + 2)
                    act.activation(mh[:, hh, 0:SEQ], w[LT][:].rearrange("p a b -> p (a b)"), ACT.Copy)\
                       .then_inc(S("dn_o_hi"), 1)
            residual_act(act, "dn_out", SEQ, 8, (8, "mlp_norm_2", KT))

        def dn_dve(dve):
            stats_dve(dve, 7, SEQ)
            slab_lo(dve, SLAB0["ab"])
            dve.wait_ge(S("stat_ready"), 8)
            dve.wait_ge(S("sumsq"), 15 * 8)
            take_scaled(dve, "ab", 0, 0, ab_t[:, 0:SEQ], SEQ)
            conv_stage_dve(dve, "dn_qk", 24, "dn_conv_w_2", CONV0["dn_in"], SEQ)
            conv_stage_dve(dve, "dn_v", 40, "dn_conv_w_2", CONV0["dn_in"] + 64, SEQ)
            scaled_stage_dve(dve, "dn_z", lambda k: tile_of(zd_t, k, SEQ), SEQ)
            dve.wait_ge(S("slab_done"), SLAB0["dn_out"])
            for t in range(16):
                dve.wait_ge(S("l2_sum"), t + 1)
                if t >= 2:
                    dve.wait_ge(S("l2_r"), t - 1)
                dve.tensor_scalar(t1[:, t % 2, 0:SEQ], ps[:, t % 4, :], EPS, 128.0 if t < 8 else 1.0, ALU.add, ALU.mult)\
                   .then_inc(S("l2_var"), 1)
                dve.wait_ge(S("l2_var"), 2 * t + 1)
                dve.reciprocal(t1[:, t % 2, 0:SEQ], t1[:, t % 2, 0:SEQ]).then_inc(S("l2_var"), 1)
                dve.wait_ge(S("l2_r"), t + 1)
                dve.tensor_tensor(X[:, t, 0:SEQ], X[:, t, 0:SEQ], t2[:, t % 2, 0:SEQ], ALU.mult).then_inc(S("l2_done"), 1)
            sem = S("dn_rows")
            flat = [w[R8].rearrange("p a b -> p (a b)") for w in big[0:5]]
            softplus_dve(dve, sem, 0, S("dn_softplus"), 3, ab_t[R8, 0:SEQ], col("dn_dt_bias_2", 0, R8), flat[0], flat[1],
                         flat[2], flat[3], flat[4])
            dve.wait_ge(S("dn_softplus"), 4)
            dve.tensor_scalar(dneg[R8, :], dneg[R8, :], -1.0, None, ALU.mult).then_inc(sem, 1)
            dve.wait_ge(sem, 10)
            dve.tensor_scalar(flat[3], flat[4], dneg[R8, :], None, ALU.mult).then_inc(sem, 1)
            dve.wait_ge(sem, 11)
            for c in range(CH):
                dve.tensor_tensor_scan(g_rows[R8, P * c:P * c + P], ones[R8, 0:P], flat[3][:, P * c:P * c + P], 0.0,
                                       ALU.mult, ALU.add).then_inc(S("dn_scan"), 1)
            vtok_dve(dve, B, SEQ, 9)
            vtok_dve(dve, k_tok, SEQ, 13)
            dve.wait_ge(S("dn_rows_t"), 1)
            dve.tensor_copy(gc_tok[:].rearrange("p a b -> p (a b)"), ps[:, 0, 0:32]).then_inc(S("dn_tok"), 1)
            dve.tensor_copy(be_tok[:].rearrange("p a b -> p (a b)"), ps[:, 1, 0:32]).then_inc(S("dn_tok"), 1)
            dve.wait_ge(S("dn_softplus"), 6)
            dve.wait_ge(S("dn_tok"), 2)
            dve.scalar_tensor_tensor(nbe_tok[:].rearrange("p a b -> p (a b)"), nbe_tok[:].rearrange("p a b -> p (a b)"),
                                     -1.0, be_tok[:].rearrange("p a b -> p (a b)"), ALU.mult, ALU.mult)\
               .then_inc(S("dn_nbe"), 1)
            dve.wait_ge(S("dn_nbe"), 1)

            for pr in range(DH // 2):
                both = [(z, 2 * pr + z, 4 * z, buf[z]) for z in range(2)]
                for z, hh, b0, w in both:
                    dve.wait_ge(S("dn_bc"), hh + 1)
                    if pr:
                        dve.wait_ge(S("dn_o"), hh - 1)
                    dve.tensor_tensor(w[KB][:].rearrange("p a b -> p (a b)"), X[:, 8 + hh, 0:SEQ], ps[:, b0 + 1, :],
                                      ALU.mult).then_inc(S("dn_kb"), 1)
                    dve.tensor_copy(glast[z][:], ps[:, b0, P - 1:SEQ:P])
                    for c in range(CH):
                        op = dve.tensor_scalar(w[DM][:, c, :], ps[:, b0, P * c:P * c + P], gc_tok[:, c, hh:hh + 1], 0.0,
                                               ALU.subtract, ALU.min)
                    op.then_inc(S("dn_dm"), 1)
                for z, hh, b0, w in both:
                    dve.wait_ge(S("dn_kk"), hh + 1)
                    dve.wait_ge(S("dn_mask"), hh + 1)
                    dve.tensor_tensor(w[LT][:], ps[:, b0 + 2, :].rearrange("p (a b) -> p a b", a=CH), w[DM][:],
                                      ALU.mult).then_inc(S("dn_lt"), 1)
                    dve.wait_ge(S("dn_lt"), hh + 1)
                    dve.tensor_tensor(w[KB][:], w[LT][:], bcast4(levels[:, 0, :]), ALU.mult).then_inc(S("dn_ltk"), 1)
                    dve.tensor_tensor(w[PM][:], ps[:, b0 + 3, :].rearrange("p (a b) -> p a b", a=CH), w[DM][:], ALU.mult)
                    dve.wait_ge(S("dn_ltk"), 14 * pr + z + 1)
                    dve.tensor_tensor(w[XTM][:], bcast4(ident[:]), w[KB][:], ALU.subtract).then_inc(S("dn_x"), 1)
                    dve.wait_ge(S("dn_pw"), 14 * pr + z + 1)
                    dve.tensor_tensor(w[XM][:], bcast4(ident[:]), ps[:, b0, :].rearrange("p (a b) -> p a b", a=CH),
                                      ALU.subtract).then_inc(S("dn_x"), 1)

                def prepare(z, hh, b0, w):
                    dve.wait_ge(S("dn_kf"), hh + 1)
                    q = w[QG][:].rearrange("p a b -> p (a b)")
                    dve.tensor_tensor(q, q, X[:, hh, 0:SEQ], ALU.mult)
                    for c in range(CH):
                        dve.tensor_scalar(w[BV][:, c, :], B[:, c, P * hh:P * hh + P], be_tok[:, c, hh:hh + 1], None, ALU.mult)
                    for c in range(CH):
                        op = dve.tensor_scalar(w[KD][:, c, :], k_tok[:, c, P * hh:P * hh + P], kfac[z][:, c:c + 1], None, ALU.mult)
                    op.then_inc(S("dn_prep"), 1)

                for k in range(1, 7):
                    for z, hh, b0, w in both:
                        dve.wait_ge(S("dn_pw"), 14 * pr + 2 * (k - 1) + z + 1)
                        if k == 1:
                            dve.wait_ge(S("dn_x"), 28 * pr + 2 * z + 1)
                        dve.tensor_tensor(w[KB][:], w[LT][:], bcast4(levels[:, k, :]), ALU.mult).then_inc(S("dn_ltk"), 1)
                    if k == 1:
                        for one in both:
                            prepare(*one)
                    for z, hh, b0, w in both:
                        dve.wait_ge(S("dn_pw"), 14 * pr + 2 * k + z + 1)
                        dve.tensor_copy(w[DM][:].rearrange("p a b -> p (a b)"), ps[:, b0, :]).then_inc(S("dn_w"), 1)
                    for z, hh, b0, w in both:
                        dve.wait_ge(S("dn_px"), 12 * pr + 2 * (k - 1) + z + 1)
                        for t, bk in ((XTM, 1), (XM, 2)):
                            v = w[t][:].rearrange("p a b -> p (a b)")
                            dve.tensor_tensor(v, v, ps[:, b0 + bk, :], ALU.subtract).then_inc(S("dn_x"), 1)
                for c in range(CH):
                    if c:
                        for z, hh, b0, w in both:
                            dve.wait_ge(S("dn_ks"), 6 * pr + 2 * (c - 1) + z + 1)
                            dve.scalar_tensor_tensor(resid[z][:], ps[:, b0, 0:P], nbe_tok[:, c, hh:hh + 1], w[BV][:, c, :],
                                                     ALU.mult, ALU.add).then_inc(S("dn_resid"), 1)
                    for z, hh, b0, w in both:
                        dve.wait_ge(S("dn_vp"), 8 * pr + 2 * c + z + 1)
                        dve.tensor_copy(vnew[z][:], ps[:, b0 + 1, 0:P]).then_inc(S("dn_vnew"), 1)
                    for z, hh, b0, w in both:
                        dve.wait_ge(S("dn_sp"), 8 * pr + 2 * c + z + 1)
                        if c:
                            dve.wait_ge(S("dn_state"), 8 * pr + 2 * (c - 1) + z + 1)
                            op = dve.scalar_tensor_tensor(state[z][:], state[z][:], eglast[z][:, c:c + 1], ps[:, b0 + 3, 0:P],
                                                          ALU.mult, ALU.add)
                        else:
                            op = dve.tensor_copy(state[z][:], ps[:, b0 + 3, 0:P])
                        op.then_inc(S("dn_state"), 1)
                for z, hh, b0, w in both:
                    dve.tensor_copy(w[LT][:].rearrange("p a b -> p (a b)"), ps[:, b0 + 2, :]).then_inc(S("dn_oraw"), 1)
                for z, hh, b0, w in both:
                    v = w[KB][:].rearrange("p a b -> p (a b)")
                    dve.wait_ge(S("dn_osum"), hh + 1)
                    dve.tensor_scalar(v, ps[:, b0 + 3, :], 1.0 / P, EPS, ALU.mult, ALU.add).then_inc(S("dn_ovar"), 1)
                    dve.wait_ge(S("dn_ovar"), 2 * hh + 1)
                    dve.reciprocal(v, v).then_inc(S("dn_ovar"), 1)
                for z, hh, b0, w in both:
                    v = w[LT][:].rearrange("p a b -> p (a b)")
                    dve.wait_ge(S("dn_ors"), hh + 1)
                    dve.scalar_tensor_tensor(v, v, col("dn_head_norm_2"), w[BV][:].rearrange("p a b -> p (a b)"),
                                             ALU.mult, ALU.mult).then_inc(S("dn_ofull"), 1)
                    dve.wait_ge(S("dn_ofull"), 2 * hh + 1)
                    if pr == 0:
                        dve.wait_ge(S("dn_z_silu"), 8)
                    dve.tensor_tensor(v, v, zd_t[:, hh, 0:SEQ], ALU.mult).then_inc(S("dn_ofull"), 1)
                for z, hh, b0, w in both:
                    dve.wait_ge(S("dn_o_hi"), hh + 1)
                    dve.tensor_tensor(ml[:, hh, 0:SEQ], w[LT][:].rearrange("p a b -> p (a b)"),
                                      mh[:, hh, 0:SEQ].bitcast(F32), ALU.subtract).then_inc(S("dn_o"), 1)
            residual_dve(dve, "dn_out", SEQ, (8, "mlp_norm_2", KT))

        def dn_pool(pool):
            pool.wait_ge(S("slab_done"), SLAB0["dn_out"])
            pool.wait_ge(S("tile_taken"), tiles_out("dn_z"))
            for t in range(16):
                if t == 0:
                    pool.wait_ge(S("conv_used"), 2 + 48)
                if t >= 2:
                    pool.wait_ge(S("l2_sum"), t - 1)
                pool.tensor_tensor((sqa if t % 2 else zsq)[:, 0:SEQ], X[:, t, 0:SEQ], X[:, t, 0:SEQ], ALU.mult)\
                    .then_inc(S("l2_sq"), 1)
            for pr in range(DH // 2):
                both = [(z, 2 * pr + z, 4 * z, buf[z]) for z in range(2)]
                for z, hh, b0, w in both:
                    pool.wait_ge(S("dn_edm"), hh + 1)
                    pool.affine_select(out=w[DM][:], in_=w[DM][:], compare_op=ALU.is_ge, fill=0.0, base=0,
                                       pattern=[[0, CH], [1, P]], channel_multiplier=-1).then_inc(S("dn_mask"), 1)
                for z, hh, b0, w in both:
                    pool.wait_ge(S("dn_oraw"), hh + 1)
                    if hh >= 2:
                        pool.wait_ge(S("dn_osum"), hh - 1)
                    v = w[LT][:].rearrange("p a b -> p (a b)")
                    pool.tensor_tensor((sqa, t_osq)[z][:, 0:SEQ], v, v, ALU.mult).then_inc(S("dn_osq"), 1)
            stats_pool(pool, 8, SEQ)

        def ffn_parts(layer, n, xi, n_next, split):
            def pool(e):
                stats_pool(e, n_next, LA)

            def tensor(e):
                ffn_pe(e, layer, xi)
                stats_pe(e, n_next, LA)
            return (tensor, lambda e: ffn_dve(e, layer, n, split), lambda e: ffn_act(e, layer, n, n_next, split), pool)

        def mlp_parts(layer, n, xi, n_next, split):
            def pool(e):
                stats_pool(e, n_next, SEQ)

            def tensor(e):
                mlp_pe(e, layer, xi)
                stats_pe(e, n_next, SEQ)
            return (tensor, lambda e: mlp_dve(e, layer, n, split), lambda e: mlp_act(e, layer, n, n_next, split), pool)

        def finish_dve(dve):
            stats_dve(dve, 9, SEQ)
            for kt in range(KT):
                dve.scalar_tensor_tensor(hv(kt, SEQ), hv(kt, SEQ), col("final_norm_2", kt), rstd[:, 0:SEQ],
                                         ALU.mult, ALU.mult).then_inc(S("y_done"), 1)

        nothing = lambda e: None
        ffn0 = ffn_parts(0, 1, 1, 2, (2, "kv_norm", 0))
        ffn1 = ffn_parts(1, 3, 4, 4, None)
        mlp0 = mlp_parts(0, 6, 6, 7, (7, "dn_norm_2", 0))
        mlp1 = mlp_parts(1, 8, 8, 9, None)
        parts = [(ssd_pe, ssd_dve, ssd_act, ssd_pool), ffn0, (sb_pe, sb_dve, sb_act, sb_pool), ffn1,
                 (nothing, join_dve, join_act, nothing), (rel_pe, rel_dve, rel_act, rel_pool), mlp0,
                 (dn_pe, dn_dve, dn_act, dn_pool), mlp1, (nothing, finish_dve, lambda e: stats_act(e, 9, SEQ), nothing)]
        pe_parts, dve_parts, act_parts, pool_parts = [[(n, p[k]) for n, p in enumerate(parts)] for k in range(4)]
        ends = ["ssd_out", "ffn0_down2", "sb_out", "ffn1_down2", "ffn1_down2", "rel_out", "mlp0_down3", "dn_out"]
        end_slab = N_SLABS
        if last < len(ends):
            end_slab = min(N_SLABS, SLAB0[ends[last]] + TILES[ends[last]] * KGS[ends[last]] + AHEAD)
        block = ctx.enter_context(nc.Block())

        @block.sync
        def _(sp):
            sp.dma_start(w_raw[:, 0, :], slabs[0]).then_inc(S("w_loaded0"), 16)
            sp.dma_start(h[:], x_in).then_inc(S("x_loaded"), 16)
            sp.dma_start(par[:], params).then_inc(S("par_loaded"), 16)
            for n in range(1, RING):
                sp.dma_start(w_raw[:, n, :], slabs[n]).then_inc(S(f"w_loaded{n}"), 16)
            sp.dma_start(cst[:], consts_in).then_inc(S("par_loaded"), 16)
            n_run = end_slab
            with sp.Fori(1, n_run // RING) as i:
                for j in range(RING):
                    sp.wait_ge(S("slab_done"), 4 * i + (j + 1 - RING))
                    sp.dma_start(w_raw[:, j, :], slabs[bass.ds(4 * i + j, 1)].rearrange("a p n -> (a p) n"))\
                      .then_inc(S(f"w_loaded{j}"), 16)
            for n in range(n_run // RING * RING, n_run):
                sp.wait_ge(S("slab_done"), n - RING + 1)
                sp.dma_start(w_raw[:, n % RING, :], slabs[n]).then_inc(S(f"w_loaded{n % RING}"), 16)
            if last < 9:
                sp.wait_ge(S("dbg"), 1)
                sp.dma_start(out, h[:]).then_inc(S("out_stored"), 16)
                sp.wait_ge(S("out_stored"), 16)
            else:
                for kt in range(KT):
                    sp.wait_ge(S("y_done"), kt + 1)
                    sp.dma_start(out[:, kt, :], hv(kt, SEQ)).then_inc(S("out_stored"), 16)
                sp.wait_ge(S("out_stored"), 16 * KT)

        @block.gpsimd
        def _(pool):
            for want, part in pool_parts:
                if want <= last:
                    part(pool)

        @block.scalar
        def _(act):
            act.sem_inc(S("conv_used"), 2)
            act.wait_ge(S("par_loaded"), 32)
            for s in range(AHEAD):
                slab_hi(act, s - AHEAD)
            for want, part in act_parts:
                if want <= last:
                    part(act)

        @block.vector
        def _(dve):
            dve.sem_inc(S("tile_taken"), 2)
            dve.memset(pad[:, :, 0:3], 0.0).then_inc(S("pad_zero"), 1)
            dve.wait_ge(S("par_loaded"), 32)
            dve.wait_ge(S("pad_zero"), 1)
            for s in range(AHEAD):
                slab_lo(dve, s - AHEAD)
            for want, part in dve_parts:
                if want <= last:
                    part(dve)
            if last < 9:
                dve.wait_ge(S("tile_taken"), 1)
                dve.drain()
                dve.memset(t2[:, 0, 0:1], 0.0).then_inc(S("dbg"), 1)

        @block.tensor
        def _(pe):
            pe.wait_ge(S("par_loaded"), 32)
            for want, part in pe_parts:
                if want <= last:
                    part(pe)


def slab_rows(np, w, cols=None):
    k, m = w.shape
    kg = -(-k // D)
    w = np.pad(w, ((0, kg * D - k), (0, -m % P)))
    w = w.reshape(kg, KT, P, w.shape[1] // P, P)
    return np.ascontiguousarray(w.transpose(3, 0, 2, 1, 4)).reshape(-1, P, D)


def tiles_of(a):
    n = a.shape[0] // P
    return a.reshape(n, P, -1).transpose(1, 0, 2).reshape(P, -1)


def column(np, a):
    return np.pad(a.reshape(-1, 1), ((0, P - a.size), (0, 0)))


def interleave(np, w):
    lead = w.shape[:-1]
    return w.reshape(*lead, 2, FT, P).swapaxes(-3, -2).reshape(*lead, 2 * FF)


def host_arrays(np, a):
    ssd = a["ssd_w_in"][0]
    z, xs, bc, dt = np.split(ssd, [SSM_IN, 2 * SSM_IN, 2 * SSM_IN + 1024], axis=1)
    slabs = [slab_rows(np, w) for w in (dt, bc, xs, z, a["ssd_w_out"][0])]

    def ffn(layer):
        up, down = interleave(np, a["ffn_w_up"][layer]), a["ffn_w_down"][layer]
        at = 0
        for k in FFN_ROUNDS:
            slabs.append(slab_rows(np, up[:, 2 * P * at:2 * P * (at + k)]))
            slabs.append(slab_rows(np, down[P * at:P * (at + k)]))
            at += k

    def mlp(layer):
        for r in range(MT // KT):
            slabs.append(slab_rows(np, a["mlp_w_up_2"][layer][:, D * r:D * (r + 1)]))
            slabs.append(slab_rows(np, a["mlp_w_down_2"][layer][D * r:D * (r + 1)]))

    ffn(0)
    slabs += [slab_rows(np, w) for w in (a["w_kv"], a["sb_w_q"][0], a["sb_w_o"][0])]
    ffn(1)
    slabs += [slab_rows(np, w) for w in (a["attn_w_qkv_2"][0], a["attn_w_o_2"][0])]
    mlp(0)
    dn = a["dn_w_in_2"][0]
    ab = np.concatenate([np.pad(dn[:, 4 * D:4 * D + 8], ((0, 0), (0, 24))), dn[:, 4 * D + 8:]], axis=1)
    slabs += [slab_rows(np, w) for w in (ab, dn[:, :4 * D], a["dn_w_o_2"][0])]
    mlp(1)

    conv = np.concatenate([a["ssd_conv_w"][0][:, SSM_IN:], a["ssd_conv_w"][0][:, :SSM_IN]], axis=1).T
    conv_b = np.concatenate([a["ssd_conv_b"][0][SSM_IN:], a["ssd_conv_b"][0][:SSM_IN]])
    values = {
        "ssd_norm": tiles_of(a["ssd_norm"][0]), "ssd_conv_w": tiles_of(conv), "ssd_conv_b": tiles_of(conv_b),
        "ssd_dt_bias": column(np, a["ssd_dt_bias"][0]), "ssd_a_log": column(np, a["ssd_a_log"][0]),
        "ssd_d_skip": tiles_of(np.repeat(a["ssd_d_skip"][0], SSM_IN // SSM_HEADS)),
        "ssd_gate_norm": tiles_of(a["ssd_gate_norm"][0]), "kv_norm": tiles_of(a["kv_norm"]),
        "sb_norm": tiles_of(a["sb_norm"][0]), "ffn_norm": tiles_of(a["ffn_norm"].reshape(-1)),
        "ffn_conv_w": np.concatenate([tiles_of(interleave(np, a["ffn_conv_w"][i]).T) for i in range(2)], axis=1),
        "ffn_conv_b": np.concatenate([tiles_of(interleave(np, a["ffn_conv_b"][i])) for i in range(2)], axis=1),
        "final_norm": tiles_of(a["final_norm"]), "attn_norm_2": tiles_of(a["attn_norm_2"][0]),
        "dn_norm_2": tiles_of(a["dn_norm_2"][0]), "dn_conv_w_2": tiles_of(a["dn_conv_w_2"][0].T),
        "dn_a_log_2": column(np, a["dn_a_log_2"][0]), "dn_dt_bias_2": column(np, a["dn_dt_bias_2"][0]),
        "dn_head_norm_2": column(np, a["dn_head_norm_2"][0]), "mlp_norm_2": tiles_of(a["mlp_norm_2"].reshape(-1)),
        "final_norm_2": tiles_of(a["final_norm_2"]),
    }
    params = np.concatenate([values[n] for n, _ in PARAM_COLS], axis=1)
    assert params.shape == (P, N_PARAM)

    x = np.concatenate([a["meta_tokens"], a["x"][0]], axis=0).T
    rel = np.pad(a["attn_rel_bias_2"][0], ((0, 0), (0, 255)), mode="edge")[:, ::-1][:, :REL_ROW]

    r, c = np.arange(P)[:, None], np.arange(P)[None, :]
    level = [((r >> (k + 1)) == (c >> (k + 1))) & ((c >> k) & 1 == 1) & ((r >> k) & 1 == 0) for k in range(7)]
    one = np.ones((P, P))
    consts = np.concatenate([r == c, -one, -1.0 * (r >= c), r <= c, r + c == P - 1, *level, np.ones((P, LA))], axis=1)
    return {
        "slabs": np.concatenate(slabs, axis=0), "params": params,
        "x": x.reshape(KT, P, LA).transpose(1, 0, 2), "rel": rel, "consts": consts.astype(np.float32),
    }


_LAST = 99


def kernel(**inputs):
    import numpy as np
    import concourse.bacc as bacc
    from concourse.bass_utils import run_bass_kernel_spmd as run

    arrays = {k: np.ascontiguousarray(v) for k, v in host_arrays(np, {k: np.asarray(v) for k, v in inputs.items()}).items()}
    assert arrays["slabs"].shape[0] == N_SLABS
    nc = bacc.Bacc("TRN2", target_bir_lowering=False, num_devices=1)
    names = ("slabs", "params", "x", "rel", "consts")
    aps = [nc.dram_tensor(f"in_{n}", arrays[n].shape, F32, kind="ExternalInput").ap() for n in names]
    width = SEQ if _LAST >= 9 else LA
    out = nc.dram_tensor("out_y", (P, KT, width), F32, kind="ExternalOutput").ap()
    build_program(nc, *aps, out, _LAST)
    r = run(nc, [{f"in_{n}": arrays[n] for n in names}], core_ids=[0])
    y = r.results[0]["out_y"]
    return np.ascontiguousarray(y.transpose(2, 1, 0)[-SEQ:]).reshape(1, SEQ, D)
```

```python
from contextlib import ExitStack

import concourse.bass as bass
from concourse import mybir

F32 = mybir.dt.float32
F32R = mybir.dt.float32r
ACT = mybir.ActivationFunctionType
ALU = mybir.AluOpType
AX = mybir.AxisListType.X

P = 128
D = 1024
KT = D // P
META = 16
SEQ = 512
LA = META + SEQ
EPS = 1e-6
SSM_IN = 2048
GROUPS = 4
SSM_HEADS = 32
HPG = SSM_HEADS // GROUPS
XT = SSM_IN // P
FF = 2816
FT = FF // P
FFN_ROUNDS = [8, 8, FT - 16]
MT = 4096 // P
RING = 4
AHEAD = 2
BIG = 1e30

PARAM_COLS = [
    ("ssd_norm", KT), ("ssd_conv_w", 24 * 4), ("ssd_conv_b", 24), ("ssd_dt_bias", 1), ("ssd_a_log", 1),
    ("ssd_d_skip", XT), ("ssd_gate_norm", XT), ("kv_norm", KT), ("sb_norm", KT), ("ffn_norm", 2 * KT),
    ("ffn_conv_w", 2 * 2 * FT * 3), ("ffn_conv_b", 2 * 2 * FT), ("final_norm", KT), ("attn_norm_2", KT),
    ("dn_norm_2", KT), ("dn_conv_w_2", 24 * 4), ("dn_a_log_2", 1), ("dn_dt_bias_2", 1),
    ("dn_head_norm_2", 1), ("mlp_norm_2", 2 * KT), ("final_norm_2", KT),
]
PARAM_AT = {}
_n = 0
for _name, _c in PARAM_COLS:
    PARAM_AT[_name] = _n
    _n += _c
N_PARAM = _n
N_CONST = 12 * P + LA
REL_ROW = 640

STAGES = [("dt", 1, 1), ("bc", 8, 1), ("xs", 16, 1), ("z", 16, 1), ("ssd_out", 8, 2)]


def _ffn_stages(layer):
    for r, k in enumerate(FFN_ROUNDS):
        yield (f"ffn{layer}_up{r}", 2 * k, 1)
        yield (f"ffn{layer}_down{r}", KT, 1)


def _mlp_stages(layer):
    for r in range(MT // KT):
        yield (f"mlp{layer}_up{r}", KT, 1)
        yield (f"mlp{layer}_down{r}", KT, 1)


STAGES += list(_ffn_stages(0)) + [("kv", 16, 1), ("q", 8, 1), ("sb_out", 8, 1)] + list(_ffn_stages(1))
STAGES += [("rq", 8, 1), ("rk", 8, 1), ("rv", 8, 1), ("rel_out", 8, 1)] + list(_mlp_stages(0))
STAGES += [("ab", 1, 1), ("dn_qk", 16, 1), ("dn_v", 8, 1), ("dn_z", 8, 1), ("dn_out", 8, 1)] + list(_mlp_stages(1))
SLAB0, TILE0, TILES, KGS = {}, {}, {}, {}
_s = _t = 0
for _name, _tiles, _kgs in STAGES:
    SLAB0[_name], TILE0[_name], TILES[_name], KGS[_name] = _s, _t, _tiles, _kgs
    _s += _tiles * _kgs
    _t += _tiles
N_SLABS = _s

NORM_AFTER = [None, "ssd_out", "ffn0_down2", "sb_out", "ffn1_down2", None, "rel_out", "mlp0_down3",
              "dn_out", "mlp1_down3"]
CONV0 = {"ffn0": 96, "ffn1": 96 + 132, "dn_in": 96 + 264}
MID0 = {"ffn0": 0, "ffn1": FT, "mlp0": 2 * FT, "mlp1": 2 * FT + MT}

LBLK = [(128 * i, min(P, LA - 128 * i), LA - 128 * i) for i in range(5)]
LOFF = [0, 528, 928, 1200, 1344]
LPK = 1360
LBANK = [[(0, 0, 0, 256), (1, 0, 256, 272)], [(2, 0, 128, 400)], [(3, 0, 256, 272)],
         [(3, 272, 384, 144)], [(3, 416, 512, 16)]]


def build_program(nc, slabs, params, x_in, rel_in, consts_in, out):
    ctx = ExitStack()
    with ctx:
        sems = {}

        def S(name):
            if name not in sems:
                sems[name] = ctx.enter_context(nc.semaphore(name))
            return sems[name]

        cursor = [(nc.sbuf_base + 63) // 64 * 64]

        def place(name, shape, dt=F32, at=None):
            size = 4
            for n in shape[1:]:
                size *= n
            if at is None:
                at = cursor[0]
                cursor[0] += (size + 31) // 32 * 32
            return nc.alloc_sbuf_tensor_at(name, shape, dt, offset=at), at

        def sb(name, *shape, dt=F32, at=None):
            return place(name, [P, *shape], dt, at)[0]

        h = sb("h", KT, LA)
        xh, A0 = place("x_hi", [P, KT, LA], F32R)
        xl, _ = place("x_lo", [P, KT, LA], F32R)
        A_SIZE = 2 * KT * LA * 4
        w_raw, W0 = place("w_raw", [P, RING, D])
        w_low = sb("w_low", RING, D, dt=F32R, at=W0)
        w_high = sb("w_high", RING, D, dt=F32R)
        mh, M0 = place("mid_hi", [P, KT, LA], F32R)
        ml, M1 = place("mid_lo", [P, KT, LA], F32R)
        X, X0 = place("mix_x", [P, 16, LA])
        B, B0 = place("mix_b", [P, 5, D])
        z_t = sb("z_t", XT, LA, at=M0)
        bc_t = sb("bc_t", 8, LA, at=B0)
        hg_hi = sb("hg_hi", XT, LA, dt=F32R, at=M0)
        hg_lo = sb("hg_lo", XT, LA, dt=F32R, at=X0)
        v_tmp = sb("v_tmp", KT, LA, at=M0)
        zd_t = sb("zd_t", KT, LA, at=M1)

        rstd = sb("rstd", LA)
        rvar = sb("rvar", LA)
        sqa = sb("sqa", LA)
        sqb = sb("sqb", LA)
        eps_col = sb("eps", 1)
        par = sb("par", N_PARAM)
        cst = sb("consts", N_CONST)
        ident = cst[:, 0:P]
        neg_ones = cst[:, P:2 * P]
        neg_tri = cst[:, 2 * P:3 * P]
        causal = cst[:, 3 * P:4 * P]
        flip = cst[:, 4 * P:5 * P]
        levels = cst[:, 5 * P:12 * P].rearrange("p (k n) -> p k n", k=7)
        ones = cst[:, 12 * P:N_CONST]
        pad, PAD_AT = place("conv_in", [P, 2, 3 + LA])
        cacc, CACC_AT = place("conv_acc", [P, 2, LA])
        t1, T1_AT = place("t1", [P, 2, LA])
        t2, T2_AT = place("t2", [P, 2, LA])
        C0 = cursor[0]
        C_SIZE = nc.sbuf_usable_end - C0
        ps = ctx.enter_context(nc.psum_tensor("ps", [P, 8, 512], F32))

        def scratch(prefix, start, size):
            at = [start]

            def take(name, *shape):
                at[0] = (at[0] + 31) // 32 * 32
                n = 4
                for s in shape:
                    n *= s
                at[0] += n
                assert at[0] <= start + size, (prefix, name, at[0] - start - size)
                return sb(prefix + name, *shape, at=at[0] - n)
            return take

        def col(name, k=0, rows=slice(0, P)):
            return par[rows, PARAM_AT[name] + k:PARAM_AT[name] + k + 1]

        def rcol(name, base, step_expr):
            return par[:, bass.ds(PARAM_AT[name] + base + step_expr, 1)]

        def ps_tile(slot, T):
            return ps[:, 2 * slot:2 * slot + 2, 0:264] if T == LA else ps[:, 2 * slot, 0:SEQ]

        def halves(T):
            return ((0, 264), (264, 264)) if T == LA else ((0, SEQ),)

        def cut(ap, T):
            return ap.rearrange("p (a b) -> p a b", a=2) if T == LA else ap

        def hv(kt, T):
            return h[:, kt, LA - T:LA]

        def after_residual(n, kt):
            if n == 0:
                return S("x_loaded"), 16
            if n == 5:
                return S("x2_done"), kt + 1
            return S("tile_taken"), 2 + TILE0[NORM_AFTER[n]] + kt + 1

        def slab_hi(act, s, i=0):
            n = s + AHEAD
            act.wait_ge(S(f"w_loaded{n % RING}"), 16 * (n // RING + 1) + 16 * i)
            act.activation(w_high[:, n % RING, :], w_raw[:, n % RING, :], ACT.Copy).then_inc(S("w_hi"), 1)

        def slab_lo(dve, s, i=0):
            n = s + AHEAD
            dve.wait_ge(S("w_hi"), n + 1 + 4 * i)
            dve.tensor_tensor(w_low[:, n % RING, :], w_raw[:, n % RING, :],
                              w_high[:, n % RING, :].bitcast(F32), ALU.subtract).then_inc(S("w_lo"), 1)

        def steps(eng, name, body, lastloop=False):
            n = TILES[name] * KGS[name]
            if n < RING or n == RING:
                for j in range(n):
                    body(j, 0)
                return
            with eng.Fori(0, n // RING) as i:
                for j in range(RING):
                    body(j, i)

        def gemm(pe, name, hi, lo, T, blocks=KT, ready=None, between=None, norm=None):
            s0, t0, kgs = SLAB0[name], TILE0[name], KGS[name]

            def body(j, i):
                slot, kg = (s0 + j) % RING, j % kgs
                tslot = (t0 + j // kgs) % 2
                pe.wait_ge(S("w_lo"), s0 + j + 1 + 4 * i)
                if kg == 0:
                    pe.wait_ge(S("tile_taken"), t0 + j // kgs + 1 + (4 // kgs) * i)
                for b in range(blocks):
                    kb = kg * KT + b
                    if ready is not None and j < kgs:
                        pe.wait_ge(ready[0], ready[1] + kb + 1)
                    wh = w_high[:, slot, b * P:(b + 1) * P]
                    wl = w_low[:, slot, b * P:(b + 1) * P]
                    end = kg == kgs - 1 and b == blocks - 1
                    for w, a, first, fin in ((wh, hi, kb == 0, False), (wh, lo, False, False), (wl, hi, False, end)):
                        for k, (c, n) in enumerate(halves(T)):
                            mm = pe.matmul(ps[:, 2 * tslot + k, 0:n], w, a[:, kb, c:c + n], start=first, stop=fin)
                mm.then_inc(S("slab_done"), 1)
            if norm is not None:
                n = TILES[name] * kgs
                body(0, 0)
                stats_pe(pe, norm, T)
                for j in range(1, min(n, RING)):
                    body(j, 0)
                if n > RING:
                    with pe.Fori(1, n // RING) as i:
                        for j in range(RING):
                            body(j, i)
                return
            if between is None:
                steps(pe, name, body)
                return
            for j in range(TILES[name] * kgs):
                body(j, 0)
                between(j)

        def taken(name, j, i, per=4):
            return 2 + TILE0[name] + j + 1 + per * i

        def take_scaled(dve, name, j, i, dst, T, scale=None):
            dve.wait_ge(S("slab_done"), SLAB0[name] + j + 1 + 4 * i)
            src = ps_tile((TILE0[name] + j) % 2, T)
            if scale is None:
                op = dve.tensor_tensor(cut(dst, T), src, cut(rstd[:, 0:T], T), ALU.mult)
            else:
                op = dve.scalar_tensor_tensor(cut(dst, T), src, scale, cut(rstd[:, 0:T], T), ALU.mult, ALU.mult)
            op.then_inc(S("tile_taken"), 1)

        def conv_taps(dve, name, j, i, width, wcol, conv0, T):
            src, acc = pad[:, j % 2, :], cacc[:, j % 2, 0:T]
            off = 4 - width
            dve.wait_ge(S("tile_taken"), taken(name, j, i))
            dve.tensor_scalar(acc, src[:, off:off + T], wcol(0), None, ALU.mult).then_inc(S("conv"), 1)
            for k in range(1, width):
                dve.wait_ge(S("conv"), conv0 + width * j + k + width * 4 * i)
                dve.scalar_tensor_tensor(acc, src[:, off + k:off + k + T], wcol(k), acc,
                                         ALU.mult, ALU.add).then_inc(S("conv"), 1)

        def split_hi(act, n, xi, kt, gain, T, gk=0):
            sem, v = after_residual(n, kt)
            act.wait_ge(sem, v)
            act.activation(xh[:, kt, 0:T], hv(kt, T), ACT.Copy, scale=col(gain, gk + kt)).then_inc(S("x_hi"), 1)

        def split_lo(dve, xi, kt, gain, T, gk=0):
            dve.wait_ge(S("x_hi"), KT * xi + kt + 1)
            dve.scalar_tensor_tensor(xl[:, kt, 0:T], hv(kt, T), col(gain, gk + kt), xh[:, kt, 0:T].bitcast(F32),
                                     ALU.mult, ALU.subtract).then_inc(S("x_lo"), 1)

        def residual_dve(dve, name, T, split=None):
            s0, kgs = SLAB0[name], KGS[name]
            for u in range(KT):
                for kg in range(kgs):
                    s = s0 + u * kgs + kg
                    if s + AHEAD < N_SLABS:
                        slab_lo(dve, s)
                dve.wait_ge(S("slab_done"), s0 + (u + 1) * kgs)
                dve.tensor_tensor(cut(hv(u, T), T), ps_tile((TILE0[name] + u) % 2, T), cut(hv(u, T), T),
                                  ALU.add).then_inc(S("tile_taken"), 1)
                if split and u >= 1:
                    split_lo(dve, split[0], u - 1, split[1], T, split[2])
            if split:
                split_lo(dve, split[0], KT - 1, split[1], T, split[2])

        def residual_act(act, name, T, n=None, split=None):
            s0, kgs = SLAB0[name], KGS[name]
            for u in range(KT):
                for kg in range(kgs):
                    s = s0 + u * kgs + kg
                    if s + AHEAD < N_SLABS:
                        slab_hi(act, s)
                if split:
                    split_hi(act, n, split[0], u, split[1], T, split[2])

        def stats_pool(pool, n, T):
            c = 15 * n
            for kt in range(KT):
                sem, v = after_residual(n, kt)
                pool.wait_ge(sem, v)
                if kt == 0:
                    if n:
                        pool.wait_ge(S("stat_ready"), n)
                    pool.tensor_tensor(sqa[:, 0:T], hv(0, T), hv(0, T), ALU.mult).then_inc(S("sumsq"), 1)
                    c += 1
                    continue
                pool.wait_ge(S("sumsq"), c)
                pool.tensor_tensor(sqb[:, 0:T], hv(kt, T), hv(kt, T), ALU.mult).then_inc(S("sumsq"), 1)
                pool.wait_ge(S("sumsq"), c + 1)
                pool.tensor_tensor(sqa[:, 0:T], sqa[:, 0:T], sqb[:, 0:T], ALU.add).then_inc(S("sumsq"), 1)
                c += 2

        def stats_pe(pe, n, T):
            pe.wait_ge(S("sumsq"), 15 * (n + 1))
            for k, (c, m) in enumerate(halves(T)):
                mm = pe.matmul(ps[:, 4 + k, 0:m], ones[:, 0:P], sqa[:, c:c + m], start=True, stop=True)
            mm.then_inc(S("stat_ready"), 1)

        def stats_dve(dve, n, T):
            dve.wait_ge(S("stat_ready"), n + 1)
            dve.tensor_scalar(cut(rvar[:, 0:T], T), ps_tile(2, T), 1.0 / D, EPS, ALU.mult, ALU.add)\
               .then_inc(S("stat_var"), 1)
            dve.wait_ge(S("stat_var"), 2 * n + 1)
            dve.reciprocal(rvar[:, 0:T], rvar[:, 0:T]).then_inc(S("stat_var"), 1)
            dve.wait_ge(S("rstd_ready"), n + 1)

        def stats_act(act, n, T):
            act.wait_ge(S("stat_var"), 2 * (n + 1))
            act.activation(rstd[:, 0:T], rvar[:, 0:T], ACT.Sqrt).then_inc(S("rstd_ready"), 1)

        def ffn_pe(pe, layer, n, xi):
            pair = 0
            for r, k in enumerate(FFN_ROUNDS):
                gemm(pe, f"ffn{layer}_up{r}", xh, xl, LA, ready=(S("x_lo"), KT * xi) if r == 0 else None,
                     norm=n if r == 0 else None)
                gemm(pe, f"ffn{layer}_down{r}", mh, ml, LA, k, ready=(S("mid_lo"), MID0[f"ffn{layer}"] + pair))
                pair += k

        def ffn_dve(dve, layer, n, split):
            stats_dve(dve, n, LA)
            pair = 0
            for r, k in enumerate(FFN_ROUNDS):
                name = f"ffn{layer}_up{r}"
                conv0 = CONV0[f"ffn{layer}"] + 6 * pair
                mid0 = MID0[f"ffn{layer}"] + pair
                g0 = layer * FT + pair

                def hid_lo(q, i):
                    dve.wait_ge(S("mid_hi"), mid0 + q + 1 + 2 * i)
                    dve.tensor_tensor(ml[:, bass.ds(q + 2 * i, 1), :].rearrange("p a t -> p (a t)"), t1[:, q, :],
                                      mh[:, bass.ds(q + 2 * i, 1), :].rearrange("p a t -> p (a t)").bitcast(F32),
                                      ALU.subtract).then_inc(S("mid_lo"), 1)

                def body(j, i):
                    q = j // 2
                    tile = layer * 2 * FT + 2 * pair + j
                    take_scaled(dve, name, j, i, pad[:, j % 2, 3:3 + LA], LA)
                    slab_lo(dve, SLAB0[name] + j, i)
                    conv_taps(dve, name, j, i, 3, lambda t: rcol("ffn_conv_w", tile * 3 + t, 12 * i), conv0, LA)
                    if j == 2:
                        hid_lo(0, i)
                    if j % 2:
                        dve.wait_ge(S("conv"), conv0 + 3 * (j + 1) + 12 * i)
                        dve.wait_ge(S("gate"), g0 + q + 1 + 2 * i)
                        dve.scalar_tensor_tensor(t1[:, q, :], cacc[:, 1, :], rcol("ffn_conv_b", tile, 4 * i),
                                                 t2[:, q, :], ALU.add, ALU.mult).then_inc(S("hidden"), 1)
                    if j == 3:
                        hid_lo(1, i)
                steps(dve, name, body)
                pair += k
                residual_dve(dve, f"ffn{layer}_down{r}", LA, split if r == 2 else None)

        def ffn_act(act, layer, n, n_next, split):
            stats_act(act, n, LA)
            pair = 0
            for r, k in enumerate(FFN_ROUNDS):
                name = f"ffn{layer}_up{r}"
                conv0 = CONV0[f"ffn{layer}"] + 6 * pair
                g0 = layer * FT + pair

                def body(j, i):
                    q = j // 2
                    tile = layer * 2 * FT + 2 * pair + j
                    slab_hi(act, SLAB0[name] + j, i)
                    if j % 2 == 0:
                        act.wait_ge(S("conv"), conv0 + 3 * (j + 1) + 12 * i)
                        act.activation(t2[:, q, :], cacc[:, 0, :], ACT.Silu,
                                       bias=rcol("ffn_conv_b", tile, 4 * i)).then_inc(S("gate"), 1)
                    else:
                        act.wait_ge(S("hidden"), g0 + q + 1 + 2 * i)
                        act.activation(mh[:, bass.ds(q + 2 * i, 1), :].rearrange("p a t -> p (a t)"), t1[:, q, :],
                                       ACT.Copy).then_inc(S("mid_hi"), 1)
                steps(act, name, body)
                pair += k
                residual_act(act, f"ffn{layer}_down{r}", LA, n_next, split if r == 2 else None)

        def mlp_pe(pe, layer, n, xi):
            for r in range(MT // KT):
                gemm(pe, f"mlp{layer}_up{r}", xh, xl, SEQ, ready=(S("x_lo"), KT * xi) if r == 0 else None,
                     norm=n if r == 0 else None)
                gemm(pe, f"mlp{layer}_down{r}", mh, ml, SEQ, ready=(S("mid_lo"), MID0[f"mlp{layer}"] + KT * r))

        def mlp_dve(dve, layer, n, split):
            stats_dve(dve, n, SEQ)
            for r in range(MT // KT):
                name = f"mlp{layer}_up{r}"
                mid0, u0 = MID0[f"mlp{layer}"] + KT * r, 32 * layer + KT * r

                def hid_lo(j, i):
                    dve.wait_ge(S("mid_hi"), mid0 + j + 1 + 4 * i)
                    dve.wait_ge(S("squared"), u0 + j + 1 + 4 * i)
                    dve.tensor_tensor(ml[:, bass.ds(j + 4 * i, 1), 0:SEQ].rearrange("p a t -> p (a t)"),
                                      t2[:, j % 2, 0:SEQ],
                                      mh[:, bass.ds(j + 4 * i, 1), 0:SEQ].rearrange("p a t -> p (a t)").bitcast(F32),
                                      ALU.subtract).then_inc(S("mid_lo"), 1)

                def body(j, i):
                    slab_lo(dve, SLAB0[name] + j, i)
                    dve.wait_ge(S("slab_done"), SLAB0[name] + j + 1 + 4 * i)
                    dve.scalar_tensor_tensor(t1[:, j % 2, 0:SEQ], ps_tile((TILE0[name] + j) % 2, SEQ), 0.0,
                                             rstd[:, 0:SEQ], ALU.max, ALU.mult).then_inc(S("tile_taken"), 1)
                    if j:
                        hid_lo(j - 1, i)
                    dve.wait_ge(S("tile_taken"), taken(name, j, i))
                    dve.tensor_tensor(t2[:, j % 2, 0:SEQ], t1[:, j % 2, 0:SEQ], t1[:, j % 2, 0:SEQ],
                                      ALU.mult).then_inc(S("squared"), 1)
                    if j == 3:
                        hid_lo(3, i)
                steps(dve, name, body)
                residual_dve(dve, f"mlp{layer}_down{r}", SEQ, split if r == 3 else None)

        def mlp_act(act, layer, n, n_next, split):
            stats_act(act, n, SEQ)
            for r in range(MT // KT):
                name = f"mlp{layer}_up{r}"

                def body(j, i):
                    slab_hi(act, SLAB0[name] + j, i)
                    act.wait_ge(S("tile_taken"), taken(name, j, i))
                    act.activation(mh[:, bass.ds(j + 4 * i, 1), 0:SEQ].rearrange("p a t -> p (a t)"),
                                   t1[:, j % 2, 0:SEQ], ACT.Square).then_inc(S("mid_hi"), 1)
                steps(act, name, body)
                residual_act(act, f"mlp{layer}_down{r}", SEQ, n_next, split if r == 3 else None)

        def softplus_act(act, sem, base, x, bias, e, l):
            act.activation(e, x, ACT.Abs, bias=bias).then_inc(sem, 1)
            act.wait_ge(sem, base + 1)
            act.activation(e, e, ACT.Exp, scale=-1.0).then_inc(sem, 1)
            act.wait_ge(sem, base + 2)
            act.activation(l, e, ACT.Ln, bias=1.0).then_inc(sem, 1)

        def softplus_dve(dve, sem, base, act_sem, act_val, x, bias, e, l, u, m, dst):
            def step(k, op):
                op.then_inc(sem, 1)
                dve.wait_ge(sem, base + k)
            dve.wait_ge(act_sem, act_val)
            step(1, dve.tensor_scalar(u, e, 1.0, -1.0, ALU.add, ALU.add))
            step(2, dve.tensor_scalar(m, u, 0.0, None, ALU.is_equal))
            step(3, dve.tensor_tensor(u, u, m, ALU.add))
            step(4, dve.tensor_tensor(l, l, m, ALU.add))
            step(5, dve.reciprocal(u, u))
            step(6, dve.tensor_tensor(l, l, e, ALU.mult))
            step(7, dve.tensor_tensor(l, l, u, ALU.mult))
            step(8, dve.tensor_scalar(m, x, bias, 0.0, ALU.add, ALU.max))
            step(9, dve.tensor_tensor(dst, m, l, ALU.add))

        def tiles_out(name):
            return 2 + TILE0[name] + TILES[name]

        def scaled_stage_dve(dve, name, dst, T, scale=None):
            def body(j, i):
                slab_lo(dve, SLAB0[name] + j, i)
                take_scaled(dve, name, j, i, dst(j + 4 * i), T, scale)
            steps(dve, name, body)

        def slabs_act(act, name):
            steps(act, name, lambda j, i: slab_hi(act, SLAB0[name] + j, i))

        def conv_stage_dve(dve, name, first, wname, conv0, T):
            def body(j, i):
                take_scaled(dve, name, j, i, pad[:, j % 2, 3:3 + T], T)
                slab_lo(dve, SLAB0[name] + j, i)
                dve.wait_ge(S("conv_used"), first + j + 1 + 4 * i)
                conv_taps(dve, name, j, i, 4, lambda t: rcol(wname, 4 * (first % 24 + j) + t, 16 * i), conv0, T)
            steps(dve, name, body)

        def conv_stage_act(act, name, first, bname, conv0, T, dst):
            def body(j, i):
                slab_hi(act, SLAB0[name] + j, i)
                act.wait_ge(S("conv"), conv0 + 4 * (j + 1) + 16 * i)
                kw = {"bias": rcol(bname, first + j, 4 * i)} if bname else {}
                act.activation(dst(j + 4 * i), cacc[:, j % 2, 0:T], ACT.Silu, **kw).then_inc(S("conv_used"), 1)
            steps(act, name, body)

        def tile_of(t, k, T):
            return t[:, bass.ds(k, 1), 0:T].rearrange("p a t -> p (a t)")

        def vtok_pe(pe, src, T, sem, base, first, bank=4):
            for i in range(-(-T // P)):
                n = min(P, T - P * i)
                b = bank + 2 * (i % 2)
                if i >= 2:
                    pe.wait_ge(S("vtok_taken"), first + i - 1)
                if i == 0:
                    pe.wait_ge(sem, base)
                for f in range(KT):
                    mm = pe.transpose(ps[0:n, b + f // 4, P * (f % 4):P * (f % 4 + 1)], src(f)[:, P * i:P * i + n], ident[:])
                mm.then_inc(S("vtok_ready"), 1)

        def vtok_dve(dve, dst, T, first, bank=4):
            for i in range(-(-T // P)):
                n = min(P, T - P * i)
                b = bank + 2 * (i % 2)
                dve.wait_ge(S("vtok_ready"), first + i + 1)
                dve.tensor_copy(dst[0:n, i, :].rearrange("p (a n) -> p a n", a=2), ps[0:n, b:b + 2, :])\
                   .then_inc(S("vtok_taken"), 1)

        take = scratch("ssd_", A0, A_SIZE)
        dec = take("decay", 3, LPK)
        cbm = take("cb", LPK)
        x_tok = take("x_tok", 5, 512)
        dt_tok = take("dt_tok", 5, SSM_HEADS)
        a_tok = take("a_tok", 5, SSM_HEADS)
        a_neg = t1[:, 0, 0:4 * SSM_HEADS].rearrange("p (a b) -> p a b", a=4)
        gsq = [cacc[:, 0, :], cacc[:, 1, :]]
        dt_rows, a_rows = rvar, sqb
        CB_BANK = (0, 1, 4, 5)
        take_c = scratch("ssdc_", C0, C_SIZE)
        dt_in = take_c("dt_in", LA)
        nega = take_c("nega", 1)
        R32 = slice(0, SSM_HEADS)
        HALF = ((0, 0, 256), (1, 256, 272))
        PIECES = []
        for s0_, ns_, nl_ in LBLK:
            PIECES.append([(bk, max(s0_ - l0, 0), max(s0_, l0), l0 + n - max(s0_, l0))
                           for bk, l0, n in HALF if l0 + n > s0_])

        def packed(i, t):
            return LOFF[i] + t - LBLK[i][0]

        def ssd_pe(pe):
            gemm(pe, "dt", xh, xl, LA, ready=(S("x_lo"), 0), norm=0)
            for name in ("bc", "xs", "z"):
                gemm(pe, name, xh, xl, LA)
            pe.wait_ge(S("tile_taken"), tiles_out("z"))
            pe.wait_ge(S("conv_used"), 2 + 24)

            pe.wait_ge(S("ssd_scan"), 1)
            for i, (s0, n, _) in enumerate(LBLK):
                pe.transpose(ps[0:n, 6, 32 * i:32 * i + 32], dt_rows[R32, s0:s0 + n], ident[R32, R32])
            for i, (s0, n, _) in enumerate(LBLK):
                mm = pe.transpose(ps[0:n, 7, 32 * i:32 * i + 32], a_rows[R32, s0:s0 + n], ident[R32, R32])
            mm.then_inc(S("ssd_rows_t"), 1)

            def bcast(hh):
                if hh == 0:
                    pe.wait_ge(S("ssd_tok"), 1)
                if hh >= 2:
                    pe.wait_ge(S("ssd_exp"), hh - 1)
                if hh % HPG == 1:
                    pe.wait_ge(S("ssd_xt_taken"), 5 * (hh // HPG) + 5)
                for bk, l0, n in HALF:
                    mm = pe.matmul(ps[:, 6 * (1 - hh % 2) + bk, 0:n], ident[R32, hh:hh + 1].to_broadcast((SSM_HEADS, P)),
                                   a_rows[R32, l0:l0 + n], start=True, stop=True)
                mm.then_inc(S("ssd_bc"), 1)

            def cb_products(g):
                if g:
                    pe.wait_ge(S("ssd_exp"), HPG * g)
                    pe.wait_ge(S("ssd_y_taken"), 4 * g - 1)
                for i, (s0, n, _) in enumerate(LBLK):
                    for bk, c, t, m in LBANK[i]:
                        mm = pe.matmul(ps[0:n, CB_BANK[bk], c:c + m], bc_t[:, g, s0:s0 + n], bc_t[:, GROUPS + g, t:t + m],
                                       start=True, stop=True)
                mm.then_inc(S("ssd_cb"), 1)

            def x_transposes(g):
                pe.wait_ge(S("ssd_cb_taken"), g + 1)
                for i, (s0, n, _) in enumerate(LBLK):
                    if i == 4:
                        pe.wait_ge(S("ssd_xt_taken"), 5 * g + 1)
                    for f in range(4):
                        mm = pe.transpose(ps[0:n, CB_BANK[i % 4], P * f:P * f + P], X[:, 4 * g + f, s0:s0 + n], ident[:])
                    mm.then_inc(S("ssd_xt"), 1)

            def y_product(hh):
                p, po, e = hh // 2, 64 * (hh % 2), hh % HPG
                yb = 4 if p % 2 == 0 else 2
                if hh % 2 == 0 and p >= 2:
                    pe.wait_ge(S("ssd_y_taken"), p - 1)
                if e == 4 and hh > HPG:
                    pe.wait_ge(S("ssd_gln"), hh // HPG)
                if e == 0:
                    pe.wait_ge(S("ssd_xt_taken"), 5 * (hh // HPG) + 5)
                pe.wait_ge(S("ssd_m"), hh + 1)
                for i, (s0, n, _) in enumerate(LBLK):
                    for bk, c, t, m in PIECES[i]:
                        mm = pe.matmul(ps[po:po + 64, yb + bk, c:c + m], x_tok[0:n, i, 64 * e:64 * e + 64],
                                       dec[0:n, hh % 3, packed(i, t):packed(i, t) + m], start=i == 0,
                                       stop=(bk, i) in ((0, 1), (1, 4)), skip_group_check=True)
                mm.then_inc(S("ssd_y"), 1)

            def group_sum(g):
                pe.wait_ge(S("ssd_gsq"), 7 * (g + 1))
                pe.wait_ge(S("ssd_y_taken"), 4 * g + 5 if g + 1 < GROUPS else 15)
                for k, (c, m) in enumerate(halves(LA)):
                    mm = pe.matmul(ps[:, 4 + k, 0:m], ones[:, 0:P], gsq[g % 2][:, c:c + m], start=True, stop=True)
                mm.then_inc(S("ssd_gsum"), 1)

            bcast(0)
            cb_products(0)
            x_transposes(0)
            bcast(1)
            for hh in range(SSM_HEADS):
                g, e = hh // HPG, hh % HPG
                last_of_group = e == HPG - 1 and g + 1 < GROUPS
                if last_of_group:
                    cb_products(g + 1)
                elif hh + 2 < SSM_HEADS:
                    bcast(hh + 2)
                if e == 3 and g:
                    group_sum(g - 1)
                y_product(hh)
                if last_of_group:
                    x_transposes(g + 1)
                    bcast(hh + 2)
            group_sum(GROUPS - 1)
            pe.wait_ge(S("ssd_exp"), SSM_HEADS)
            pe.wait_ge(S("ssd_gln"), GROUPS)
            pe.wait_ge(S("ssd_y_taken"), 16)
            gemm(pe, "ssd_out", hg_hi, hg_lo, LA, ready=(S("hg_lo"), 0))

        def ssd_act(act):
            for kt in range(KT):
                split_hi(act, 0, 0, kt, "ssd_norm", LA)
            stats_act(act, 0, LA)
            slabs_act(act, "dt")
            conv_stage_act(act, "bc", 0, "ssd_conv_b", 0, LA, lambda k: tile_of(bc_t, k, LA))
            conv_stage_act(act, "xs", 8, "ssd_conv_b", 32, LA, lambda k: tile_of(X, k, LA))

            def z_body(j, i):
                slab_hi(act, SLAB0["z"] + j, i)
                act.wait_ge(S("tile_taken"), taken("z", j, i))
                zt = tile_of(z_t, j + 4 * i, LA)
                act.activation(zt, zt, ACT.Silu).then_inc(S("z_silu"), 1)
            steps(act, "z", z_body)
            act.wait_ge(S("slab_done"), SLAB0["ssd_out"])
            sem = S("ssd_softplus")
            softplus_act(act, sem, 0, dt_in[R32, :], col("ssd_dt_bias", 0, R32), dec[R32, 0, 0:LA], dec[R32, 1, 0:LA])
            act.activation(nega[R32, :], col("ssd_a_log", 0, R32), ACT.Exp).then_inc(sem, 1)

            def decay(hh):
                act.wait_ge(S("ssd_min"), hh + 1)
                d, b0 = dec[:, hh % 3, :], 6 * (1 - hh % 2)
                for i, bk, c, t, m in ((0, 0, 128, 128, 128), (0, 1, 0, 256, 272), (1, 1, 0, 256, 272)):
                    act.activation(d[:, packed(i, t):packed(i, t) + m], ps[:, b0 + bk, c:c + m], ACT.Exp,
                                   bias=a_neg[:, i, hh:hh + 1])
                for v in (d[:, 0:P], d[:, LOFF[1]:LOFF[1] + P], d[:, LOFF[2]:LOFF[4]]):
                    act.activation(v, v, ACT.Exp)
                act.activation(d[0:META, LOFF[4]:LPK], d[0:META, LOFF[4]:LPK], ACT.Exp).then_inc(S("ssd_exp"), 1)

            def group_factor(g):
                act.wait_ge(S("ssd_gsum"), g + 1)
                if g:
                    act.wait_ge(S("ssd_grs"), g)
                    act.wait_ge(S("hg_full"), 4 * g)
                act.activation(cut(rvar[:], LA), ps[:, 4:6, 0:264], ACT.Ln, scale=1.0 / 512, bias=eps_col[:])\
                   .then_inc(S("ssd_gln"), 1)
                act.wait_ge(S("ssd_gln"), g + 1)
                act.activation(rstd[:], rvar[:], ACT.Exp, scale=-0.5).then_inc(S("ssd_grs"), 1)

            def group_hi(g, f):
                t = 4 * g + f
                act.wait_ge(S("hg_full"), t + 1)
                act.activation(hg_hi[:, t, :], X[:, t, :], ACT.Copy).then_inc(S("hg_hi"), 1)

            decay(0)
            decay(1)
            for hh in range(SSM_HEADS):
                g, e = hh // HPG, hh % HPG
                if hh + 2 < SSM_HEADS:
                    decay(hh + 2)
                if g and e == 3:
                    group_factor(g - 1)
                if g and e >= 4:
                    group_hi(g - 1, e - 4)
            group_factor(GROUPS - 1)
            for f in range(4):
                group_hi(GROUPS - 1, f)
            residual_act(act, "ssd_out", LA, 1, (1, "ffn_norm", 0))

        def ssd_dve(dve):
            for kt in range(KT):
                split_lo(dve, 0, kt, "ssd_norm", LA)
            stats_dve(dve, 0, LA)
            slab_lo(dve, SLAB0["dt"])
            take_scaled(dve, "dt", 0, 0, dt_in[:, :], LA)
            conv_stage_dve(dve, "bc", 0, "ssd_conv_w", 0, LA)
            conv_stage_dve(dve, "xs", 8, "ssd_conv_w", 32, LA)
            scaled_stage_dve(dve, "z", lambda k: tile_of(z_t, k, LA), LA)

            sem = S("ssd_rows")
            dve.wait_ge(S("slab_done"), SLAB0["ssd_out"])
            softplus_dve(dve, sem, 0, S("ssd_softplus"), 3, dt_in[R32, :], col("ssd_dt_bias", 0, R32), dec[R32, 0, 0:LA],
                         dec[R32, 1, 0:LA], cbm[R32, 0:LA], cbm[R32, LA:2 * LA], dt_rows[R32, :])
            dve.wait_ge(S("ssd_softplus"), 4)
            dve.tensor_scalar(nega[R32, :], nega[R32, :], -1.0, None, ALU.mult).then_inc(sem, 1)
            dve.wait_ge(sem, 10)
            dve.tensor_scalar(cbm[R32, 0:LA], dt_rows[R32, :], nega[R32, :], None, ALU.mult).then_inc(sem, 1)
            dve.wait_ge(sem, 11)
            dve.wait_ge(S("sumsq"), 15)
            dve.tensor_tensor_scan(a_rows[R32, :], ones[R32, :], cbm[R32, 0:LA], 0.0, ALU.mult, ALU.add)\
               .then_inc(S("ssd_scan"), 1)
            dve.wait_ge(S("ssd_rows_t"), 1)
            for t, bk in ((dt_tok, 6), (a_tok, 7)):
                dve.tensor_copy(t[:, 0:4, :].rearrange("p a b -> p (a b)"), ps[:, bk, 0:128])
                op = dve.tensor_copy(t[0:META, 4, :], ps[0:META, bk, 128:160])
            op.then_inc(S("ssd_tok"), 1)
            dve.wait_ge(S("ssd_tok"), 1)
            dve.tensor_scalar(a_neg[:], a_tok[:, 0:4, :], -1.0, None, ALU.mult)

            def take_cb(g):
                dve.wait_ge(S("ssd_cb"), g + 1)
                for i, (s0, n, _) in enumerate(LBLK):
                    for bk, c, t, m in LBANK[i]:
                        bk = CB_BANK[bk]
                        if t == s0:
                            op = dve.tensor_tensor(cbm[0:n, LOFF[i]:LOFF[i] + n], ps[0:n, bk, c:c + n], causal[0:n, 0:n], ALU.mult)
                            c, t, m = c + n, t + n, m - n
                        if m:
                            op = dve.tensor_copy(cbm[0:n, packed(i, t):packed(i, t) + m], ps[0:n, bk, c:c + m])
                op.then_inc(S("ssd_cb_taken"), 1)

            def take_x(g):
                if g:
                    dve.wait_ge(S("ssd_y"), HPG * g)
                for i, (s0, n, _) in enumerate(LBLK):
                    dve.wait_ge(S("ssd_xt"), 5 * g + i + 1)
                    dve.tensor_tensor(x_tok[0:n, i, :].rearrange("p (e d) -> p e d", e=HPG),
                                      ps[0:n, CB_BANK[i % 4], :].rearrange("p (e d) -> p e d", e=HPG),
                                      dt_tok[0:n, i, HPG * g:HPG * g + HPG].rearrange("p (e o) -> p e o", o=1)
                                      .to_broadcast((n, HPG, 64)), ALU.mult).then_inc(S("ssd_xt_taken"), 1)

            def log_decay(hh):
                dve.wait_ge(S("ssd_bc"), hh + 1)
                if hh >= 3:
                    dve.wait_ge(S("ssd_y"), hh - 2)
                for i, (s0, n, nl) in enumerate(LBLK):
                    bk, m = (0 if i < 2 else 1), (P if i < 2 else nl)
                    c = s0 - 256 * bk
                    op = dve.tensor_scalar(dec[0:n, hh % 3, LOFF[i]:LOFF[i] + m], ps[0:n, 6 * (1 - hh % 2) + bk, c:c + m],
                                           a_tok[0:n, i, hh:hh + 1], 0.0, ALU.subtract, ALU.min)
                op.then_inc(S("ssd_min"), 1)

            def weights(hh):
                dve.wait_ge(S("ssd_exp"), hh + 1)
                if hh % HPG == 0:
                    dve.wait_ge(S("ssd_cb_taken"), hh // HPG + 1)
                d = dec[:, hh % 3, :]
                dve.tensor_tensor(d[:, 0:LOFF[4]], d[:, 0:LOFF[4]], cbm[:, 0:LOFF[4]], ALU.mult)
                dve.tensor_tensor(d[0:META, LOFF[4]:LPK], d[0:META, LOFF[4]:LPK], cbm[0:META, LOFF[4]:LPK],
                                  ALU.mult).then_inc(S("ssd_m"), 1)

            def take_y(p):
                yb = 4 if p % 2 == 0 else 2
                dve.wait_ge(S("ssd_y"), 2 * p + 2)
                for bk, l0, n in HALF:
                    op = dve.scalar_tensor_tensor(X[:, p, l0:l0 + n], X[:, p, l0:l0 + n], col("ssd_d_skip", p),
                                                  ps[:, yb + bk, 0:n], ALU.mult, ALU.add)
                op.then_inc(S("ssd_y_taken"), 1)
                dve.wait_ge(S("ssd_y_taken"), p + 1)
                if p == 0:
                    dve.wait_ge(S("z_silu"), 16)
                dve.tensor_tensor(X[:, p, :], X[:, p, :], z_t[:, p, :], ALU.mult).then_inc(S("ssd_gated"), 1)

            def group_full(g, f):
                t = 4 * g + f
                dve.wait_ge(S("ssd_grs"), g + 1)
                dve.scalar_tensor_tensor(X[:, t, :], X[:, t, :], col("ssd_gate_norm", t), rstd[:], ALU.mult,
                                         ALU.mult).then_inc(S("hg_full"), 1)

            def group_lo(g, f):
                t = 4 * g + f
                dve.wait_ge(S("hg_hi"), t + 1)
                dve.tensor_tensor(hg_lo[:, t, :], X[:, t, :], hg_hi[:, t, :].bitcast(F32),
                                  ALU.subtract).then_inc(S("hg_lo"), 1)

            log_decay(0)
            take_cb(0)
            weights(0)
            take_x(0)
            log_decay(1)
            for hh in range(SSM_HEADS):
                g, e = hh // HPG, hh % HPG
                if e == HPG - 1 and g + 1 < GROUPS:
                    take_cb(g + 1)
                    weights(hh + 1)
                    take_x(g + 1)
                    log_decay(hh + 2)
                else:
                    if hh + 2 < SSM_HEADS:
                        log_decay(hh + 2)
                    if hh + 1 < SSM_HEADS:
                        weights(hh + 1)
                if hh % 2 == 0 and hh:
                    take_y(hh // 2 - 1)
                if g and e >= 4:
                    group_full(g - 1, e - 4)
                    if e > 4:
                        group_lo(g - 1, e - 5)
                if g > 1 and e == 0:
                    group_lo(g - 2, 3)
            take_y(SSM_HEADS // 2 - 1)
            group_lo(GROUPS - 2, 3)
            for f in range(4):
                group_full(GROUPS - 1, f)
                if f:
                    group_lo(GROUPS - 1, f - 1)
            group_lo(GROUPS - 1, 3)
            residual_dve(dve, "ssd_out", LA, (1, "ffn_norm", 0))

        def ssd_pool(pool):
            stats_pool(pool, 0, LA)
            c = 0
            for g in range(GROUPS):
                acc = gsq[g % 2]
                for f in range(4):
                    t = 4 * g + f
                    pool.wait_ge(S("ssd_gated"), t + 1)
                    if f == 0:
                        if g >= 2:
                            pool.wait_ge(S("ssd_gsum"), g - 1)
                        pool.tensor_tensor(acc[:], X[:, t, :], X[:, t, :], ALU.mult).then_inc(S("ssd_gsq"), 1)
                        c += 1
                        continue
                    pool.wait_ge(S("ssd_gsq"), c)
                    pool.tensor_tensor(t2[:, 0, :], X[:, t, :], X[:, t, :], ALU.mult).then_inc(S("ssd_gsq"), 1)
                    pool.wait_ge(S("ssd_gsq"), c + 1)
                    pool.tensor_tensor(acc[:], acc[:], t2[:, 0, :], ALU.add).then_inc(S("ssd_gsq"), 1)
                    c += 2
            pool.wait_ge(S("ssd_gsum"), GROUPS)
            stats_pool(pool, 1, LA)

        take = scratch("sb_", A0, A_SIZE)
        sp_t = take("softplus", 2, LPK)
        sw_t = take("weights", 2, LPK)
        SB_PARTS = [((4, 3, 2), ((P, 3, 0, LOFF[2], 416), (META, 3, 416, LOFF[4], 16)),
                     ((P, LOFF[2], LOFF[4]), (META, LOFF[4], LPK))),
                    ((1,), ((P, 2, 0, LOFF[1], 400),), ((P, LOFF[1], LOFF[2]),)),
                    ((0,), ((P, 0, 0, 0, 256), (P, 1, 0, 256, 272)), ((P, 0, LOFF[1]),))]
        NH = 16

        def sb_pe(pe):
            gemm(pe, "kv", xh, xl, LA, ready=(S("x_lo"), 16), norm=2)
            vtok_pe(pe, lambda f: X[:, 8 + f, :], LA, S("tile_taken"), tiles_out("kv"), 0)
            gemm(pe, "q", xh, xl, LA, ready=(S("x_lo"), 24))
            pe.wait_ge(S("tile_taken"), tiles_out("q"))
            pe.wait_ge(S("vtok_taken"), 5)

            def logits(hh):
                f, po, b0 = hh // 2, 64 * (hh % 2), 4 * (hh % 2)
                if hh >= 2:
                    pe.wait_ge(S("sb_o"), hh - 1)
                for i, (s0, n, _) in enumerate(LBLK):
                    for bk, c, t, m in LBANK[i]:
                        mm = pe.matmul(ps[0:n, b0 + bk, c:c + m], X[po:po + 64, f, s0:s0 + n], X[po:po + 64, 8 + f, t:t + m],
                                       start=i <= 2, stop=True, skip_group_check=True)
                mm.then_inc(S("sb_logits"), 1)

            def subtract_sums(hh):
                b0 = 4 * (hh % 2)
                for k, (blocks, _, _) in enumerate(SB_PARTS):
                    pe.wait_ge(S("sb_masked"), 3 * hh + k + 1)
                    for i in blocks:
                        n = LBLK[i][1]
                        for bk, c, t, m in LBANK[i]:
                            mm = pe.matmul(ps[0:n, b0 + bk, c:c + m], neg_tri[0:n, 0:n],
                                           sp_t[0:n, hh % 2, packed(i, t):packed(i, t) + m],
                                           start=False, stop=True, skip_group_check=True)
                            for j in range(i + 1, 5):
                                sj, nj, _ = LBLK[j]
                                a = max(t, sj)
                                if a < t + m:
                                    mm = pe.matmul(ps[0:n, b0 + bk, c + a - t:c + m], neg_ones[0:nj, 0:n],
                                                   sp_t[0:nj, hh % 2, packed(j, a):packed(j, a) + t + m - a],
                                                   start=False, stop=True, skip_group_check=True)
                    mm.then_inc(S("sb_sums"), 1)

            def values(hh):
                po, b0 = 64 * (hh % 2), 4 * (hh % 2)
                pe.wait_ge(S("sb_min"), 3 * hh + 3)
                for k, (blocks, _, _) in enumerate(SB_PARTS):
                    pe.wait_ge(S("sb_w"), 3 * hh + k + 1)
                    for i in blocks:
                        n = LBLK[i][1]
                        for bk, c, t, m in PIECES[i]:
                            mm = pe.matmul(ps[po:po + 64, b0 + bk, c:c + m], B[0:n, i, 64 * hh:64 * hh + 64],
                                           sw_t[0:n, hh % 2, packed(i, t):packed(i, t) + m],
                                           start=(bk, i) in ((1, 4), (0, 1)), stop=i == 0, skip_group_check=True)
                mm.then_inc(S("sb_values"), 1)

            logits(0)
            for hh in range(NH):
                if hh:
                    values(hh - 1)
                subtract_sums(hh)
                if hh + 1 < NH:
                    logits(hh + 1)
            values(NH - 1)
            pe.wait_ge(S("sb_o"), NH)
            gemm(pe, "sb_out", mh, ml, LA)

        def sb_act(act):
            stats_act(act, 2, LA)
            slabs_act(act, "kv")
            act.wait_ge(S("slab_done"), SLAB0["q"])
            for kt in range(KT):
                split_hi(act, 2, 3, kt, "sb_norm", LA)
            slabs_act(act, "q")
            act.wait_ge(S("slab_done"), SLAB0["sb_out"])

            def softplus_parts(hh):
                b0, w = 4 * (hh % 2), sw_t[:, hh % 2, :]
                act.wait_ge(S("sb_logits"), hh + 1)
                if hh >= 2:
                    act.wait_ge(S("sb_values"), hh - 1)
                for _, spans, _ in SB_PARTS:
                    for n, bk, c, o, m in spans:
                        op = act.activation(w[0:n, o:o + m], ps[0:n, b0 + bk, c:c + m], ACT.Abs)
                op.then_inc(S("sb_abs"), 1)
                act.wait_ge(S("sb_abs"), hh + 1)
                act.activation(w[:, 0:LOFF[4]], w[:, 0:LOFF[4]], ACT.Exp, scale=-1.0)
                act.activation(w[0:META, LOFF[4]:LPK], w[0:META, LOFF[4]:LPK], ACT.Exp, scale=-1.0).then_inc(S("sb_e"), 1)
                act.wait_ge(S("sb_e"), hh + 1)
                for _, _, parts in SB_PARTS:
                    for n, o, e in parts:
                        op = act.activation(w[0:n, o:e], w[0:n, o:e], ACT.Ln, bias=1.0)
                    op.then_inc(S("sb_ln"), 1)

            def weights(hh):
                w = sw_t[:, hh % 2, :]
                for k, (_, _, parts) in enumerate(SB_PARTS):
                    act.wait_ge(S("sb_min"), 3 * hh + k + 1)
                    for n, o, e in parts:
                        op = act.activation(w[0:n, o:e], w[0:n, o:e], ACT.Exp)
                    op.then_inc(S("sb_exp"), 1)

            def out_hi(hh):
                po, b0 = 64 * (hh % 2), 4 * (hh % 2)
                act.wait_ge(S("sb_values"), hh + 1)
                for bk, l0, n in HALF:
                    op = act.activation(mh[po:po + 64, hh // 2, l0:l0 + n], ps[po:po + 64, b0 + bk, 0:n], ACT.Copy)
                op.then_inc(S("sb_o_hi"), 1)

            softplus_parts(0)
            for hh in range(NH):
                if hh:
                    out_hi(hh - 1)
                weights(hh)
                if hh + 1 < NH:
                    softplus_parts(hh + 1)
            out_hi(NH - 1)
            residual_act(act, "sb_out", LA, 3, (4, "ffn_norm", KT))

        def sb_dve(dve):
            stats_dve(dve, 2, LA)
            scaled_stage_dve(dve, "kv", lambda k: tile_of(X, k, LA), LA)
            for kt in range(KT):
                split_lo(dve, 3, kt, "sb_norm", LA)
            vtok_dve(dve, B, LA, 0)
            scaled_stage_dve(dve, "q", lambda k: tile_of(X, 8 + k, LA), LA, scale=0.125)

            def softplus_sum(hh):
                b0, w, s = 4 * (hh % 2), sw_t[:, hh % 2, :], sp_t[:, hh % 2, :]
                if hh >= 2:
                    dve.wait_ge(S("sb_sums"), 3 * (hh - 1))
                for k, (_, spans, _) in enumerate(SB_PARTS):
                    dve.wait_ge(S("sb_ln"), 3 * hh + k + 1)
                    for n, bk, c, o, m in spans:
                        op = dve.scalar_tensor_tensor(s[0:n, o:o + m], ps[0:n, b0 + bk, c:c + m], 0.0, w[0:n, o:o + m],
                                                      ALU.max, ALU.add)
                    op.then_inc(S("sb_softplus"), 1)

            def log_weights(hh):
                b0, w = 4 * (hh % 2), sw_t[:, hh % 2, :]
                for k, (_, spans, _) in enumerate(SB_PARTS):
                    dve.wait_ge(S("sb_sums"), 3 * hh + k + 1)
                    for n, bk, c, o, m in spans:
                        op = dve.tensor_scalar(w[0:n, o:o + m], ps[0:n, b0 + bk, c:c + m], 0.0, None, ALU.min)
                    op.then_inc(S("sb_min"), 1)

            def out_lo(hh):
                po, b0 = 64 * (hh % 2), 4 * (hh % 2)
                dve.wait_ge(S("sb_o_hi"), hh + 1)
                for bk, l0, n in HALF:
                    op = dve.tensor_tensor(ml[po:po + 64, hh // 2, l0:l0 + n], ps[po:po + 64, b0 + bk, 0:n],
                                           mh[po:po + 64, hh // 2, l0:l0 + n].bitcast(F32), ALU.subtract)
                op.then_inc(S("sb_o"), 1)

            softplus_sum(0)
            for hh in range(NH):
                if hh:
                    out_lo(hh - 1)
                log_weights(hh)
                if hh + 1 < NH:
                    softplus_sum(hh + 1)
            out_lo(NH - 1)
            residual_dve(dve, "sb_out", LA, (4, "ffn_norm", KT))

        def sb_pool(pool):
            def keep_earlier(t, hh, ready, sem):
                for k, (blocks, _, _) in enumerate(SB_PARTS):
                    pool.wait_ge(ready, 3 * hh + k + 1)
                    for i in blocks:
                        n = LBLK[i][1]
                        v = t[0:n, hh % 2, LOFF[i]:LOFF[i] + n]
                        op = pool.affine_select(out=v, in_=v, compare_op=ALU.is_gt, fill=0.0, base=0,
                                                pattern=[[1, n]], channel_multiplier=-1)
                    op.then_inc(sem, 1)

            keep_earlier(sp_t, 0, S("sb_softplus"), S("sb_masked"))
            for hh in range(NH):
                keep_earlier(sw_t, hh, S("sb_exp"), S("sb_w"))
                if hh + 1 < NH:
                    keep_earlier(sp_t, hh + 1, S("sb_softplus"), S("sb_masked"))
            stats_pool(pool, 3, LA)

        def join_dve(dve):
            stats_dve(dve, 4, LA)
            for kt in range(KT):
                dve.scalar_tensor_tensor(hv(kt, SEQ), hv(kt, SEQ), col("final_norm", kt), rstd[:, META:LA],
                                         ALU.mult, ALU.mult).then_inc(S("x2_done"), 1)
            for kt in range(KT):
                split_lo(dve, 5, kt, "attn_norm_2", SEQ)

        def join_act(act):
            stats_act(act, 4, LA)
            act.wait_ge(S("slab_done"), SLAB0["rq"])
            for kt in range(KT):
                split_hi(act, 5, 5, kt, "attn_norm_2", SEQ)

        take = scratch("rel_", A0, A_SIZE)
        rel_t = take("bias", 2, SEQ)
        prob = take("prob", 2, 1280)
        probT = take("probT", 2, 1280)
        rmax = take("rmax", 2, 4)
        rsum = take("rsum", 2, 4)
        POFF = [0, 128, 384, 768]
        TOFF = [0, 512, 896, 1152]

        def rel_pe(pe):
            gemm(pe, "rq", xh, xl, SEQ, ready=(S("x_lo"), 40), norm=5)
            gemm(pe, "rk", xh, xl, SEQ)
            gemm(pe, "rv", xh, xl, SEQ)
            pe.wait_ge(S("tile_taken"), tiles_out("rv"))
            vtok_pe(pe, lambda f: v_tmp[:, f, :], SEQ, S("tile_taken"), tiles_out("rv"), 5)
            pe.wait_ge(S("vtok_taken"), 9)

            def scores(hh):
                f, po = hh // 2, 64 * (hh % 2)
                pe.wait_ge(S("rel_bias"), 2 * hh + 2)
                for i in range(4):
                    n = P * (i + 1)
                    if hh:
                        pe.wait_ge(S("rel_exp"), 4 * (hh - 1) + i + 1)
                    pe.matmul(ps[:, i, 0:n], X[po:po + 64, f, P * i:P * i + P], X[po:po + 64, 8 + f, 0:n],
                              start=True, stop=False)
                    mm = pe.matmul(ps[:, i, 0:n], flip[:], rel_t[:, hh % 2, 384 - P * i:SEQ], start=False, stop=True)
                    mm.then_inc(S("rel_scores"), 1)

            def transposes(hh):
                if hh:
                    pe.wait_ge(S("rel_o"), hh)
                    pe.wait_ge(S("rel_ta"), hh)
                pe.wait_ge(S("rel_prob"), hh + 1)
                for j in range(4):
                    for i in range(j, 4):
                        mm = pe.transpose(ps[:, 4 + j, P * (i - j):P * (i - j + 1)],
                                          prob[:, hh % 2, POFF[i] + P * j:POFF[i] + P * j + P], ident[:])
                mm.then_inc(S("rel_t"), 1)

            def values(hh):
                po = 64 * (hh % 2)
                pe.wait_ge(S("rel_ta"), hh + 1)
                pe.wait_ge(S("rel_tb"), hh + 1)
                for j in range(4):
                    n = SEQ - P * j
                    mm = pe.matmul(ps[po:po + 64, 4, P * j:SEQ], B[:, j, 64 * hh:64 * hh + 64],
                                   probT[:, hh % 2, TOFF[j]:TOFF[j] + n], start=j == 0, stop=j == 3, skip_group_check=True)
                mm.then_inc(S("rel_values"), 1)

            scores(0)
            for hh in range(NH):
                if hh + 1 < NH:
                    scores(hh + 1)
                transposes(hh)
                values(hh)
            pe.wait_ge(S("rel_o"), NH)
            gemm(pe, "rel_out", mh, ml, SEQ)

        def rel_act(act):
            stats_act(act, 5, SEQ)
            for name in ("rq", "rk", "rv"):
                slabs_act(act, name)

            def exps(hh):
                act.wait_ge(S("rel_max"), 2 * hh + 2)
                if hh >= 2:
                    act.wait_ge(S("rel_t"), hh - 1)
                for i in range(4):
                    n = P * (i + 1)
                    act.activation(prob[:, hh % 2, POFF[i]:POFF[i] + n], ps[:, i, 0:n], ACT.Exp,
                                   bias=rmax[:, hh % 2, i:i + 1], accum_out=rsum[:, hh % 2, i:i + 1]).then_inc(S("rel_exp"), 1)

            def take_t(hh):
                act.wait_ge(S("rel_t"), hh + 1)
                if hh >= 2:
                    act.wait_ge(S("rel_values"), hh - 1)
                act.activation(probT[:, hh % 2, 0:512], ps[:, 4, :], ACT.Copy).then_inc(S("rel_ta"), 1)

            def out_hi(hh):
                po = 64 * (hh % 2)
                act.wait_ge(S("rel_values"), hh + 1)
                act.activation(mh[po:po + 64, hh // 2, 0:SEQ], ps[po:po + 64, 4, :], ACT.Copy).then_inc(S("rel_o_hi"), 1)

            act.wait_ge(S("slab_done"), SLAB0["rel_out"])
            exps(0)
            for hh in range(NH):
                take_t(hh)
                if hh + 1 < NH:
                    exps(hh + 1)
                out_hi(hh)
            residual_act(act, "rel_out", SEQ, 6, (6, "mlp_norm_2", 0))

        def rel_dve(dve):
            stats_dve(dve, 5, SEQ)
            scaled_stage_dve(dve, "rq", lambda k: tile_of(X, k, SEQ), SEQ, scale=0.125)
            scaled_stage_dve(dve, "rk", lambda k: tile_of(X, 8 + k, SEQ), SEQ)
            scaled_stage_dve(dve, "rv", lambda k: tile_of(v_tmp, k, SEQ), SEQ)
            vtok_dve(dve, B, SEQ, 5)

            def maxima(hh):
                for i in range(4):
                    dve.wait_ge(S("rel_scores"), 4 * hh + i + 1)
                    op = dve.tensor_reduce(rmax[:, hh % 2, i:i + 1], ps[:, i, 0:P * (i + 1)], AX, ALU.max)
                op.then_inc(S("rel_max"), 1)
                dve.wait_ge(S("rel_max"), 2 * hh + 1)
                dve.tensor_scalar(rmax[:, hh % 2, :], rmax[:, hh % 2, :], -1.0, None, ALU.mult).then_inc(S("rel_max"), 1)

            def normalise(hh):
                r = rsum[:, hh % 2, :]
                dve.wait_ge(S("rel_exp"), 4 * hh + 4)
                dve.reciprocal(r, r).then_inc(S("rel_recip"), 1)
                dve.wait_ge(S("rel_recip"), hh + 1)
                for i in range(4):
                    v = prob[:, hh % 2, POFF[i]:POFF[i] + P * (i + 1)]
                    op = dve.tensor_scalar(v, v, r[:, i:i + 1], None, ALU.mult)
                op.then_inc(S("rel_prob"), 1)

            def take_t(hh):
                dve.wait_ge(S("rel_t"), hh + 1)
                if hh >= 2:
                    dve.wait_ge(S("rel_values"), hh - 1)
                for j in range(1, 4):
                    n = SEQ - P * j
                    op = dve.tensor_copy(probT[:, hh % 2, TOFF[j]:TOFF[j] + n], ps[:, 4 + j, 0:n])
                op.then_inc(S("rel_tb"), 1)

            def out_lo(hh):
                po = 64 * (hh % 2)
                dve.wait_ge(S("rel_o_hi"), hh + 1)
                dve.tensor_tensor(ml[po:po + 64, hh // 2, 0:SEQ], ps[po:po + 64, 4, :],
                                  mh[po:po + 64, hh // 2, 0:SEQ].bitcast(F32), ALU.subtract).then_inc(S("rel_o"), 1)

            maxima(0)
            for hh in range(NH):
                normalise(hh)
                if hh + 1 < NH:
                    maxima(hh + 1)
                take_t(hh)
                out_lo(hh)
            residual_dve(dve, "rel_out", SEQ, (6, "mlp_norm_2", 0))

        def rel_pool(pool):
            stats_pool(pool, 5, SEQ)
            pool.wait_ge(S("slab_done"), SLAB0["rel_out"])
            for hh in range(NH):
                if hh >= 2:
                    pool.wait_ge(S("rel_scores"), 4 * (hh - 1))
                src = bass.AP(rel_in.tensor, hh * REL_ROW, [[1, P], [1, SEQ]])
                pool.dma_start(rel_t[:, hh % 2, :], src).then_inc(S("rel_loaded"), 16)
                pool.wait_ge(S("rel_loaded"), 16 * (hh + 1))
                pool.memset(rel_t[64:P, hh % 2, 448:SEQ], -BIG).then_inc(S("rel_bias"), 2)
            stats_pool(pool, 6, SEQ)

        DH = 8
        CH = 4
        take = scratch("dn_", A0, A_SIZE)
        k_tok = take("k_tok", CH, D)
        big = [take(f"big{i}", CH, P) for i in range(8)]
        t1a = [sb(f"dn_t{i}", CH, P, at=at) for i, at in enumerate(
            [T1_AT, T1_AT + 2048, T2_AT, T2_AT + 2048, PAD_AT, PAD_AT + 2048, CACC_AT, CACC_AT + 2048])]
        take_c = scratch("dnc_", C0, C_SIZE)
        big += t1a + [take_c("c0", CH, P), take_c("c1", CH, P)]
        take_b = scratch("dnb_", B0 + 4 * D * 4, D * 4)
        state = [take_b(f"state{z}", P) for z in range(2)]
        vnew = [take_b(f"vnew{z}", P) for z in range(2)]
        resid = [take_b(f"resid{z}", P) for z in range(2)]
        gc_tok = take_b("gc_tok", CH, DH)
        be_tok = take_b("be_tok", CH, DH)
        nbe_tok = take_b("nbe_tok", CH, DH)
        glast = [take_b(f"glast{z}", CH) for z in range(2)]
        eglast = [take_b(f"eglast{z}", CH) for z in range(2)]
        kfac = [take_b(f"kfac{z}", CH) for z in range(2)]
        dneg = take_b("dneg", 1)
        KB, QG, BV, DM, LT, PM, XM, XTM, KD = range(9)
        buf = [big[0:9], big[9:18]]
        R8, RB = slice(0, DH), slice(32, 32 + DH)
        osq = [sqa, rstd]
        l2_buf = [sqa, t1[:, 0, :], t1[:, 1, :], t2[:, 0, :], t2[:, 1, :], cacc[:, 0, :], cacc[:, 1, :], pad[:, 0, 3:3 + LA]]
        row_buf = [B[R8, k, 0:SEQ] for k in range(5)]
        ab_t, g_rows = sqb, rvar

        def kc(hh, c):
            return X[:, 8 + hh, P * c:P * c + P]

        def bcast4(m):
            return m.rearrange("p (o n) -> p o n", o=1).to_broadcast((P, CH, P))

        def dn_pe(pe):
            gemm(pe, "ab", xh, xl, SEQ, ready=(S("x_lo"), KT * 7), norm=7)
            for name in ("dn_qk", "dn_v"):
                gemm(pe, name, xh, xl, SEQ)

            def l2_sums(j):
                if j == 0:
                    return
                for t in (2 * j - 2, 2 * j - 1):
                    pe.wait_ge(S("l2_sq"), t + 1)
                    if t >= 4:
                        pe.wait_ge(S("l2_ln"), t - 3)
                    pe.matmul(ps[:, 4 + t % 4, :], ones[:, 0:P], l2_buf[t % 8][:, 0:SEQ], start=True,
                              stop=True).then_inc(S("l2_sum"), 1)
            gemm(pe, "dn_z", xh, xl, SEQ, between=l2_sums)
            l2_sums(8)
            pe.wait_ge(S("tile_taken"), tiles_out("dn_z"))
            vtok_pe(pe, lambda f: v_tmp[:, f, :], SEQ, S("conv_used"), 2 + 48, 9, bank=0)
            pe.wait_ge(S("l2_ln"), 16)
            vtok_pe(pe, lambda f: X[:, 8 + f, :], SEQ, S("l2_done"), 16, 13)
            pe.wait_ge(S("vtok_taken"), 13)
            pe.wait_ge(S("dn_scan"), CH)
            pe.wait_ge(S("dn_softplus"), 5)
            for c in range(CH):
                pe.transpose(ps[:, 0, 8 * c:8 * c + 8], g_rows[R8, P * c:P * c + P], ident[R8, R8])
            for c in range(CH):
                mm = pe.transpose(ps[:, 1, 8 * c:8 * c + 8], ab_t[RB, P * c:P * c + P], ident[RB, RB])
            mm.then_inc(S("dn_rows_t"), 1)
            pe.wait_ge(S("dn_tok"), 2)
            pe.wait_ge(S("vtok_taken"), 17)

            def out_sums(pr):
                for z in range(2):
                    pe.wait_ge(S("dn_osq"), 2 * pr + z + 1)
                    pe.wait_ge(S("dn_state"), 8 * pr + 6 + z + 1)
                    pe.matmul(ps[:, 4 * z + 3, :], ones[:, 0:P], osq[z][:, 0:SEQ], start=True, stop=True)\
                      .then_inc(S("dn_osum"), 1)

            for pr in range(DH // 2):
                both = [(z, 2 * pr + z, 4 * z, buf[z]) for z in range(2)]
                for z, hh, b0, w in both:
                    if pr:
                        pe.wait_ge(S("dn_vnew"), 8 * (pr - 1) + 6 + z + 1)
                    pe.matmul(ps[:, b0, :], ident[R8, hh:hh + 1].to_broadcast((DH, P)), g_rows[R8, 0:SEQ],
                              start=True, stop=True)
                    pe.matmul(ps[:, b0 + 1, :], ident[RB, 32 + hh:33 + hh].to_broadcast((DH, P)), ab_t[RB, 0:SEQ],
                              start=True, stop=True).then_inc(S("dn_bc"), 1)
                if pr:
                    out_sums(pr - 1)
                for z, hh, b0, w in both:
                    pe.wait_ge(S("dn_kb"), hh + 1)
                    if pr:
                        pe.wait_ge(S("dn_oraw"), hh - 1)
                        pe.wait_ge(S("dn_oln"), hh - 1)
                    for c in range(CH):
                        pe.matmul(ps[:, b0 + 2, P * c:P * c + P], kc(hh, c), w[KB][:, c, :], start=True, stop=True)
                    for c in range(CH):
                        mm = pe.matmul(ps[:, b0 + 3, P * c:P * c + P], kc(hh, c), X[:, hh, P * c:P * c + P],
                                       start=True, stop=True)
                    mm.then_inc(S("dn_kk"), 1)
                for z, hh, b0, w in both:
                    pe.wait_ge(S("dn_l0"), hh + 1)
                    pe.wait_ge(S("dn_egc"), hh + 1)
                    for c in range(CH):
                        mm = pe.transpose(ps[:, b0, P * c:P * c + P], w[KB][:, c, :], ident[:])
                    mm.then_inc(S("dn_pw"), 1)
                for k in range(1, 7):
                    for z, hh, b0, w in both:
                        pe.wait_ge(S("dn_lk"), 12 * pr + 2 * (k - 1) + z + 1)
                        pe.wait_ge(S("dn_x"), 26 * pr + 4 * (k - 1) + 2 * z + 2)
                        for c in range(CH):
                            mm = pe.matmul(ps[:, b0, P * c:P * c + P], w[KB][:, c, :], w[XM][:, c, :], start=True, stop=True)
                        mm.then_inc(S("dn_pw"), 1)
                    for z, hh, b0, w in both:
                        pe.wait_ge(S("dn_w"), 12 * pr + 2 * (k - 1) + z + 1)
                        for c in range(CH):
                            mm = pe.matmul(ps[:, b0 + 1, P * c:P * c + P], w[DM][:, c, :], w[XTM][:, c, :], start=True, stop=True)
                        if k < 6:
                            for c in range(CH):
                                mm = pe.matmul(ps[:, b0 + 2, P * c:P * c + P], w[XTM][:, c, :], w[DM][:, c, :],
                                               start=True, stop=True)
                        mm.then_inc(S("dn_px"), 1)
                for c in range(CH):
                    if c:
                        for z, hh, b0, w in both:
                            pe.wait_ge(S("dn_state"), 8 * pr + 2 * (c - 1) + z + 1)
                            pe.matmul(ps[:, b0, 0:P], kc(hh, c), state[z][:], start=True, stop=True).then_inc(S("dn_ks"), 1)
                    for z, hh, b0, w in both:
                        if c:
                            pe.wait_ge(S("dn_resid"), 6 * pr + 2 * (c - 1) + z + 1)
                        else:
                            pe.wait_ge(S("dn_x"), 26 * pr + 24 + z + 1)
                            pe.wait_ge(S("dn_prep"), hh + 1)
                        pe.matmul(ps[:, b0 + 1, 0:P], w[XTM][:, c, :], resid[z][:] if c else w[BV][:, 0, :],
                                  start=True, stop=True).then_inc(S("dn_vp"), 1)
                    for z, hh, b0, w in both:
                        pe.wait_ge(S("dn_vnew"), 8 * pr + 2 * c + z + 1)
                        pe.matmul(ps[:, b0 + 2, P * c:P * c + P], vnew[z][:], w[PM][:, c, :], start=True, stop=c == 0)
                        if c:
                            pe.matmul(ps[:, b0 + 2, P * c:P * c + P], state[z][:], w[QG][:, c, :], start=False, stop=True)
                        pe.matmul(ps[:, b0 + 3, 0:P], w[KD][:, c, :], vnew[z][:], start=True, stop=True).then_inc(S("dn_sp"), 1)
            out_sums(DH // 2 - 1)
            pe.wait_ge(S("dn_oln"), DH)
            pe.wait_ge(S("dn_o"), 1)
            gemm(pe, "dn_out", mh, ml, SEQ, ready=(S("dn_o"), 0))

        def dn_act(act):
            stats_act(act, 7, SEQ)
            slabs_act(act, "ab")
            conv_stage_act(act, "dn_qk", 24, None, CONV0["dn_in"], SEQ, lambda k: tile_of(X, k, SEQ))
            conv_stage_act(act, "dn_v", 40, None, CONV0["dn_in"] + 64, SEQ, lambda k: tile_of(v_tmp, k, SEQ))


            def l2_factors(g):
                for t in range(4 * g, 4 * g + 4):
                    act.wait_ge(S("l2_sum"), t + 1)
                    act.activation(l2_buf[t % 8][:, 0:SEQ], ps[:, 4 + t % 4, :], ACT.Ln, bias=eps_col[:]).then_inc(S("l2_ln"), 1)
                for t in range(4 * g, 4 * g + 4):
                    act.wait_ge(S("l2_ln"), t + 1)
                    act.activation(l2_buf[t % 8][:, 0:SEQ], l2_buf[t % 8][:, 0:SEQ], ACT.Exp, scale=-0.5).then_inc(S("l2_r"), 1)

            sem = S("dn_softplus")
            for j in range(KT):
                slab_hi(act, SLAB0["dn_z"] + j)
                if j == 0:
                    softplus_act(act, sem, 0, ab_t[R8, 0:SEQ], col("dn_dt_bias_2", 0, R8), row_buf[0], row_buf[1])
                    act.activation(dneg[R8, :], col("dn_a_log_2", 0, R8), ACT.Exp).then_inc(sem, 1)
                    act.activation(ab_t[RB, 0:SEQ], ab_t[RB, 0:SEQ], ACT.Sigmoid).then_inc(sem, 1)
                elif j % 2 == 0:
                    l2_factors(j // 2 - 1)
            l2_factors(3)
            for j in range(KT):
                act.wait_ge(S("tile_taken"), taken("dn_z", j, 0))
                act.activation(zd_t[:, j, 0:SEQ], zd_t[:, j, 0:SEQ], ACT.Silu).then_inc(S("dn_z_silu"), 1)
            act.wait_ge(S("dn_tok"), 1)
            act.activation(nbe_tok[:].rearrange("p a b -> p (a b)"), gc_tok[:].rearrange("p a b -> p (a b)"),
                           ACT.Exp).then_inc(sem, 1)

            def out_factors(pr):
                for z in range(2):
                    act.wait_ge(S("dn_sp"), 8 * pr + 6 + z + 1)
                    act.activation(osq[z][:, 0:SEQ], ps[:, 4 * z + 2, :], ACT.Square).then_inc(S("dn_osq"), 1)
                for z in range(2):
                    act.wait_ge(S("dn_osum"), 2 * pr + z + 1)
                    act.activation(osq[z][:, 0:SEQ], ps[:, 4 * z + 3, :], ACT.Ln, scale=1.0 / P,
                                   bias=eps_col[:]).then_inc(S("dn_oln"), 1)
                for z in range(2):
                    act.wait_ge(S("dn_oln"), 2 * pr + z + 1)
                    act.activation(osq[z][:, 0:SEQ], osq[z][:, 0:SEQ], ACT.Exp, scale=-0.5).then_inc(S("dn_ors"), 1)

            def out_hi(pr):
                for z in range(2):
                    hh = 2 * pr + z
                    act.wait_ge(S("dn_ofull"), 2 * hh + 2)
                    act.activation(mh[:, hh, 0:SEQ], zd_t[:, hh, 0:SEQ], ACT.Copy).then_inc(S("dn_o_hi"), 1)

            for pr in range(DH // 2):
                both = [(z, 2 * pr + z, 4 * z, buf[z]) for z in range(2)]
                for z, hh, b0, w in both:
                    act.wait_ge(S("dn_dm"), hh + 1)
                    act.activation(w[DM][:], w[DM][:], ACT.Exp).then_inc(S("dn_edm"), 1)
                    act.activation(w[QG][:].rearrange("p a b -> p (a b)"), ps[:, b0, :], ACT.Exp).then_inc(S("dn_egc"), 1)
                    for c in range(CH):
                        act.activation(kfac[z][:, c:c + 1], gc_tok[:, c, hh:hh + 1], ACT.Exp, scale=-1.0,
                                       bias=glast[z][:, c:c + 1])
                    act.activation(eglast[z][:], glast[z][:], ACT.Exp).then_inc(S("dn_kf"), 1)
                for k in range(1, 7):
                    for z, hh, b0, w in both:
                        act.wait_ge(S("dn_pw"), 14 * pr + 2 * k + z + 1)
                        act.activation(w[DM][:].rearrange("p a b -> p (a b)"), ps[:, b0, :], ACT.Copy).then_inc(S("dn_w"), 1)
                    if k == 2 and pr:
                        out_hi(pr - 1)
                out_factors(pr)
            out_hi(DH // 2 - 1)
            residual_act(act, "dn_out", SEQ, 8, (8, "mlp_norm_2", KT))

        def dn_dve(dve):
            stats_dve(dve, 7, SEQ)
            slab_lo(dve, SLAB0["ab"])
            dve.wait_ge(S("stat_ready"), 8)
            dve.wait_ge(S("sumsq"), 15 * 8)
            take_scaled(dve, "ab", 0, 0, ab_t[:, 0:SEQ], SEQ)
            conv_stage_dve(dve, "dn_qk", 24, "dn_conv_w_2", CONV0["dn_in"], SEQ)
            conv_stage_dve(dve, "dn_v", 40, "dn_conv_w_2", CONV0["dn_in"] + 64, SEQ)
            sem = S("dn_rows")

            def decay_rows():
                softplus_dve(dve, sem, 0, S("dn_softplus"), 3, ab_t[R8, 0:SEQ], col("dn_dt_bias_2", 0, R8), *row_buf)
                dve.wait_ge(S("dn_softplus"), 4)
                dve.tensor_scalar(dneg[R8, :], dneg[R8, :], -1.0, None, ALU.mult).then_inc(sem, 1)
                dve.wait_ge(sem, 10)
                dve.tensor_scalar(row_buf[3], row_buf[4], dneg[R8, :], None, ALU.mult).then_inc(sem, 1)
                dve.wait_ge(sem, 11)
                for c in range(CH):
                    dve.tensor_tensor_scan(g_rows[R8, P * c:P * c + P], ones[R8, 0:P], row_buf[3][:, P * c:P * c + P], 0.0,
                                           ALU.mult, ALU.add).then_inc(S("dn_scan"), 1)

            def l2_apply(g):
                for t in range(4 * g, 4 * g + 4):
                    dve.wait_ge(S("l2_r"), t + 1)
                    dve.scalar_tensor_tensor(X[:, t, 0:SEQ], X[:, t, 0:SEQ], P ** -0.5 if t < 8 else 1.0,
                                             l2_buf[t % 8][:, 0:SEQ], ALU.mult, ALU.mult).then_inc(S("l2_done"), 1)

            for j in range(KT):
                take_scaled(dve, "dn_z", j, 0, zd_t[:, j, 0:SEQ], SEQ)
                slab_lo(dve, SLAB0["dn_z"] + j)
                if j == 1:
                    decay_rows()
                if j in (4, 6):
                    l2_apply(j // 2 - 2)
            l2_apply(2)
            vtok_dve(dve, B, SEQ, 9, bank=0)
            l2_apply(3)
            dve.wait_ge(S("slab_done"), SLAB0["dn_out"])
            vtok_dve(dve, k_tok, SEQ, 13)
            dve.wait_ge(S("dn_rows_t"), 1)
            dve.tensor_copy(gc_tok[:].rearrange("p a b -> p (a b)"), ps[:, 0, 0:32]).then_inc(S("dn_tok"), 1)
            dve.tensor_copy(be_tok[:].rearrange("p a b -> p (a b)"), ps[:, 1, 0:32]).then_inc(S("dn_tok"), 1)
            dve.wait_ge(S("dn_softplus"), 6)
            dve.wait_ge(S("dn_tok"), 2)
            dve.scalar_tensor_tensor(nbe_tok[:].rearrange("p a b -> p (a b)"), nbe_tok[:].rearrange("p a b -> p (a b)"),
                                     -1.0, be_tok[:].rearrange("p a b -> p (a b)"), ALU.mult, ALU.mult)\
               .then_inc(S("dn_nbe"), 1)
            dve.wait_ge(S("dn_nbe"), 1)

            def norm_out(pr):
                for z in range(2):
                    hh = 2 * pr + z
                    o, g = v_tmp[:, hh, 0:SEQ], zd_t[:, hh, 0:SEQ]
                    dve.wait_ge(S("dn_ors"), hh + 1)
                    dve.wait_ge(S("dn_oraw"), hh + 1)
                    dve.scalar_tensor_tensor(o, o, col("dn_head_norm_2"), osq[z][:, 0:SEQ],
                                             ALU.mult, ALU.mult).then_inc(S("dn_ofull"), 1)
                    dve.wait_ge(S("dn_ofull"), 2 * hh + 1)
                    if pr == 0:
                        dve.wait_ge(S("dn_z_silu"), 8)
                    dve.tensor_tensor(g, o, g, ALU.mult).then_inc(S("dn_ofull"), 1)

            def out_lo(pr):
                for z in range(2):
                    hh = 2 * pr + z
                    dve.wait_ge(S("dn_o_hi"), hh + 1)
                    dve.tensor_tensor(ml[:, hh, 0:SEQ], zd_t[:, hh, 0:SEQ], mh[:, hh, 0:SEQ].bitcast(F32),
                                      ALU.subtract).then_inc(S("dn_o"), 1)

            for pr in range(DH // 2):
                both = [(z, 2 * pr + z, 4 * z, buf[z]) for z in range(2)]
                for z, hh, b0, w in both:
                    dve.wait_ge(S("dn_bc"), hh + 1)
                    dve.tensor_tensor(w[KB][:].rearrange("p a b -> p (a b)"), X[:, 8 + hh, 0:SEQ], ps[:, b0 + 1, :],
                                      ALU.mult).then_inc(S("dn_kb"), 1)
                    dve.tensor_copy(glast[z][:], ps[:, b0, P - 1:SEQ:P])
                    for c in range(CH):
                        op = dve.tensor_scalar(w[DM][:, c, :], ps[:, b0, P * c:P * c + P], gc_tok[:, c, hh:hh + 1], 0.0,
                                               ALU.subtract, ALU.min)
                    op.then_inc(S("dn_dm"), 1)
                for z, hh, b0, w in both:
                    dve.wait_ge(S("dn_kk"), hh + 1)
                    dve.wait_ge(S("dn_mask"), hh + 1)
                    dve.tensor_tensor(w[LT][:], ps[:, b0 + 2, :].rearrange("p (a b) -> p a b", a=CH), w[DM][:],
                                      ALU.mult).then_inc(S("dn_lt"), 1)
                    dve.wait_ge(S("dn_lt"), hh + 1)
                    dve.tensor_tensor(w[KB][:], w[LT][:], bcast4(levels[:, 0, :]), ALU.mult).then_inc(S("dn_l0"), 1)
                    dve.tensor_tensor(w[PM][:], ps[:, b0 + 3, :].rearrange("p (a b) -> p a b", a=CH), w[DM][:], ALU.mult)
                    dve.wait_ge(S("dn_l0"), hh + 1)
                    dve.tensor_tensor(w[XTM][:], bcast4(ident[:]), w[KB][:], ALU.subtract).then_inc(S("dn_x"), 1)
                    dve.wait_ge(S("dn_pw"), 14 * pr + z + 1)
                    dve.tensor_tensor(w[XM][:], bcast4(ident[:]), ps[:, b0, :].rearrange("p (a b) -> p a b", a=CH),
                                      ALU.subtract).then_inc(S("dn_x"), 1)

                def prepare(z, hh, b0, w):
                    dve.wait_ge(S("dn_kf"), hh + 1)
                    q = w[QG][:].rearrange("p a b -> p (a b)")
                    dve.tensor_tensor(q, q, X[:, hh, 0:SEQ], ALU.mult)
                    for c in range(CH):
                        dve.tensor_scalar(w[BV][:, c, :], B[:, c, P * hh:P * hh + P], be_tok[:, c, hh:hh + 1], None, ALU.mult)
                    for c in range(CH):
                        op = dve.tensor_scalar(w[KD][:, c, :], k_tok[:, c, P * hh:P * hh + P], kfac[z][:, c:c + 1], None, ALU.mult)
                    op.then_inc(S("dn_prep"), 1)

                for one in both:
                    prepare(*one)
                if pr:
                    norm_out(pr - 1)
                for k in range(1, 7):
                    for z, hh, b0, w in both:
                        dve.wait_ge(S("dn_px"), 12 * pr + 2 * (k - 1) + z + 1)
                        for t, bk in ((XTM, 1), (XM, 2))[:2 if k < 6 else 1]:
                            v = w[t][:].rearrange("p a b -> p (a b)")
                            dve.tensor_tensor(v, v, ps[:, b0 + bk, :], ALU.subtract).then_inc(S("dn_x"), 1)
                    if k == 3 and pr:
                        out_lo(pr - 1)
                for c in range(CH):
                    if c:
                        for z, hh, b0, w in both:
                            dve.wait_ge(S("dn_ks"), 6 * pr + 2 * (c - 1) + z + 1)
                            dve.scalar_tensor_tensor(resid[z][:], ps[:, b0, 0:P], nbe_tok[:, c, hh:hh + 1], w[BV][:, c, :],
                                                     ALU.mult, ALU.add).then_inc(S("dn_resid"), 1)
                    for z, hh, b0, w in both:
                        dve.wait_ge(S("dn_vp"), 8 * pr + 2 * c + z + 1)
                        dve.tensor_copy(vnew[z][:], ps[:, b0 + 1, 0:P]).then_inc(S("dn_vnew"), 1)
                    for z, hh, b0, w in both:
                        dve.wait_ge(S("dn_sp"), 8 * pr + 2 * c + z + 1)
                        if c:
                            dve.wait_ge(S("dn_state"), 8 * pr + 2 * (c - 1) + z + 1)
                            op = dve.scalar_tensor_tensor(state[z][:], state[z][:], eglast[z][:, c:c + 1], ps[:, b0 + 3, 0:P],
                                                          ALU.mult, ALU.add)
                        else:
                            op = dve.tensor_copy(state[z][:], ps[:, b0 + 3, 0:P])
                        op.then_inc(S("dn_state"), 1)
                for z, hh, b0, w in both:
                    dve.wait_ge(S("dn_osq"), hh + 1)
                    dve.tensor_copy(v_tmp[:, hh, 0:SEQ], ps[:, b0 + 2, :]).then_inc(S("dn_oraw"), 1)
            norm_out(DH // 2 - 1)
            out_lo(DH // 2 - 1)
            residual_dve(dve, "dn_out", SEQ, (8, "mlp_norm_2", KT))

        def dn_pool(pool):
            for t in range(16):
                if t == 0:
                    pool.wait_ge(S("conv_used"), 2 + 24 + 16)
                    pool.wait_ge(S("stat_ready"), 8)
                if t == 5:
                    pool.wait_ge(S("conv_used"), 2 + 48)
                if t >= 8:
                    pool.wait_ge(S("l2_done"), t - 7)
                pool.tensor_tensor(l2_buf[t % 8][:, 0:SEQ], X[:, t, 0:SEQ], X[:, t, 0:SEQ], ALU.mult)\
                    .then_inc(S("l2_sq"), 1)
            for pr in range(DH // 2):
                both = [(z, 2 * pr + z, 4 * z, buf[z]) for z in range(2)]
                for z, hh, b0, w in both:
                    pool.wait_ge(S("dn_edm"), hh + 1)
                    pool.affine_select(out=w[DM][:], in_=w[DM][:], compare_op=ALU.is_ge, fill=0.0, base=0,
                                       pattern=[[0, CH], [1, P]], channel_multiplier=-1).then_inc(S("dn_mask"), 1)
                for k in range(1, 7):
                    for z, hh, b0, w in both:
                        pool.wait_ge(S("dn_pw"), 14 * pr + 2 * (k - 1) + z + 1)
                        if k == 1:
                            pool.wait_ge(S("dn_x"), 26 * pr + 2 * z + 1)
                        pool.tensor_tensor(w[KB][:], w[LT][:], bcast4(levels[:, k, :]), ALU.mult).then_inc(S("dn_lk"), 1)
            stats_pool(pool, 8, SEQ)

        def ffn_parts(layer, n, xi, n_next, split):
            def pool(e):
                stats_pool(e, n_next, LA)

            def tensor(e):
                ffn_pe(e, layer, n, xi)
                if n_next == 4:
                    stats_pe(e, n_next, LA)
            return (tensor, lambda e: ffn_dve(e, layer, n, split), lambda e: ffn_act(e, layer, n, n_next, split), pool)

        def mlp_parts(layer, n, xi, n_next, split):
            def pool(e):
                stats_pool(e, n_next, SEQ)

            def tensor(e):
                mlp_pe(e, layer, n, xi)
                if n_next == 9:
                    stats_pe(e, n_next, SEQ)
            return (tensor, lambda e: mlp_dve(e, layer, n, split), lambda e: mlp_act(e, layer, n, n_next, split), pool)

        def finish_dve(dve):
            stats_dve(dve, 9, SEQ)
            for kt in range(KT):
                dve.scalar_tensor_tensor(hv(kt, SEQ), hv(kt, SEQ), col("final_norm_2", kt), rstd[:, 0:SEQ],
                                         ALU.mult, ALU.mult).then_inc(S("y_done"), 1)

        nothing = lambda e: None
        ffn0 = ffn_parts(0, 1, 1, 2, (2, "kv_norm", 0))
        ffn1 = ffn_parts(1, 3, 4, 4, None)
        mlp0 = mlp_parts(0, 6, 6, 7, (7, "dn_norm_2", 0))
        mlp1 = mlp_parts(1, 8, 8, 9, None)
        parts = [(ssd_pe, ssd_dve, ssd_act, ssd_pool), ffn0, (sb_pe, sb_dve, sb_act, sb_pool), ffn1,
                 (nothing, join_dve, join_act, nothing), (rel_pe, rel_dve, rel_act, rel_pool), mlp0,
                 (dn_pe, dn_dve, dn_act, dn_pool), mlp1, (nothing, finish_dve, lambda e: stats_act(e, 9, SEQ), nothing)]
        pe_parts, dve_parts, act_parts, pool_parts = [[p[k] for p in parts] for k in range(4)]
        block = ctx.enter_context(nc.Block())

        @block.sync
        def _(sp):
            sp.dma_start(w_raw[:, 0, :], slabs[0]).then_inc(S("w_loaded0"), 16)
            sp.dma_start(h[:], x_in).then_inc(S("x_loaded"), 16)
            sp.dma_start(par[:], params).then_inc(S("par_loaded"), 16)
            for n in range(1, RING):
                sp.dma_start(w_raw[:, n, :], slabs[n]).then_inc(S(f"w_loaded{n}"), 16)
            sp.dma_start(cst[:], consts_in).then_inc(S("par_loaded"), 16)
            with sp.Fori(1, N_SLABS // RING) as i:
                for j in range(RING):
                    sp.wait_ge(S("slab_done"), 4 * i + (j + 1 - RING))
                    sp.dma_start(w_raw[:, j, :], slabs[bass.ds(4 * i + j, 1)].rearrange("a p n -> (a p) n"))\
                      .then_inc(S(f"w_loaded{j}"), 16)
            for n in range(N_SLABS // RING * RING, N_SLABS):
                sp.wait_ge(S("slab_done"), n - RING + 1)
                sp.dma_start(w_raw[:, n % RING, :], slabs[n]).then_inc(S(f"w_loaded{n % RING}"), 16)
            for kt in range(KT):
                sp.wait_ge(S("y_done"), kt + 1)
                sp.dma_start(out[:, kt, :], hv(kt, SEQ)).then_inc(S("out_stored"), 16)
            sp.wait_ge(S("out_stored"), 16 * KT)

        @block.gpsimd
        def _(pool):
            for part in pool_parts:
                part(pool)

        @block.scalar
        def _(act):
            act.sem_inc(S("conv_used"), 2)
            act.wait_ge(S("par_loaded"), 32)
            for s in range(AHEAD):
                slab_hi(act, s - AHEAD)
            for part in act_parts:
                part(act)

        @block.vector
        def _(dve):
            dve.sem_inc(S("tile_taken"), 2)
            dve.memset(eps_col[:], EPS)
            dve.memset(pad[:, :, 0:3], 0.0).then_inc(S("pad_zero"), 1)
            dve.wait_ge(S("par_loaded"), 32)
            dve.wait_ge(S("pad_zero"), 1)
            for s in range(AHEAD):
                slab_lo(dve, s - AHEAD)
            for part in dve_parts:
                part(dve)

        @block.tensor
        def _(pe):
            pe.wait_ge(S("par_loaded"), 32)
            for part in pe_parts:
                part(pe)


def slab_rows(np, w, cols=None):
    k, m = w.shape
    kg = -(-k // D)
    w = np.pad(w, ((0, kg * D - k), (0, -m % P)))
    w = w.reshape(kg, KT, P, w.shape[1] // P, P)
    return np.ascontiguousarray(w.transpose(3, 0, 2, 1, 4)).reshape(-1, P, D)


def tiles_of(a):
    n = a.shape[0] // P
    return a.reshape(n, P, -1).transpose(1, 0, 2).reshape(P, -1)


def column(np, a):
    return np.pad(a.reshape(-1, 1), ((0, P - a.size), (0, 0)))


def interleave(np, w):
    lead = w.shape[:-1]
    return w.reshape(*lead, 2, FT, P).swapaxes(-3, -2).reshape(*lead, 2 * FF)


def host_arrays(np, a):
    ssd = a["ssd_w_in"][0]
    z, xs, bc, dt = np.split(ssd, [SSM_IN, 2 * SSM_IN, 2 * SSM_IN + 1024], axis=1)
    slabs = [slab_rows(np, w) for w in (dt, bc, xs, z, a["ssd_w_out"][0])]

    def ffn(layer):
        up, down = interleave(np, a["ffn_w_up"][layer]), a["ffn_w_down"][layer]
        at = 0
        for k in FFN_ROUNDS:
            slabs.append(slab_rows(np, up[:, 2 * P * at:2 * P * (at + k)]))
            slabs.append(slab_rows(np, down[P * at:P * (at + k)]))
            at += k

    def mlp(layer):
        for r in range(MT // KT):
            slabs.append(slab_rows(np, a["mlp_w_up_2"][layer][:, D * r:D * (r + 1)]))
            slabs.append(slab_rows(np, a["mlp_w_down_2"][layer][D * r:D * (r + 1)]))

    ffn(0)
    slabs += [slab_rows(np, w) for w in (a["w_kv"], a["sb_w_q"][0], a["sb_w_o"][0])]
    ffn(1)
    slabs += [slab_rows(np, w) for w in (a["attn_w_qkv_2"][0], a["attn_w_o_2"][0])]
    mlp(0)
    dn = a["dn_w_in_2"][0]
    ab = np.concatenate([np.pad(dn[:, 4 * D:4 * D + 8], ((0, 0), (0, 24))), dn[:, 4 * D + 8:]], axis=1)
    slabs += [slab_rows(np, w) for w in (ab, dn[:, :4 * D], a["dn_w_o_2"][0])]
    mlp(1)

    conv = np.concatenate([a["ssd_conv_w"][0][:, SSM_IN:], a["ssd_conv_w"][0][:, :SSM_IN]], axis=1).T
    conv_b = np.concatenate([a["ssd_conv_b"][0][SSM_IN:], a["ssd_conv_b"][0][:SSM_IN]])
    values = {
        "ssd_norm": tiles_of(a["ssd_norm"][0]), "ssd_conv_w": tiles_of(conv), "ssd_conv_b": tiles_of(conv_b),
        "ssd_dt_bias": column(np, a["ssd_dt_bias"][0]), "ssd_a_log": column(np, a["ssd_a_log"][0]),
        "ssd_d_skip": tiles_of(np.repeat(a["ssd_d_skip"][0], SSM_IN // SSM_HEADS)),
        "ssd_gate_norm": tiles_of(a["ssd_gate_norm"][0]), "kv_norm": tiles_of(a["kv_norm"]),
        "sb_norm": tiles_of(a["sb_norm"][0]), "ffn_norm": tiles_of(a["ffn_norm"].reshape(-1)),
        "ffn_conv_w": np.concatenate([tiles_of(interleave(np, a["ffn_conv_w"][i]).T) for i in range(2)], axis=1),
        "ffn_conv_b": np.concatenate([tiles_of(interleave(np, a["ffn_conv_b"][i])) for i in range(2)], axis=1),
        "final_norm": tiles_of(a["final_norm"]), "attn_norm_2": tiles_of(a["attn_norm_2"][0]),
        "dn_norm_2": tiles_of(a["dn_norm_2"][0]), "dn_conv_w_2": tiles_of(a["dn_conv_w_2"][0].T),
        "dn_a_log_2": column(np, a["dn_a_log_2"][0]), "dn_dt_bias_2": column(np, a["dn_dt_bias_2"][0]),
        "dn_head_norm_2": column(np, a["dn_head_norm_2"][0]), "mlp_norm_2": tiles_of(a["mlp_norm_2"].reshape(-1)),
        "final_norm_2": tiles_of(a["final_norm_2"]),
    }
    params = np.concatenate([values[n] for n, _ in PARAM_COLS], axis=1)
    assert params.shape == (P, N_PARAM)

    x = np.concatenate([a["meta_tokens"], a["x"][0]], axis=0).T
    rel = np.pad(a["attn_rel_bias_2"][0], ((0, 0), (0, 255)), mode="edge")[:, ::-1][:, :REL_ROW]

    r, c = np.arange(P)[:, None], np.arange(P)[None, :]
    level = [((r >> (k + 1)) == (c >> (k + 1))) & ((c >> k) & 1 == 1) & ((r >> k) & 1 == 0) for k in range(7)]
    one = np.ones((P, P))
    consts = np.concatenate([r == c, -one, -1.0 * (r >= c), r <= c, r + c == P - 1, *level, np.ones((P, LA))], axis=1)
    return {
        "slabs": np.concatenate(slabs, axis=0), "params": params,
        "x": x.reshape(KT, P, LA).transpose(1, 0, 2), "rel": rel, "consts": consts.astype(np.float32),
    }


def kernel(**inputs):
    import numpy as np
    import concourse.bacc as bacc
    from concourse.bass_utils import run_bass_kernel_spmd as run

    arrays = {k: np.ascontiguousarray(v) for k, v in host_arrays(np, {k: np.asarray(v) for k, v in inputs.items()}).items()}
    assert arrays["slabs"].shape[0] == N_SLABS
    nc = bacc.Bacc("TRN2", target_bir_lowering=False, num_devices=1)
    names = ("slabs", "params", "x", "rel", "consts")
    aps = [nc.dram_tensor(f"in_{n}", arrays[n].shape, F32, kind="ExternalInput").ap() for n in names]
    out = nc.dram_tensor("out_y", (P, KT, SEQ), F32, kind="ExternalOutput").ap()
    build_program(nc, *aps, out)
    r = run(nc, [{f"in_{n}": arrays[n] for n in names}], core_ids=[0])
    y = r.results[0]["out_y"]
    return np.ascontiguousarray(y.transpose(2, 1, 0)).reshape(1, SEQ, D)
```
